# Optimizing a Trainium2 kernel written in Bass

```python
import math
import jax, jax.numpy as jnp
from jax import lax
import numpy as np

D_MODEL = 1024
BATCH = 1
SEQ = 512
DEPTH = 2

D_FF = 2816
EPS = 1e-6
ROPE_THETA = 10000.0
Q_BLOCK = 128
N_BRANCH = 3
SB_HEADS = 8
SB_HD = 64
MLA_HEADS = 8
MLA_NOPE = 64
MLA_ROPE = 32
MLA_V = 64
MLA_Q_LORA = 256
MLA_KV_LORA = 128
NSA_HEADS = 8
NSA_GROUPS = 2
NSA_REP = NSA_HEADS // NSA_GROUPS
NSA_HD = 64
CMP_LEN = 32
CMP_STRIDE = 16
CMP_HIDDEN = 128
SLC_LEN = 64
SLC_TOPK = 16
SLC_Q_CHUNK = 64
WIN = 512
FORCE_SCORE = 1e3
NEG_INF = -1e30
SB_W = SB_HEADS * SB_HD
NSA_KV_W = NSA_GROUPS * NSA_HD
IN_SIZES = (SB_W, SB_W, SB_W,
            MLA_Q_LORA, MLA_KV_LORA, MLA_ROPE,
            NSA_HEADS * NSA_HD,
            NSA_KV_W, NSA_KV_W, NSA_KV_W, NSA_KV_W, NSA_KV_W, NSA_KV_W,
            N_BRANCH * NSA_HEADS,
            N_BRANCH * D_MODEL)
N_IN = sum(IN_SIZES)


def rms_norm(x, g):
    xf = x.astype(jnp.float32)
    y = xf * lax.rsqrt(jnp.mean(xf * xf, axis=-1, keepdims=True) + EPS)
    return (y * g.astype(jnp.float32)).astype(x.dtype)

def rope(x, pos):
    d = x.shape[-1]
    half = d // 2
    inv = jnp.exp(-math.log(ROPE_THETA) * jnp.arange(half, dtype=jnp.float32) * (2.0 / d))
    ang = pos.astype(jnp.float32)[:, None] * inv[None, :]
    cos = jnp.cos(ang)[None, :, None, :]
    sin = jnp.sin(ang)[None, :, None, :]
    xf = x.astype(jnp.float32)
    x1, x2 = xf[..., :half], xf[..., half:]
    return jnp.concatenate([x1 * cos - x2 * sin, x1 * sin + x2 * cos], axis=-1).astype(x.dtype)

def masked_softmax(s, mask):
    s = jnp.where(mask, s.astype(jnp.float32), NEG_INF)
    m = jnp.max(s, axis=-1, keepdims=True)
    e = jnp.where(mask, jnp.exp(s - m), 0.0)
    return e / jnp.maximum(jnp.sum(e, axis=-1, keepdims=True), 1e-30)

def swiglu_ffn(x, g, wi, wo):
    a, b = jnp.split(rms_norm(x, g) @ wi, 2, axis=-1)
    return (jax.nn.silu(a) * b) @ wo

def to_blocks(x, blk):
    B, S = x.shape[:2]
    return jnp.moveaxis(x.reshape((B, S // blk, blk) + x.shape[2:]), 1, 0)

def from_blocks(y):
    y = jnp.moveaxis(y, 0, 1)
    return y.reshape((y.shape[0], -1) + y.shape[3:])

def stick_breaking_attention(q, k, v):
    B, S, H, d = q.shape
    scale = 1.0 / math.sqrt(d)
    kpos = jnp.arange(S)

    def block(args):
        qb, i = args
        qpos = i * Q_BLOCK + jnp.arange(Q_BLOCK)
        z = jnp.einsum('bqhd,bkhd->bhqk', qb, k).astype(jnp.float32) * scale
        strict = kpos[None, :] < qpos[:, None]
        log_one_minus = jnp.where(strict, -jax.nn.softplus(z), 0.0)
        suffix = lax.cumsum(log_one_minus, axis=3, reverse=True) - log_one_minus
        w = jnp.where(strict, jnp.exp(jax.nn.log_sigmoid(z) + suffix), 0.0)
        return jnp.einsum('bhqk,bkhd->bqhd', w.astype(v.dtype), v)

    return from_blocks(lax.map(block, (to_blocks(q, Q_BLOCK), jnp.arange(S // Q_BLOCK))))

def causal_attention(q, k, v):
    B, S, H, d = q.shape
    scale = 1.0 / math.sqrt(d)
    kpos = jnp.arange(S)

    def block(args):
        qb, i = args
        qpos = i * Q_BLOCK + jnp.arange(Q_BLOCK)
        s = jnp.einsum('bqhd,bkhd->bhqk', qb, k).astype(jnp.float32) * scale
        p = masked_softmax(s, kpos[None, :] <= qpos[:, None])
        return jnp.einsum('bhqk,bkhd->bqhd', p.astype(v.dtype), v)

    return from_blocks(lax.map(block, (to_blocks(q, Q_BLOCK), jnp.arange(S // Q_BLOCK))))

def mla_attention(c_q, c_kv, k_r, q_norm, w_uq, kv_norm, w_ukv, gain_q, gain_k, pos):
    B, S, _ = c_q.shape
    q = (rms_norm(c_q, q_norm) @ w_uq).reshape(B, S, MLA_HEADS, MLA_NOPE + MLA_ROPE)
    kv = (rms_norm(c_kv, kv_norm) @ w_ukv).reshape(B, S, MLA_HEADS, MLA_NOPE + MLA_V)
    k_nope, v = kv[..., :MLA_NOPE], kv[..., MLA_NOPE:]
    k = jnp.concatenate([k_nope, jnp.broadcast_to(k_r[:, :, None, :], (B, S, MLA_HEADS, MLA_ROPE))], axis=-1)
    q = rms_norm(q, gain_q)
    k = rms_norm(k, gain_k)
    q = jnp.concatenate([q[..., :MLA_NOPE], rope(q[..., MLA_NOPE:], pos)], axis=-1)
    k = jnp.concatenate([k[..., :MLA_NOPE], rope(k[..., MLA_NOPE:], pos)], axis=-1)
    return causal_attention(q, k, v).reshape(B, S, MLA_HEADS * MLA_V)

def nsa_attention(q_in, cmp_k_in, cmp_v_in, slc_k_in, slc_v_in, win_k_in, win_v_in, gate_logits,
                  q_gain, k_gain, cmp_pos_k, cmp_pos_v, cmp_wk1, cmp_wk2, cmp_wv1, cmp_wv2, pos):
    B, S, _ = q_in.shape
    G, R, hd = NSA_GROUPS, NSA_REP, NSA_HD
    scale = 1.0 / math.sqrt(hd)
    q = rope(rms_norm(q_in.reshape(B, S, NSA_HEADS, hd), q_gain), pos).reshape(B, S, G, R, hd)

    n_cmp = (S - CMP_LEN) // CMP_STRIDE + 1
    starts = jnp.arange(n_cmp) * CMP_STRIDE
    ends = starts + (CMP_LEN - 1)
    idx = starts[:, None] + jnp.arange(CMP_LEN)[None, :]

    def compress(t, pe, w1, w2):
        tb = t.reshape(B, S, G, hd)[:, idx] + pe[None, None, :, None, :]
        tb = jnp.moveaxis(tb, 3, 2).reshape(B, n_cmp, G, CMP_LEN * hd)
        return jax.nn.gelu(tb @ w1) @ w2

    k_cmp = rope(rms_norm(compress(cmp_k_in, cmp_pos_k, cmp_wk1, cmp_wk2), k_gain), ends)
    v_cmp = compress(cmp_v_in, cmp_pos_v, cmp_wv1, cmp_wv2)
    s_cmp = jnp.einsum('bsgrd,bngd->bgrsn', q, k_cmp).astype(jnp.float32) * scale
    p_cmp = masked_softmax(s_cmp, ends[None, :] <= pos[:, None])
    o_cmp = jnp.einsum('bgrsn,bngd->bsgrd', p_cmp.astype(v_cmp.dtype), v_cmp)

    n_slc = S // SLC_LEN
    n_sel = min(SLC_TOPK, n_slc)
    c0 = np.arange(n_cmp)[:, None] * CMP_STRIDE
    s0 = np.arange(n_slc)[None, :] * SLC_LEN
    overlap = np.clip(np.minimum(c0 + CMP_LEN, s0 + SLC_LEN) - np.maximum(c0, s0), 0, None) / CMP_LEN
    importance = jnp.einsum('bgrsn,nj->bgsj', p_cmp, jnp.asarray(overlap, jnp.float32))
    blk = jnp.arange(n_slc)[None, :]
    cur = (pos // SLC_LEN)[:, None]
    forced = (blk == 0) | (blk == cur) | (blk == cur - 1)
    score = jnp.where(blk > cur, -1.0, jnp.where(forced, FORCE_SCORE, importance))
    _, sel = lax.top_k(score, n_sel)

    k_s = rope(rms_norm(slc_k_in.reshape(B, S, G, hd), k_gain), pos)
    kb = jnp.moveaxis(k_s.reshape(B, n_slc, SLC_LEN, G, hd), 3, 1)
    vb = jnp.moveaxis(slc_v_in.reshape(B, n_slc, SLC_LEN, G, hd), 3, 1)
    bi = jnp.arange(B)[:, None, None, None]
    gi = jnp.arange(G)[None, :, None, None]
    n_chunk = S // SLC_Q_CHUNK
    n_tok = n_sel * SLC_LEN
    sel_c = jnp.moveaxis(sel.reshape(B, G, n_chunk, SLC_Q_CHUNK, n_sel), 2, 0)

    def slc_chunk(args):
        qc, sc, i = args
        qpos = i * SLC_Q_CHUNK + jnp.arange(SLC_Q_CHUNK)
        kg = kb[bi, gi, sc].reshape(B, G, SLC_Q_CHUNK, n_tok, hd)
        vg = vb[bi, gi, sc].reshape(B, G, SLC_Q_CHUNK, n_tok, hd)
        tok = (sc[..., None] * SLC_LEN + jnp.arange(SLC_LEN)).reshape(B, G, 1, SLC_Q_CHUNK, n_tok)
        s = jnp.einsum('bqgrd,bgqkd->bgrqk', qc, kg).astype(jnp.float32) * scale
        p = masked_softmax(s, tok <= qpos[:, None])
        return jnp.einsum('bgrqk,bgqkd->bqgrd', p.astype(vg.dtype), vg)

    o_slc = from_blocks(lax.map(slc_chunk, (to_blocks(q, SLC_Q_CHUNK), sel_c, jnp.arange(n_chunk))))

    k_w = rope(rms_norm(win_k_in.reshape(B, S, G, hd), k_gain), pos)
    pad = ((0, 0), (WIN, 0), (0, 0), (0, 0))
    kp = jnp.pad(k_w, pad)
    vp = jnp.pad(win_v_in.reshape(B, S, G, hd), pad)

    def win_block(args):
        qb, i = args
        start = i * Q_BLOCK
        kk = lax.dynamic_slice_in_dim(kp, start, Q_BLOCK + WIN, axis=1)
        vv = lax.dynamic_slice_in_dim(vp, start, Q_BLOCK + WIN, axis=1)
        qpos = start + jnp.arange(Q_BLOCK)
        kpos = start - WIN + jnp.arange(Q_BLOCK + WIN)
        dist = qpos[:, None] - kpos[None, :]
        mask = (dist >= 0) & (dist < WIN) & (kpos[None, :] >= 0)
        s = jnp.einsum('bqgrd,bkgd->bgrqk', qb, kk).astype(jnp.float32) * scale
        p = masked_softmax(s, mask)
        return jnp.einsum('bgrqk,bkgd->bqgrd', p.astype(vv.dtype), vv)

    o_win = from_blocks(lax.map(win_block, (to_blocks(q, Q_BLOCK), jnp.arange(S // Q_BLOCK))))

    g = jax.nn.sigmoid(gate_logits.astype(jnp.float32)).reshape(B, S, N_BRANCH, G, R, 1).astype(q.dtype)
    o = g[:, :, 0] * o_cmp + g[:, :, 1] * o_slc + g[:, :, 2] * o_win
    return o.reshape(B, S, NSA_HEADS * hd)

def first_inputs(seed: int = 0) -> dict:
    key = jax.random.key(seed)
    ks = jax.random.split(key, 28)
    L = DEPTH
    cmp_in = CMP_LEN * NSA_HD

    def nrm(k, shape, scale):
        return jax.random.normal(k, shape, jnp.float32) * scale

    def gain(k, n):
        return 1.0 + 0.05 * jax.random.normal(k, (L, n), jnp.float32)

    return {
        'x': nrm(ks[0], (BATCH, SEQ, D_MODEL), 1.0),
        'ffn1_norm': gain(ks[1], D_MODEL),
        'ffn1_wi': nrm(ks[2], (L, D_MODEL, 2 * D_FF), D_MODEL ** -0.5),
        'ffn1_wo': nrm(ks[3], (L, D_FF, D_MODEL), D_FF ** -0.5),
        'mix_norm': gain(ks[4], D_MODEL),
        'w_in': nrm(ks[5], (L, D_MODEL, N_IN), D_MODEL ** -0.5),
        'mla_q_norm': gain(ks[6], MLA_Q_LORA),
        'mla_w_uq': nrm(ks[7], (L, MLA_Q_LORA, MLA_HEADS * (MLA_NOPE + MLA_ROPE)), MLA_Q_LORA ** -0.5),
        'mla_kv_norm': gain(ks[8], MLA_KV_LORA),
        'mla_w_ukv': nrm(ks[9], (L, MLA_KV_LORA, MLA_HEADS * (MLA_NOPE + MLA_V)), MLA_KV_LORA ** -0.5),
        'mla_qk_gain_q': gain(ks[10], MLA_NOPE + MLA_ROPE),
        'mla_qk_gain_k': gain(ks[11], MLA_NOPE + MLA_ROPE),
        'nsa_q_gain': gain(ks[12], NSA_HD),
        'nsa_k_gain': gain(ks[13], NSA_HD),
        'cmp_pos_k': nrm(ks[14], (L, CMP_LEN, NSA_HD), 0.5),
        'cmp_pos_v': nrm(ks[15], (L, CMP_LEN, NSA_HD), 0.5),
        'cmp_wk1': nrm(ks[16], (L, cmp_in, CMP_HIDDEN), cmp_in ** -0.5),
        'cmp_wk2': nrm(ks[17], (L, CMP_HIDDEN, NSA_HD), CMP_HIDDEN ** -0.5),
        'cmp_wv1': nrm(ks[18], (L, cmp_in, CMP_HIDDEN), cmp_in ** -0.5),
        'cmp_wv2': nrm(ks[19], (L, CMP_HIDDEN, NSA_HD), CMP_HIDDEN ** -0.5),
        'proj_sb': nrm(ks[20], (L, SB_W, D_MODEL), SB_W ** -0.5),
        'proj_mla': nrm(ks[21], (L, MLA_HEADS * MLA_V, D_MODEL), (MLA_HEADS * MLA_V) ** -0.5),
        'proj_nsa': nrm(ks[22], (L, NSA_HEADS * NSA_HD, D_MODEL), (NSA_HEADS * NSA_HD) ** -0.5),
        'w_out': nrm(ks[23], (L, D_MODEL, D_MODEL), D_MODEL ** -0.5),
        'ffn2_norm': gain(ks[24], D_MODEL),
        'ffn2_wi': nrm(ks[25], (L, D_MODEL, 2 * D_FF), D_MODEL ** -0.5),
        'ffn2_wo': nrm(ks[26], (L, D_FF, D_MODEL), D_FF ** -0.5),
    }

def first_block(x, ffn1_norm, ffn1_wi, ffn1_wo, mix_norm, w_in, mla_q_norm, mla_w_uq, mla_kv_norm,
              mla_w_ukv, mla_qk_gain_q, mla_qk_gain_k, nsa_q_gain, nsa_k_gain, cmp_pos_k, cmp_pos_v,
              cmp_wk1, cmp_wk2, cmp_wv1, cmp_wv2, proj_sb, proj_mla, proj_nsa, w_out,
              ffn2_norm, ffn2_wi, ffn2_wo):
    B, S, _ = x.shape
    pos = jnp.arange(S, dtype=jnp.int32)
    offsets = np.cumsum(IN_SIZES)[:-1].tolist()
    for l in range(DEPTH):
        x = x + 0.5 * swiglu_ffn(x, ffn1_norm[l], ffn1_wi[l], ffn1_wo[l])
        h = rms_norm(x, mix_norm[l])
        (sb_q, sb_k, sb_v, mla_cq, mla_ckv, mla_kr, nsa_q, ck, cv, sk, sv, wk, wv,
         nsa_gate, merge_gate) = jnp.split(h @ w_in[l], offsets, axis=-1)
        o_sb = stick_breaking_attention(sb_q.reshape(B, S, SB_HEADS, SB_HD),
                                        sb_k.reshape(B, S, SB_HEADS, SB_HD),
                                        sb_v.reshape(B, S, SB_HEADS, SB_HD)).reshape(B, S, SB_W)
        o_mla = mla_attention(mla_cq, mla_ckv, mla_kr, mla_q_norm[l], mla_w_uq[l], mla_kv_norm[l],
                              mla_w_ukv[l], mla_qk_gain_q[l], mla_qk_gain_k[l], pos)
        o_nsa = nsa_attention(nsa_q, ck, cv, sk, sv, wk, wv, nsa_gate, nsa_q_gain[l], nsa_k_gain[l],
                              cmp_pos_k[l], cmp_pos_v[l], cmp_wk1[l], cmp_wk2[l], cmp_wv1[l], cmp_wv2[l], pos)
        gates = jax.nn.sigmoid(merge_gate.astype(jnp.float32)).reshape(B, S, N_BRANCH, D_MODEL).astype(x.dtype)
        y = (gates[:, :, 0] * (o_sb @ proj_sb[l])
             + gates[:, :, 1] * (o_mla @ proj_mla[l])
             + gates[:, :, 2] * (o_nsa @ proj_nsa[l]))
        x = x + y @ w_out[l]
        x = x + 0.5 * swiglu_ffn(x, ffn2_norm[l], ffn2_wi[l], ffn2_wo[l])
    return x


DEPTH_2 = 1

D_MIX = D_MODEL
GDN_HEADS = 4
GDN_DK = 128
GDN_DV = 128
MLSTM_HEADS = 4
MLSTM_DK = 128
MLSTM_DV = 128
N_DIR = 2
CONV_K = 5
CHUNK = 64
PEER_HEADS = 8
PEER_NKEYS = 128
PEER_N = PEER_NKEYS * PEER_NKEYS
PEER_DKEY = 256
PEER_TOPK = 16
PEER_BLOCK = 128

GDN_QK = GDN_HEADS * GDN_DK
GDN_V = GDN_HEADS * GDN_DV
ML_QK = MLSTM_HEADS * MLSTM_DK
ML_V = MLSTM_HEADS * MLSTM_DV
SPLIT_SIZES = (GDN_QK, GDN_QK, GDN_V, GDN_V, N_DIR * GDN_HEADS, N_DIR * GDN_HEADS,
               ML_QK, ML_QK, ML_V, ML_V, N_DIR * MLSTM_HEADS, N_DIR * MLSTM_HEADS)
D_IN = sum(SPLIT_SIZES)


def _rmsnorm(x, g):
    x32 = x.astype(jnp.float32)
    y = x32 * lax.rsqrt(jnp.mean(x32 * x32, axis=-1, keepdims=True) + EPS)
    return (y * g.astype(jnp.float32)).astype(x.dtype)

def _l2norm(x):
    return x * lax.rsqrt(jnp.sum(x * x, axis=-1, keepdims=True) + EPS)

def _to_heads(x, n_heads):
    b, s, _ = x.shape
    return x.astype(jnp.float32).reshape(b, s, n_heads, -1).transpose(0, 2, 1, 3)

def _chunk(x):
    b, h, s = x.shape[:3]
    return x.reshape(b, h, s // CHUNK, CHUNK, *x.shape[3:])

def _flip(x):
    return jnp.flip(x, axis=2)

def _conv_centred(x, w):
    c = x.shape[-1]
    rhs = w.astype(jnp.float32).T[:, None, :]
    return lax.conv_general_dilated(x, rhs, window_strides=(1,),
                                    padding=[(CONV_K // 2, CONV_K // 2)],
                                    dimension_numbers=("NWC", "WIO", "NWC"),
                                    feature_group_count=c)

def _gated_delta_rule(q, k, v, g, beta):
    b_, h_, s_, dk = q.shape
    dv = v.shape[-1]
    q, k, v, g, beta = (_chunk(a) for a in (q, k, v, g, beta))
    g = jnp.cumsum(g, axis=-1)
    incl = jnp.tril(jnp.ones((CHUNK, CHUNK), dtype=bool))
    strict = jnp.tril(jnp.ones((CHUNK, CHUNK), dtype=bool), k=-1)
    decay = jnp.exp(jnp.where(incl, g[..., :, None] - g[..., None, :], -jnp.inf))
    k_beta = k * beta[..., None]
    a_mat = jnp.where(strict, jnp.einsum("bhncd,bhnsd->bhncs", k_beta, k) * decay, 0.0)
    eye = jnp.eye(CHUNK, dtype=q.dtype)
    t_mat = lax.linalg.triangular_solve(eye + a_mat, jnp.broadcast_to(eye, a_mat.shape),
                                        left_side=True, lower=True)
    u = jnp.einsum("bhncs,bhnse->bhnce", t_mat, v * beta[..., None])
    w = jnp.einsum("bhncs,bhnsd->bhncd", t_mat, k_beta * jnp.exp(g)[..., None])
    qk = jnp.where(incl, jnp.einsum("bhncd,bhnsd->bhncs", q, k) * decay, 0.0)
    q_dec = q * jnp.exp(g)[..., None]
    k_dec = k * jnp.exp(g[..., -1:] - g)[..., None]
    g_tot = jnp.exp(g[..., -1])

    def step(state, inp):
        u_c, w_c, qk_c, qd_c, kd_c, gt_c = inp
        v_new = u_c - jnp.einsum("bhcd,bhde->bhce", w_c, state)
        o_c = (jnp.einsum("bhcd,bhde->bhce", qd_c, state)
               + jnp.einsum("bhcs,bhse->bhce", qk_c, v_new))
        state = state * gt_c[..., None, None] + jnp.einsum("bhcd,bhce->bhde", kd_c, v_new)
        return state, o_c

    xs = tuple(jnp.moveaxis(a, 2, 0) for a in (u, w, qk, q_dec, k_dec, g_tot))
    _, o = lax.scan(step, jnp.zeros((b_, h_, dk, dv), q.dtype), xs)
    return jnp.moveaxis(o, 0, 2).reshape(b_, h_, s_, dv)

def _mlstm(q, k, v, i_pre, f_pre):
    b_, h_, s_, dk = q.shape
    dv = v.shape[-1]
    q, k, v, i_pre, f_pre = (_chunk(a) for a in (q, k, v, i_pre, f_pre))
    incl = jnp.tril(jnp.ones((CHUNK, CHUNK), dtype=bool))
    bcum = jnp.cumsum(jax.nn.log_sigmoid(f_pre), axis=-1)
    d_log = jnp.where(incl, bcum[..., :, None] - bcum[..., None, :] + i_pre[..., None, :], -jnp.inf)
    m_intra = jnp.max(d_log, axis=-1)
    p = jnp.exp(d_log - m_intra[..., None]) * jnp.einsum("bhncd,bhnsd->bhncs", q, k)
    num_intra = jnp.einsum("bhncs,bhnse->bhnce", p, v)
    den_intra = jnp.sum(p, axis=-1)
    b_last = bcum[..., -1]
    w_log = b_last[..., None] - bcum + i_pre
    m_w = jnp.max(w_log, axis=-1)
    wgt = jnp.exp(w_log - m_w[..., None])
    dc = jnp.einsum("bhnc,bhncd,bhnce->bhnde", wgt, k, v)
    dn = jnp.einsum("bhnc,bhncd->bhnd", wgt, k)

    def step(carry, inp):
        c_st, n_st, m_st = carry
        q_c, b_c, mi_c, num_c, den_c, bl_c, mw_c, dc_c, dn_c = inp
        inter_log = b_c + m_st[..., None]
        m_t = jnp.maximum(inter_log, mi_c)
        s_inter = jnp.exp(inter_log - m_t)
        s_intra = jnp.exp(mi_c - m_t)
        num = (s_inter[..., None] * jnp.einsum("bhcd,bhde->bhce", q_c, c_st)
               + s_intra[..., None] * num_c)
        den = s_inter * jnp.einsum("bhcd,bhd->bhc", q_c, n_st) + s_intra * den_c
        h = num / jnp.maximum(jnp.abs(den), jnp.exp(-m_t))[..., None]
        m_new = jnp.maximum(bl_c + m_st, mw_c)
        s_old = jnp.exp(bl_c + m_st - m_new)
        s_new = jnp.exp(mw_c - m_new)
        c_st = s_old[..., None, None] * c_st + s_new[..., None, None] * dc_c
        n_st = s_old[..., None] * n_st + s_new[..., None] * dn_c
        return (c_st, n_st, m_new), h

    xs = tuple(jnp.moveaxis(a, 2, 0) for a in
               (q, bcum, m_intra, num_intra, den_intra, b_last, m_w, dc, dn))
    init = (jnp.zeros((b_, h_, dk, dv), q.dtype), jnp.zeros((b_, h_, dk), q.dtype),
            jnp.zeros((b_, h_), q.dtype))
    _, h = lax.scan(step, init, xs)
    return jnp.moveaxis(h, 0, 2).reshape(b_, h_, s_, dv)

def _gdn_group(q, k, v, z, a, bb, conv_w, a_log, dt_bias, norm_g):
    bsz, s, _ = q.shape
    qkv = jax.nn.silu(_conv_centred(jnp.concatenate([q, k, v], axis=-1).astype(jnp.float32), conv_w))
    qh = _l2norm(_to_heads(qkv[..., :GDN_QK], GDN_HEADS)) * (GDN_DK ** -0.5)
    kh = _l2norm(_to_heads(qkv[..., GDN_QK:2 * GDN_QK], GDN_HEADS))
    vh = _to_heads(qkv[..., 2 * GDN_QK:], GDN_HEADS)
    a = a.astype(jnp.float32).reshape(bsz, s, N_DIR, GDN_HEADS)
    bb = bb.astype(jnp.float32).reshape(bsz, s, N_DIR, GDN_HEADS)
    g = -jnp.exp(a_log.astype(jnp.float32)) * jax.nn.softplus(a + dt_bias.astype(jnp.float32))
    beta = jax.nn.sigmoid(bb)
    g = g.transpose(2, 0, 3, 1)
    beta = beta.transpose(2, 0, 3, 1)
    o_f = _gated_delta_rule(qh, kh, vh, g[0], beta[0])
    o_b = _flip(_gated_delta_rule(_flip(qh), _flip(kh), _flip(vh), _flip(g[1]), _flip(beta[1])))
    o = (o_f + o_b).transpose(0, 2, 1, 3)
    o = o * lax.rsqrt(jnp.mean(o * o, axis=-1, keepdims=True) + EPS) * norm_g.astype(jnp.float32)
    return o.reshape(bsz, s, GDN_V) * jax.nn.silu(z.astype(jnp.float32))

def _mlstm_group(q, k, v, o_gate, i_in, f_in, i_bias, f_bias, norm_g):
    bsz, s, _ = q.shape
    qh = _to_heads(q, MLSTM_HEADS)
    kh = _to_heads(k, MLSTM_HEADS) * (MLSTM_DK ** -0.5)
    vh = _to_heads(v, MLSTM_HEADS)
    i_pre = (i_in.astype(jnp.float32).reshape(bsz, s, N_DIR, MLSTM_HEADS)
             + i_bias.astype(jnp.float32)).transpose(2, 0, 3, 1)
    f_pre = (f_in.astype(jnp.float32).reshape(bsz, s, N_DIR, MLSTM_HEADS)
             + f_bias.astype(jnp.float32)).transpose(2, 0, 3, 1)
    h_f = _mlstm(qh, kh, vh, i_pre[0], f_pre[0])
    h_b = _flip(_mlstm(_flip(qh), _flip(kh), _flip(vh), _flip(i_pre[1]), _flip(f_pre[1])))
    h = (h_f + h_b).transpose(0, 2, 1, 3)
    h = (h * lax.rsqrt(jnp.mean(h * h, axis=-1, keepdims=True) + EPS)).reshape(bsz, s, ML_V)
    return h * norm_g.astype(jnp.float32) * jax.nn.sigmoid(o_gate.astype(jnp.float32))

def _peer(h, w_q, sub_keys, u_tab, v_tab):
    bsz, s, d = h.shape
    t = h.reshape(-1, d)
    n_tok = t.shape[0]
    qry = (t @ w_q).astype(jnp.float32).reshape(n_tok, PEER_HEADS, 2, PEER_DKEY // 2)
    scores = jnp.einsum("thpd,hpkd->thpk", qry, sub_keys.astype(jnp.float32))
    s_top, i_top = lax.top_k(scores, PEER_TOPK)
    cand = (s_top[:, :, 0, :, None] + s_top[:, :, 1, None, :]).reshape(n_tok, PEER_HEADS, -1)
    cand_idx = (i_top[:, :, 0, :, None] * PEER_NKEYS + i_top[:, :, 1, None, :]).reshape(n_tok, PEER_HEADS, -1)
    best, pos = lax.top_k(cand, PEER_TOPK)
    idx = jnp.take_along_axis(cand_idx, pos, axis=-1)
    gate = jax.nn.softmax(best, axis=-1)
    nb = n_tok // PEER_BLOCK

    def block_fn(args):
        tb, ib, gb = args
        u = u_tab[ib]
        act = jax.nn.gelu(jnp.einsum("td,thkd->thk", tb, u).astype(jnp.float32), approximate=False)
        vv = v_tab[ib]
        return jnp.einsum("thk,thkd->td", (gb * act).astype(vv.dtype), vv)

    out = lax.map(block_fn, (t.reshape(nb, PEER_BLOCK, d),
                             idx.reshape(nb, PEER_BLOCK, PEER_HEADS, PEER_TOPK),
                             gate.reshape(nb, PEER_BLOCK, PEER_HEADS, PEER_TOPK)))
    return out.reshape(bsz, s, d).astype(h.dtype)

def second_inputs(seed: int = 0) -> dict:
    key = jax.random.key(seed)
    ks = jax.random.split(key, 20)
    f32 = jnp.float32
    nrm = lambda k, shp, sc: jax.random.normal(k, shp, f32) * sc
    dt = jnp.exp(jax.random.uniform(ks[5], (DEPTH_2, N_DIR, GDN_HEADS), f32,
                                    np.log(1e-3).astype(np.float32), np.log(1e-1).astype(np.float32)))
    return {
        "x": nrm(ks[0], (BATCH, SEQ, D_MODEL), 1.0),
        "norm1_g": 1.0 + nrm(ks[1], (DEPTH_2, D_MODEL), 0.02),
        "w_in": nrm(ks[2], (DEPTH_2, D_MODEL, D_IN), D_MODEL ** -0.5),
        "conv_w": nrm(ks[3], (DEPTH_2, 2 * GDN_QK + GDN_V, CONV_K), CONV_K ** -0.5),
        "gdn_a_log": jnp.log(jax.random.uniform(ks[4], (DEPTH_2, N_DIR, GDN_HEADS), f32, 1.0, 16.0)),
        "gdn_dt_bias": jnp.log(jnp.expm1(dt)),
        "gdn_norm_g": 1.0 + nrm(ks[6], (DEPTH_2, GDN_DV), 0.02),
        "mlstm_i_bias": nrm(ks[7], (DEPTH_2, N_DIR, MLSTM_HEADS), 0.1),
        "mlstm_f_bias": jax.random.uniform(ks[8], (DEPTH_2, N_DIR, MLSTM_HEADS), f32, 3.0, 6.0),
        "mlstm_norm_g": 1.0 + nrm(ks[9], (DEPTH_2, ML_V), 0.02),
        "w_out": nrm(ks[10], (DEPTH_2, D_MIX, D_MODEL), D_MIX ** -0.5),
        "norm2_g": 1.0 + nrm(ks[11], (DEPTH_2, D_MODEL), 0.02),
        "peer_wq": nrm(ks[12], (DEPTH_2, D_MODEL, PEER_HEADS * PEER_DKEY), D_MODEL ** -0.5),
        "peer_keys": nrm(ks[13], (DEPTH_2, PEER_HEADS, 2, PEER_NKEYS, PEER_DKEY // 2), (PEER_DKEY // 2) ** -0.5),
        "peer_u": nrm(ks[14], (DEPTH_2, PEER_N, D_MODEL), D_MODEL ** -0.5),
        "peer_v": nrm(ks[15], (DEPTH_2, PEER_N, D_MODEL), PEER_HEADS ** -0.5),
        "normf_g": 1.0 + nrm(ks[16], (D_MODEL,), 0.02),
    }

def second_block(x, norm1_g, w_in, conv_w, gdn_a_log, gdn_dt_bias, gdn_norm_g, mlstm_i_bias,
              mlstm_f_bias, mlstm_norm_g, w_out, norm2_g, peer_wq, peer_keys, peer_u, peer_v,
              normf_g):
    offsets = [int(o) for o in np.cumsum(SPLIT_SIZES)[:-1]]
    for l in range(DEPTH_2):
        h = _rmsnorm(x, norm1_g[l])
        p = h @ w_in[l]
        (gq, gk, gv, gz, ga, gb, mq, mk, mv, mo, mi, mf) = jnp.split(p, offsets, axis=-1)
        y_a = _gdn_group(gq, gk, gv, gz, ga, gb, conv_w[l], gdn_a_log[l], gdn_dt_bias[l], gdn_norm_g[l])
        y_b = _mlstm_group(mq, mk, mv, mo, mi, mf, mlstm_i_bias[l], mlstm_f_bias[l], mlstm_norm_g[l])
        y = jnp.concatenate([y_a, y_b], axis=-1).astype(x.dtype)
        x = x + y @ w_out[l]
        h2 = _rmsnorm(x, norm2_g[l])
        x = x + _peer(h2, peer_wq[l], peer_keys[l], peer_u[l], peer_v[l])
    return _rmsnorm(x, normf_g)


def setup_inputs(seed=0):
    out = dict(first_inputs(seed))
    for name, value in second_inputs(seed + 1).items():
        if name != "x":
            out[name + "_2"] = value
    return out


def reference(
    x, ffn1_norm, ffn1_wi, ffn1_wo, mix_norm, w_in, mla_q_norm, mla_w_uq, mla_kv_norm,
    mla_w_ukv, mla_qk_gain_q, mla_qk_gain_k, nsa_q_gain, nsa_k_gain, cmp_pos_k, cmp_pos_v,
    cmp_wk1, cmp_wk2, cmp_wv1, cmp_wv2, proj_sb, proj_mla, proj_nsa, w_out, ffn2_norm, ffn2_wi,
    ffn2_wo, norm1_g_2, w_in_2, conv_w_2, gdn_a_log_2, gdn_dt_bias_2, gdn_norm_g_2,
    mlstm_i_bias_2, mlstm_f_bias_2, mlstm_norm_g_2, w_out_2, norm2_g_2, peer_wq_2, peer_keys_2,
    peer_u_2, peer_v_2, normf_g_2,
):
    x = first_block(
        x, ffn1_norm, ffn1_wi, ffn1_wo, mix_norm, w_in, mla_q_norm, mla_w_uq, mla_kv_norm,
        mla_w_ukv, mla_qk_gain_q, mla_qk_gain_k, nsa_q_gain, nsa_k_gain, cmp_pos_k, cmp_pos_v,
        cmp_wk1, cmp_wk2, cmp_wv1, cmp_wv2, proj_sb, proj_mla, proj_nsa, w_out, ffn2_norm,
        ffn2_wi, ffn2_wo,
    )
    return second_block(
        x, norm1_g_2, w_in_2, conv_w_2, gdn_a_log_2, gdn_dt_bias_2, gdn_norm_g_2,
        mlstm_i_bias_2, mlstm_f_bias_2, mlstm_norm_g_2, w_out_2, norm2_g_2, peer_wq_2,
        peer_keys_2, peer_u_2, peer_v_2, normf_g_2,
    )


_drawn_inputs = setup_inputs


def setup_inputs(seed=0):
    import zlib

    import numpy as np

    out = dict(_drawn_inputs(seed))
    spreads = {}
    factors = {'mla_q_norm': 4.257,
     'mla_kv_norm': 3.027,
     'mla_qk_gain_q': 4.301,
     'mla_qk_gain_k': 4.314,
     'nsa_q_gain': 4.6,
     'nsa_k_gain': 4.614,
     'gdn_norm_g_2': 17.104,
     'mlstm_i_bias_2': 31.639,
     'mlstm_norm_g_2': 21.248,
     'norm2_g_2': 9.908,
     'normf_g_2': 7.479}
    for name, (base, spread) in spreads.items():
        noise = np.random.default_rng([zlib.crc32(name.encode()), seed]).standard_normal(out[name].shape)
        drawn = base * np.exp(spread * noise) if base else spread * noise
        out[name] = __import__('jax').numpy.asarray(drawn.astype(out[name].dtype))
    for name, factor in factors.items():
        out[name] = (out[name] * factor).astype(out[name].dtype)
    return out
```

```python
from contextlib import ExitStack

import concourse.bass as bass
import numpy as np
from concourse import mybir

F32 = mybir.dt.float32
BF16 = mybir.dt.bfloat16
U32 = mybir.dt.uint32
ALU = mybir.AluOpType
ACT = mybir.ActivationFunctionType
AX = mybir.AxisListType

P = 128
SEQ = 512
TB = SEQ // P
D = 1024
DK = D // P
D_FF = 2816
EPS = 1e-6


def at(ap, i, n=1):
    return ap[i:i + n] if isinstance(i, int) else ap[bass.ds(i, n)]


def one(ap, i):
    return ap[i] if isinstance(i, int) else ap[bass.ds(i, 1)].rearrange("a p c -> (a p) c")


def column(ap, i):
    return ap[:, i, :] if isinstance(i, int) else ap[:, bass.ds(i, 1), :].rearrange("p a t -> p (a t)")


class Core:

    def __init__(self, nc, ctx):
        self.nc, self.ctx = nc, ctx
        self.taken, self.past = (ExitStack(), []), (ExitStack(), [])

    def sbuf(self, name, shape, dtype=F32):
        return self.ctx.enter_context(self.nc.sbuf_tensor(name, shape, dtype))

    def sem(self, name):
        s = self.taken[0].enter_context(self.nc.semaphore(name))
        self.taken[1].append(s)
        return s

    def zero_past(self, engine):
        for s in self.past[1]:
            engine.sem_clear(s)

    def next_stage(self):
        self.past[0].close()
        self.past, self.taken = self.taken, (ExitStack(), [])

    def zero_all(self):
        self.next_stage()
        with self.nc.Block() as block:
            @block.sync
            def _(sp):
                self.zero_past(sp)
        self.next_stage()


def chained(engine, sem):
    count = [0]

    def link(instruction):
        count[0] += 1
        instruction.then_inc(sem, 1)
        engine.wait_ge(sem, count[0])

    return link


def norm_steps(core, name):
    return {k: core.sem(f"{name}_{k}") for k in ("gain_loaded", "square_ready", "square_used", "mean_ready",
                                                  "root_ready", "normed")}


def norm_scalar(nc, act, m, s):
    for k in range(DK):
        if k >= 2:
            act.wait_ge(s["square_used"], k - 1)
        nc.scalar.activation(m.square[:, k % 2, :], m.x[:, k, :], ACT.Square).then_inc(s["square_ready"], 1)
    act.wait_ge(s["mean_ready"], 1)
    nc.scalar.activation(m.root, m.mean, ACT.Sqrt).then_inc(s["root_ready"], 1)


def norm_tensor(nc, pe, m, s):
    for k in range(DK):
        pe.wait_ge(s["square_ready"], k + 1)
        nc.tensor.matmul(m.bank[:, 0, :], m.ones[:], m.square[:, k % 2, :], start=k == 0,
                         stop=k == DK - 1).then_inc(s["square_used"], 1)


def norm_vector(nc, dve, m, s, gain):
    dve.wait_ge(s["square_used"], DK)
    nc.vector.tensor_scalar(m.mean, m.bank[:, 0, :], 1.0 / D, EPS, ALU.mult, ALU.add).then_inc(s["mean_ready"], 1)
    dve.wait_ge(s["root_ready"], 1)
    nc.vector.reciprocal(m.mean, m.root).then_inc(s["mean_ready"], 1)
    dve.wait_ge(s["mean_ready"], 2)
    dve.wait_ge(s["gain_loaded"], 16)
    for k in range(DK):
        nc.vector.scalar_tensor_tensor(m.h[:, k, :], m.x[:, k, :], gain[:, k:k + 1], m.mean,
                                       ALU.mult, ALU.mult).then_inc(s["normed"], 1)


def ffn(core, m, name, gain_dram, wi_dram, wo_dram):
    nc = core.nc
    FK = D_FF // P
    UP = 2
    DOWN = 4
    up_w = m.w[:, 0:UP * 2 * D].rearrange("p (s h k c) -> p s h k c", s=UP, h=2, k=DK)
    down_w = m.w[:, UP * 2 * D:UP * 2 * D + DOWN * D].rearrange("p (s c) -> p s c", s=DOWN)
    hidden = m.arena[:, 0:FK * SEQ].rearrange("p (k t) -> p k t", k=FK)
    silu = m.square
    wi = wi_dram.rearrange("a j p c -> (a j) p c")
    wo = wo_dram.rearrange("a k p c -> (a k) p c")

    s = norm_steps(core, name)
    up_loaded = [core.sem(f"{name}_up_loaded{i}") for i in range(UP)]
    a_done = [core.sem(f"{name}_a_done{i}") for i in range(UP)]
    b_done = [core.sem(f"{name}_b_done{i}") for i in range(UP)]
    silu_done = [core.sem(f"{name}_silu_done{i}") for i in range(UP)]
    hidden_written = [core.sem(f"{name}_hidden_written{i}") for i in range(UP)]
    down_loaded = [core.sem(f"{name}_down_loaded{i}") for i in range(DOWN)]
    down_used = [core.sem(f"{name}_down_used{i}") for i in range(DOWN)]
    down_done = core.sem(f"{name}_down_done")
    rounds = FK // UP

    with nc.Block() as block:

        @block.sync
        def _(sp):
            sp.dma_start(m.gain[:], gain_dram.rearrange("a p k -> (a p) k")).then_inc(s["gain_loaded"], 16)

            def load_up(r, i):
                sp.dma_start(m.w[:, i * 2 * D:(i + 1) * 2 * D], one(wi, r * UP + i)).then_inc(up_loaded[i], 16)

            def load_down(k, i):
                sp.dma_start(down_w[:, i, :], one(wo, k)).then_inc(down_loaded[i], 16)

            for i in range(UP):
                load_up(0, i)
            for i in range(DOWN):
                load_down(i, i)
            with sp.Fori(1, rounds) as r:
                for i in range(UP):
                    sp.wait_ge(b_done[i], r)
                    load_up(r, i)
            with sp.Fori(1, FK // DOWN) as r:
                for i in range(DOWN):
                    sp.wait_ge(down_used[i], r)
                    load_down(r * DOWN + i, i)
            for k in range(FK - FK % DOWN, FK):
                sp.wait_ge(down_used[k % DOWN], k // DOWN)
                load_down(k, k % DOWN)
            core.zero_past(sp)

        @block.tensor
        def _(pe):
            norm_tensor(nc, pe, m, s)
            pe.wait_ge(s["normed"], DK)

            def up(r, i, first):
                pe.wait_ge(up_loaded[i], r * 16 + 16)
                if not first:
                    pe.wait_ge(hidden_written[i], r)
                for half, done in ((0, a_done[i]), (1, b_done[i])):
                    for k in range(DK):
                        last = nc.tensor.matmul(m.bank[:, 2 * i + half, :], up_w[:, i, half, k, :],
                                                m.h[:, k, :], start=k == 0, stop=k == DK - 1)
                    last.then_inc(done, 1)

            for i in range(UP):
                up(0, i, True)
            with pe.Fori(1, rounds) as r:
                for i in range(UP):
                    up(r, i, False)
            for i in range(UP):
                pe.wait_ge(hidden_written[i], rounds)

            def down(k, i, r, start=False, stop=False):
                pe.wait_ge(down_loaded[i], r * 16 + 16)
                for c in range(DK):
                    rhs = column(hidden, k)
                    last = nc.tensor.matmul(m.bank[:, c, :], down_w[:, i, c * P:(c + 1) * P], rhs, start=start, stop=stop)
                    if stop:
                        last.then_inc(down_done, 1)
                if not stop:
                    last.then_inc(down_used[i], 1)

            for k in range(DOWN):
                down(k, k, 0, start=k == 0)
            with pe.Fori(1, FK // DOWN) as r:
                for i in range(DOWN):
                    down(r * DOWN + i, i, r)
            for k in range(FK - FK % DOWN, FK):
                down(k, k % DOWN, k // DOWN, stop=k == FK - 1)

        @block.scalar
        def _(act):
            norm_scalar(nc, act, m, s)

            def gate(r, i, first):
                act.wait_ge(a_done[i], r + 1)
                if not first:
                    act.wait_ge(hidden_written[i], r)
                nc.scalar.activation(silu[:, i, :], m.bank[:, 2 * i, :], ACT.Silu).then_inc(silu_done[i], 1)

            for i in range(UP):
                gate(0, i, True)
            with act.Fori(1, rounds) as r:
                for i in range(UP):
                    gate(r, i, False)

        @block.vector
        def _(dve):
            norm_vector(nc, dve, m, s, m.gain)
            with dve.Fori(0, rounds) as r:
                for i in range(UP):
                    dve.wait_ge(silu_done[i], r + 1)
                    dve.wait_ge(b_done[i], r + 1)
                    out = column(hidden, r * UP + i)
                    nc.vector.tensor_tensor(out, silu[:, i, :], m.bank[:, 2 * i + 1, :], ALU.mult)\
                        .then_inc(hidden_written[i], 1)
            for c in range(DK):
                dve.wait_ge(down_done, c + 1)
                nc.vector.scalar_tensor_tensor(m.x[:, c, :], m.bank[:, c, :], 0.5, m.x[:, c, :], ALU.mult, ALU.add)


HEADS, HD, GROUPS = 8, 64, 2
HW = HEADS * HD
Q_LORA, KV_LORA, ROPE = 256, 128, 32
QK_MLA = HD + ROPE
KV_W = GROUPS * HD
BRANCHES = 3
TOK_SIZES = dict(sb_v=HW, cq=Q_LORA, ckv=KV_LORA, kr=ROPE, nq=HW, ck=KV_W, cv=KV_W, sk=KV_W, sv=KV_W, wk=KV_W,
                 wv=KV_W, gate=BRANCHES * HEADS)
TOK_W = sum(TOK_SIZES.values())
TOK_AT = {}
for _name, _size in TOK_SIZES.items():
    TOK_AT[_name] = sum(TOK_SIZES[n] for n in TOK_AT)
TOK_STEPS = 6
TOK_C = TOK_W // TOK_STEPS
assert TOK_C * TOK_STEPS == TOK_W and TOK_C <= SEQ
CMP_LEN, CMP_STRIDE, CMP_HIDDEN = 32, 16, 128
N_CMP = (SEQ - CMP_LEN) // CMP_STRIDE + 1
NEG = -1e30


def tok(m, name):
    return m.tok[:, :, TOK_AT[name]:TOK_AT[name] + TOK_SIZES[name]]


def in_projection(core, m, gain_dram, qk_dram, tok_dram):
    nc = core.nc
    SLOTS = 2
    QK_STEPS = 2 * HW // P
    qk_w = m.w[:, 0:SLOTS * D].rearrange("p (s k c) -> p s k c", s=SLOTS, k=DK)
    tok_w = m.w[:, SLOTS * D:SLOTS * (D + DK * TOK_C)].rearrange("p (s k c) -> p s k c", s=SLOTS, k=DK)
    s = norm_steps(core, "mix")
    qk_loaded = [core.sem(f"qk_loaded{i}") for i in range(SLOTS)]
    qk_done = [core.sem(f"qk_done{i}") for i in range(SLOTS)]
    qk_copied = [core.sem(f"qk_copied{i}") for i in range(SLOTS)]
    tok_loaded = [core.sem(f"tok_loaded{i}") for i in range(SLOTS)]
    tok_done = [core.sem(f"tok_done{i}") for i in range(SLOTS)]
    tok_copied_act = [core.sem(f"tok_copied_act{i}") for i in range(SLOTS)]
    tok_copied_dve = [core.sem(f"tok_copied_dve{i}") for i in range(SLOTS)]
    qk_rounds, tok_rounds = QK_STEPS // SLOTS, TOK_STEPS // SLOTS

    with nc.Block() as block:
        @block.sync
        def _(sp):
            sp.dma_start(m.gain[:], gain_dram.rearrange("a p k -> (a p) k")).then_inc(s["gain_loaded"], 16)
            qk_in = qk_dram.rearrange("a j p c -> (a j) p c")
            tok_in = tok_dram.rearrange("a j p c -> (a j) p c")

            def load_qk(r, i):
                sp.dma_start(m.w[:, i * D:(i + 1) * D], one(qk_in, r * SLOTS + i)).then_inc(qk_loaded[i], 16)

            def load_tok(r, i):
                dst = tok_w[:, i].rearrange("p k c -> p (k c)")
                sp.dma_start(dst, one(tok_in, r * SLOTS + i)).then_inc(tok_loaded[i], 16)

            for i in range(SLOTS):
                load_qk(0, i)
            for i in range(SLOTS):
                load_tok(0, i)
            with sp.Fori(1, qk_rounds) as r:
                for i in range(SLOTS):
                    sp.wait_ge(qk_done[i], r)
                    load_qk(r, i)
            with sp.Fori(1, tok_rounds) as r:
                for i in range(SLOTS):
                    sp.wait_ge(tok_done[i], r)
                    load_tok(r, i)
            core.zero_past(sp)

        @block.tensor
        def _(pe):
            norm_tensor(nc, pe, m, s)
            pe.wait_ge(s["normed"], DK)

            def qk(r, i, first):
                pe.wait_ge(qk_loaded[i], r * 16 + 16)
                if not first:
                    pe.wait_ge(qk_copied[i], r)
                for k in range(DK):
                    last = nc.tensor.matmul(m.bank[:, i, :], qk_w[:, i, k, :], m.h[:, k, :], start=k == 0,
                                            stop=k == DK - 1)
                last.then_inc(qk_done[i], 1)

            for i in range(SLOTS):
                qk(0, i, True)
            with pe.Fori(1, qk_rounds) as r:
                for i in range(SLOTS):
                    qk(r, i, False)
            for i in range(SLOTS):
                pe.wait_ge(qk_copied[i], qk_rounds)

            def by_token(r, i, first):
                pe.wait_ge(tok_loaded[i], r * 16 + 16)
                if not first:
                    pe.wait_ge(tok_copied_act[i], r)
                    pe.wait_ge(tok_copied_dve[i], r)
                for t in range(TB):
                    for k in range(DK):
                        last = nc.tensor.matmul(m.bank[:, i * TB + t, 0:TOK_C], m.h[:, k, t * P:(t + 1) * P],
                                                tok_w[:, i, k, :], start=k == 0, stop=k == DK - 1)
                last.then_inc(tok_done[i], 1)

            for i in range(SLOTS):
                by_token(0, i, True)
            with pe.Fori(1, tok_rounds) as r:
                for i in range(SLOTS):
                    by_token(r, i, False)

        def tok_out(r, i, t):
            return m.tok[:, t, bass.ds((r * SLOTS + i) * TOK_C, TOK_C)]

        @block.scalar
        def _(act):
            norm_scalar(nc, act, m, s)
            with act.Fori(0, qk_rounds) as r:
                for i in range(SLOTS):
                    act.wait_ge(qk_done[i], r + 1)
                    nc.scalar.copy(column(m.sbqk, r * SLOTS + i), m.bank[:, i, :]).then_inc(qk_copied[i], 1)
            with act.Fori(0, tok_rounds) as r:
                for i in range(SLOTS):
                    act.wait_ge(tok_done[i], r + 1)
                    for t in (0, 1):
                        last = nc.scalar.copy(tok_out(r, i, t), m.bank[:, i * TB + t, 0:TOK_C])
                    last.then_inc(tok_copied_act[i], 1)

        @block.vector
        def _(dve):
            norm_vector(nc, dve, m, s, m.gain)
            with dve.Fori(0, tok_rounds) as r:
                for i in range(SLOTS):
                    dve.wait_ge(tok_done[i], r + 1)
                    for t in (2, 3):
                        last = nc.vector.tensor_copy(tok_out(r, i, t), m.bank[:, i * TB + t, 0:TOK_C])
                    last.then_inc(tok_copied_dve[i], 1)


def swapped(ap, heads, width):
    return ap.rearrange("p h (two c) -> p h two c", two=2)[:, :, ::-1, :]


def spread(ap, heads):
    return ap.rearrange("p (one c) -> p one c", one=1).broadcast_to([ap.shape[0], heads, ap.shape[1]])


def per_head(ap, width):
    return ap.rearrange("p (h one) -> p h one", one=1).broadcast_to([ap.shape[0], ap.shape[1], width])


def mla_prepare(core, m, uq_dram, ukv_dram, norm_dram, gain_dram):
    nc = core.nc
    NQ, NKV = HEADS * QK_MLA, HEADS * 2 * HD
    w_uq = m.w[:, 8192:8192 + 2 * NQ].rearrange("p (k c) -> p k c", k=2)
    w_ukv = m.w[:, 8192 + 2 * NQ:8192 + 2 * NQ + NKV]
    latent = m.z[:, 4096:4096 + 1536].rearrange("p (t c) -> p t c", t=TB)
    latent_t = m.late[:, 0:1536].rearrange("p (k t) -> p k t", k=3)
    q_tok = m.z[:, 4096:4096 + NQ]
    k_tok = m.z[:, 4096 + NQ:4096 + 2 * NQ]
    turn = m.z[:, 7168 - 1024:7168 - 1024 + 4 * HEADS * ROPE].rearrange("p (n h c) -> p n h c", n=4, h=HEADS)
    squares = m.square.rearrange("p a b -> p (a b)")
    sums = m.small[:, 0:8]
    head_sums = m.small[:, 8:24]
    gains = m.small[:, 24:27]
    head_gain = m.small[:, 32:32 + 2 * QK_MLA]
    loaded, weights_loaded = core.sem("mla_gains_loaded"), core.sem("mla_weights_loaded")
    squared, root_in, rooted = core.sem("mla_squared"), core.sem("mla_root_in"), core.sem("mla_rooted")
    latent_ready, turned, latent_copied = (core.sem(f"mla_latent_{n}") for n in ("ready", "turned", "copied"))
    up_done, up_copied = core.sem("mla_up_done"), core.sem("mla_up_copied")
    key_ready, key_scale = core.sem("mla_key_ready"), core.sem("mla_key_scale")
    q_ready, k_ready = core.sem("mla_q_ready"), core.sem("mla_k_ready")
    heads_turned, heads_copied = core.sem("mla_heads_turned"), core.sem("mla_heads_copied")
    dve_chain, pool_chain = core.sem("mla_dve_chain"), core.sem("mla_pool_chain")
    cq_ckv = m.tok[:, :, TOK_AT["cq"]:TOK_AT["cq"] + Q_LORA + KV_LORA]

    with nc.Block() as block:
        @block.sync
        def _(sp):
            sp.dma_start(gains, norm_dram.rearrange("a p c -> (a p) c")).then_inc(loaded, 16)
            sp.dma_start(head_gain, gain_dram.rearrange("a p c -> (a p) c")).then_inc(loaded, 16)
            sp.dma_start(m.w[:, 8192:8192 + 2 * NQ], uq_dram.rearrange("a p c -> (a p) c")).then_inc(weights_loaded, 16)
            sp.dma_start(w_ukv, ukv_dram.rearrange("a p c -> (a p) c")).then_inc(weights_loaded, 16)
            core.zero_past(sp)

        @block.scalar
        def _(act):
            for t in range(TB):
                nc.scalar.activation(m.scratch[:, t * 384:t * 384 + Q_LORA], cq_ckv[:, t, 0:Q_LORA], ACT.Square,
                                     accum_out=sums[:, t:t + 1])
                last = nc.scalar.activation(m.scratch[:, t * 384 + Q_LORA:(t + 1) * 384], cq_ckv[:, t, Q_LORA:], ACT.Square,
                                            accum_out=sums[:, TB + t:TB + t + 1])
            last.then_inc(squared, 1)
            act.wait_ge(root_in, 1)
            nc.scalar.activation(sums, sums, ACT.Sqrt).then_inc(rooted, 1)
            act.wait_ge(loaded, 32)
            for c in range(3):
                act.wait_ge(turned, c + 1)
                nc.scalar.activation(latent_t[:, c, :], m.bank[:, c, :], ACT.Copy, scale=gains[:, c:c + 1])\
                    .then_inc(latent_copied, 1)

            def copy_heads(t):
                for i, to in enumerate((m.mla_q, m.mla_q, m.mla_k, m.mla_k)):
                    act.wait_ge(heads_turned, 4 * t + i + 1)
                    h0 = (i % 2) * 4
                    nc.scalar.copy(to[:, h0:h0 + 4, t * P:(t + 1) * P],
                                   m.bank[0:QK_MLA, 4 + i, :].rearrange("p (h t) -> p h t", h=4))\
                        .then_inc(heads_copied, 1)

            for t in range(TB):
                act.wait_ge(up_done, t + 1)
                if t >= 1:
                    act.wait_ge(heads_turned, 4 * t)
                for i in range(2):
                    nc.scalar.copy(q_tok[:, i * 384:(i + 1) * 384], m.bank[:, i, 0:384])
                    last = nc.scalar.copy(m.mla_kv[:, t, i * 512:(i + 1) * 512], m.bank[:, 2 + i, :])
                last.then_inc(up_copied, 1)
                act.wait_ge(root_in, t + 2)
                nc.scalar.activation(head_sums, head_sums, ACT.Sqrt).then_inc(rooted, 1)
                copy_heads(t)

        @block.tensor
        def _(pe):
            pe.wait_ge(latent_ready, 1)
            for c in range(3):
                for t in range(TB):
                    last = nc.tensor.transpose(m.bank[:, c, t * P:(t + 1) * P], latent[:, t, c * P:(c + 1) * P],
                                               m.ident[:])
                last.then_inc(turned, 1)
            pe.wait_ge(weights_loaded, 32)
            pe.wait_ge(latent_copied, 3)

            def up(t):
                if t >= 1:
                    pe.wait_ge(up_copied, t)
                tokens = slice(t * P, (t + 1) * P)
                for i in range(2):
                    for k in range(2):
                        nc.tensor.matmul(m.bank[:, i, 0:384], latent_t[:, k, tokens], w_uq[:, k, i * 384:(i + 1) * 384],
                                         start=k == 0, stop=k == 1)
                for i in range(2):
                    last = nc.tensor.matmul(m.bank[:, 2 + i, :], latent_t[:, 2, tokens], w_ukv[:, i * 512:(i + 1) * 512],
                                            start=True, stop=True)
                last.then_inc(up_done, 1)

            up(0)
            for t in range(TB):
                if t + 1 < TB:
                    up(t + 1)
                for i, (src, ready) in enumerate(((q_tok, q_ready), (q_tok, q_ready), (k_tok, k_ready), (k_tok, k_ready))):
                    pe.wait_ge(ready, t + 1)
                    if t >= 1:
                        pe.wait_ge(heads_copied, 4 * (t - 1) + i + 1)
                    for j in range(4):
                        h = (i % 2) * 4 + j
                        last = nc.tensor.transpose(m.bank[0:QK_MLA, 4 + i, j * P:(j + 1) * P],
                                                   src[:, h * QK_MLA:(h + 1) * QK_MLA], m.ident[:])
                    last.then_inc(heads_turned, 1)

        def rotate(eng, link, heads, t, tmp):
            x = heads[:, :, HD:QK_MLA]
            link(eng.tensor_tensor(tmp[:, 0], x, spread(m.mla_cos[:, t, :], HEADS), ALU.mult))
            link(eng.tensor_tensor(tmp[:, 1].rearrange("p h (two c) -> p h two c", two=2), swapped(x, HEADS, ROPE),
                                   spread(m.mla_sin[:, t, :], HEADS).rearrange("p h (two c) -> p h two c", two=2),
                                   ALU.mult))
            return eng.tensor_tensor(x, tmp[:, 0], tmp[:, 1], ALU.add)

        @block.vector
        def _(dve):
            link = chained(dve, dve_chain)
            dve.wait_ge(squared, 1)
            link(nc.vector.tensor_scalar(sums[:, 0:TB], sums[:, 0:TB], 1.0 / Q_LORA, EPS, ALU.mult, ALU.add))
            nc.vector.tensor_scalar(sums[:, TB:], sums[:, TB:], 1.0 / KV_LORA, EPS, ALU.mult, ALU.add).then_inc(root_in, 1)
            dve.wait_ge(rooted, 1)
            link(nc.vector.reciprocal(sums, sums))
            for t in range(TB):
                nc.vector.tensor_scalar(latent[:, t, 0:Q_LORA], cq_ckv[:, t, 0:Q_LORA], sums[:, t:t + 1], None, ALU.mult)
                last = nc.vector.tensor_scalar(latent[:, t, Q_LORA:], cq_ckv[:, t, Q_LORA:], sums[:, TB + t:TB + t + 1],
                                               None, ALU.mult)
            last.then_inc(latent_ready, 1)
            dve.wait_ge(loaded, 32)
            q = q_tok.rearrange("p (h c) -> p h c", h=HEADS)
            k = k_tok.rearrange("p (h c) -> p h c", h=HEADS)
            sq = squares[:, 0:NQ]
            for t in range(TB):
                dve.wait_ge(up_copied, t + 1)
                if t >= 1:
                    dve.wait_ge(heads_turned, 4 * t)
                nc.vector.tensor_copy(k[:, :, 0:HD], m.mla_kv[:, t, :].rearrange("p (h c) -> p h c", h=HEADS)[:, :, 0:HD])
                link(nc.vector.tensor_copy(k[:, :, HD:QK_MLA], spread(tok(m, "kr")[:, t, :], HEADS)))
                link(nc.vector.tensor_tensor(sq, k_tok, k_tok, ALU.mult))
                link(nc.vector.tensor_reduce(head_sums[:, 8:16], sq.rearrange("p (h c) -> p h c", h=HEADS), AX.X, ALU.add))
                link(nc.vector.tensor_tensor(sq, q_tok, q_tok, ALU.mult))
                link(nc.vector.tensor_reduce(head_sums[:, 0:8], sq.rearrange("p (h c) -> p h c", h=HEADS), AX.X, ALU.add))
                nc.vector.tensor_scalar(head_sums, head_sums, 1.0 / QK_MLA, EPS, ALU.mult, ALU.add).then_inc(root_in, 1)
                dve.wait_ge(rooted, t + 2)
                link(nc.vector.reciprocal(head_sums, head_sums))
                nc.vector.tensor_copy(m.small[:, 240:248], head_sums[:, 8:16]).then_inc(key_scale, 1)
                link(nc.vector.tensor_scalar(head_sums[:, 0:8], head_sums[:, 0:8], QK_MLA ** -0.5, None, ALU.mult))
                link(nc.vector.tensor_tensor(q, q, per_head(head_sums[:, 0:8], QK_MLA), ALU.mult))
                link(nc.vector.tensor_tensor(q, q, spread(head_gain[:, 0:QK_MLA], HEADS), ALU.mult))
                rotate(nc.vector, link, q, t, turn[:, 0:2]).then_inc(q_ready, 1)
                dve.wait_ge(q_ready, t + 1)

        @block.gpsimd
        def _(pool):
            link = chained(pool, pool_chain)
            pool.wait_ge(loaded, 32)
            k = k_tok.rearrange("p (h c) -> p h c", h=HEADS)
            for t in range(TB):
                pool.wait_ge(key_scale, t + 1)
                link(nc.gpsimd.tensor_tensor(k, k, per_head(m.small[:, 240:248], QK_MLA), ALU.mult))
                link(nc.gpsimd.tensor_tensor(k, k, spread(head_gain[:, QK_MLA:], HEADS), ALU.mult))
                rotate(nc.gpsimd, link, k, t, turn[:, 2:4]).then_inc(k_ready, 1)
                pool.wait_ge(k_ready, t + 1)


def attention(core, m, name, q_of, k_of, v_of, mask, stick=False, gate=None, add=False, out=None):
    nc = core.nc
    UNITS = TB * HEADS
    RING = 3
    SBANK, TBANK, OBANK, XBANK = 0, 3, 5, 7
    probs, turned_p = m.probs, m.turned_p
    score_done, max_done, exp_done = (core.sem(f"{name}_{n}") for n in ("score_done", "max_done", "exp_done"))
    p_turned, p_copied, pv_done = (core.sem(f"{name}_{n}") for n in ("p_turned", "p_copied", "pv_done"))
    o_ready, o_turned, o_copied = (core.sem(f"{name}_{n}") for n in ("o_ready", "o_turned", "o_copied"))
    broken, chain = core.sem(f"{name}_broken"), core.sem(f"{name}_chain")

    def unit(n):
        return n // HEADS, n % HEADS, (n // HEADS + 1) * P

    with nc.Block() as block:
        @block.sync
        def _(sp):
            core.zero_past(sp)

        @block.tensor
        def _(pe):
            def score(n):
                b, h, keys = unit(n)
                if n >= RING:
                    pe.wait_ge(exp_done, n - RING + 1)
                bank = m.bank[:, SBANK + n % RING, 0:keys]
                nc.tensor.matmul(bank, q_of(h, b), k_of(h, keys), start=True, stop=False)
                nc.tensor.matmul(bank[:, b * P:keys], m.ident_bf[:], mask[:], start=False, stop=True)\
                    .then_inc(score_done, 1)

            def turn(n):
                b, h, keys = unit(n)
                pe.wait_ge(broken if stick else exp_done, n + 1)
                if n >= 2:
                    pe.wait_ge(p_copied, n - 1)
                for kb in range(b + 1):
                    last = nc.tensor.transpose(m.bank[:, TBANK + n % 2, kb * P:(kb + 1) * P],
                                               probs[:, n % RING, kb * P:(kb + 1) * P], m.ident[:])
                last.then_inc(p_turned, 1)

            def product(n):
                b, h, keys = unit(n)
                pe.wait_ge(p_copied, n + 1)
                if h == 0 and b >= 2:
                    pe.wait_ge(o_ready, b - 1)
                for kb in range(b + 1):
                    last = nc.tensor.matmul(m.bank[:, OBANK + b % 2, h * HD:(h + 1) * HD],
                                            turned_p[:, n % RING, kb * P:(kb + 1) * P], v_of(h, kb),
                                            start=kb == 0, stop=kb == b)
                last.then_inc(pv_done, 1)

            def turn_out(b):
                pe.wait_ge(o_ready, b + 1)
                if b >= 1:
                    pe.wait_ge(o_copied, b)
                for c in range(HW // P):
                    last = nc.tensor.transpose(m.bank[:, XBANK, c * P:(c + 1) * P], m.otok[:, b, c * P:(c + 1) * P],
                                               m.ident[:])
                last.then_inc(o_turned, 1)

            for n in range(UNITS + 8):
                if n < UNITS:
                    score(n)
                if 0 <= n - 1 < UNITS:
                    turn(n - 1)
                if 0 <= n - 2 < UNITS:
                    product(n - 2)
                b, late = divmod(n - 6, HEADS)
                if out is not None and late == 0 and 1 <= b <= TB:
                    turn_out(b - 1)

        @block.scalar
        def _(act):
            def copy_out(b):
                act.wait_ge(o_turned, b + 1)
                nc.scalar.copy(out[:, :, b * P:(b + 1) * P], m.bank[:, XBANK, :].rearrange("p (c t) -> p c t", c=HW // P))\
                    .then_inc(o_copied, 1)

            for n in range(UNITS + 9):
                if n < UNITS:
                    b, h, keys = unit(n)
                    bank = m.bank[:, SBANK + n % RING, 0:keys]
                    if stick:
                        act.wait_ge(score_done, n + 1)
                        if n >= RING:
                            act.wait_ge(broken, n - RING + 1)
                        nc.scalar.activation(m.odds[:, n % RING, 0:keys], bank, ACT.Sigmoid, scale=HD ** -0.5)
                        nc.scalar.activation(m.rest[:, n % RING, 0:keys], bank, ACT.Sigmoid, scale=-HD ** -0.5)\
                            .then_inc(exp_done, 1)
                    else:
                        act.wait_ge(max_done, n + 1)
                        if n >= RING:
                            act.wait_ge(p_turned, n - RING + 1)
                        nc.scalar.activation(probs[:, n % RING, 0:keys], bank, ACT.Exp, bias=m.neg_max[:, n % RING:n % RING + 1],
                                             accum_out=m.sums[:, b, h:h + 1]).then_inc(exp_done, 1)
                b, late = divmod(n - 7, HEADS)
                if out is not None and late == 0 and 1 <= b <= TB:
                    copy_out(b - 1)

        @block.vector
        def _(dve):
            link = chained(dve, chain)

            def copy_turned(n):
                b, h, keys = unit(n)
                dve.wait_ge(p_turned, n + 1)
                if n >= RING:
                    dve.wait_ge(pv_done, n - RING + 1)
                nc.vector.tensor_copy(turned_p[:, n % RING, 0:keys], m.bank[:, TBANK + n % 2, 0:keys]).then_inc(p_copied, 1)

            def finish(b):
                dve.wait_ge(pv_done, (b + 1) * HEADS)
                o = m.bank[:, OBANK + b % 2, :].rearrange("p (h c) -> p h c", h=HEADS)
                to = m.otok[:, b, :].rearrange("p (h c) -> p h c", h=HEADS)
                if stick:
                    nc.vector.tensor_copy(to, o).then_inc(o_ready, 1)
                    return
                factor = m.sums[:, b, :]
                link(nc.vector.reciprocal(factor, factor))
                if gate is not None:
                    link(nc.vector.tensor_tensor(factor, factor, gate(b), ALU.mult))
                if not add:
                    nc.vector.tensor_tensor(to, o, per_head(factor, HD), ALU.mult).then_inc(o_ready, 1)
                    return
                part = m.part.rearrange("p (h c) -> p h c", h=HEADS)
                link(nc.vector.tensor_tensor(part, o, per_head(factor, HD), ALU.mult))
                nc.vector.tensor_tensor(to, to, part, ALU.add).then_inc(o_ready, 1)
                dve.wait_ge(o_ready, b + 1)

            if stick:
                link(nc.vector.memset(m.ones_row[:], 1.0))
                link(nc.vector.memset(m.left.rearrange("p n k -> p (n k)"), 1.0))
            for n in range(UNITS + 6):
                if n < UNITS:
                    b, h, keys = unit(n)
                    slot = n % RING
                    if stick:
                        dve.wait_ge(exp_done, n + 1)
                        if n >= RING:
                            dve.wait_ge(broken, n - RING + 1)
                        nc.vector.tensor_tensor_scan(m.left[:, slot, 0:keys][:, ::-1], m.rest[:, slot, 0:keys][:, ::-1],
                                                     m.ones_row[:, 0:keys], 1.0, ALU.mult, ALU.mult).then_inc(max_done, 1)
                    else:
                        dve.wait_ge(score_done, n + 1)
                        if n >= RING:
                            dve.wait_ge(exp_done, n - RING + 1)
                        nc.vector.tensor_reduce(m.neg_max[:, slot:slot + 1], m.bank[:, SBANK + slot, 0:keys], AX.X, ALU.max,
                                                negate=True).then_inc(max_done, 1)
                if 0 <= n - 1 < UNITS:
                    copy_turned(n - 1)
                b, late = divmod(n - 4, HEADS)
                if late == 0 and 1 <= b <= TB:
                    finish(b - 1)

        if stick:
            @block.gpsimd
            def _(pool):
                for n in range(UNITS):
                    b, h, keys = unit(n)
                    slot = n % RING
                    pool.wait_ge(max_done, n + 1)
                    if n >= RING:
                        pool.wait_ge(p_turned, n - RING + 1)
                    nc.gpsimd.tensor_tensor(probs[:, slot, 0:keys], m.odds[:, slot, 0:keys], m.left[:, slot, 1:keys + 1],
                                            ALU.mult).then_inc(broken, 1)


def constants():
    def angles(width, positions):
        half = width // 2
        inv = np.exp(np.float32(-np.log(10000.0)) * np.arange(half, dtype=np.float32) * np.float32(2.0 / width))
        ang = positions.astype(np.float32)[:, None] * inv.astype(np.float32)[None, :]
        c, s = np.cos(ang), np.sin(ang)
        return np.concatenate([c, c], 1), np.concatenate([-s, s], 1)

    def by_block(table):
        return table.reshape(TB, P, -1).transpose(1, 0, 2).reshape(P, -1)

    def rows(table):
        out = np.zeros((P, table.shape[1]), np.float32)
        out[:len(table)] = table
        return out

    pos = np.arange(SEQ)
    ends = np.arange(N_CMP) * CMP_STRIDE + CMP_LEN - 1
    i = np.arange(P)
    (mla_cos, mla_sin), (nsa_cos, nsa_sin), (end_cos, end_sin) = angles(ROPE, pos), angles(HD, pos), angles(HD, ends)
    seen = ends[None, :] <= pos[:, None]
    return {
        "ident": np.eye(P),
        "causal": np.where(i[None, :] <= i[:, None], 0.0, NEG),
        "strict": np.where(i[None, :] < i[:, None], 0.0, NEG),
        "mla_cos": by_block(mla_cos), "mla_sin": by_block(mla_sin),
        "nsa_cos": by_block(nsa_cos), "nsa_sin": by_block(nsa_sin),
        "end_cos": rows(end_cos), "end_sin": rows(end_sin),
        "cmp_fill": by_block(np.where(seen, 0.0, NEG)), "cmp_seen": by_block(seen.astype(np.float32)),
    }


def const_array():
    return np.concatenate([np.asarray(v, np.float32) for v in constants().values()], axis=1)


def const_places():
    places, n = {}, 0
    for name, table in constants().items():
        places[name] = (n, n + table.shape[1])
        n += table.shape[1]
    return places, n


def nsa_prepare(core, m, w1_dram, small_dram, gain_dram):
    nc = core.nc
    HID = CMP_LEN * CMP_HIDDEN
    w1 = m.w[:, 0:2 * HID].rearrange("p (kv l h) -> p kv l h", kv=2, l=CMP_LEN)
    NH = HEADS + 2 * GROUPS
    KH = 2 * GROUPS
    q_tok = m.z[:, 0:HW]
    k_tok = m.z[:, 512:512 + KH * HD]
    k_twice = m.z[:, 768:768 + 2 * KH * HD]
    turn_q = m.z[:, 1280:1280 + 2 * HW].rearrange("p (n h c) -> p n h c", n=2, h=HEADS)
    turn_k = m.z[:, 2304:2304 + 2 * KH * HD].rearrange("p (n h c) -> p n h c", n=2, h=KH)
    windows = m.z[:, 2816:2816 + 2 * N_CMP * CMP_LEN].rearrange("p (kv n l) -> p kv n l", kv=2, l=CMP_LEN)
    hidden = m.z[:, 4800:4800 + 4 * N_CMP].rearrange("p (g n) -> p g n", g=4)
    kc_tok = m.z[0:N_CMP, 4928:4928 + 128].rearrange("p (h c) -> p h c", h=GROUPS)
    kc_turn = m.z[0:N_CMP, 5056:5056 + 256].rearrange("p (n h c) -> p n h c", n=2, h=GROUPS)
    kc_twice = m.z[0:N_CMP, 5312:5312 + 256]
    squares = m.square.rearrange("p a b -> p (a b)")
    sums = m.small[:, 0:TB * NH].rearrange("p (t h) -> p t h", t=TB)
    kc_sums = m.small[0:N_CMP, TB * NH:TB * NH + GROUPS]
    gains = m.nsa_small[:, 0:2 * HD]
    place = m.nsa_small[:, 2 * HD:2 * HD + 2 * CMP_LEN].rearrange("p (kv l) -> p kv l", kv=2)
    w2 = m.nsa_small[:, 192:192 + 2 * HD].rearrange("p (kv c) -> p kv c", kv=2)

    w1_loaded, small_loaded = core.sem("nsa_w1_loaded"), core.sem("nsa_small_loaded")
    squared, summed, mean_ready, rooted, scales_ready = (
        core.sem(f"nsa_{n}") for n in ("squared", "summed", "mean_ready", "rooted", "scales_ready"))
    q_ready, k_ready, turned, copied = (core.sem(f"nsa_{n}") for n in ("q_ready", "k_ready", "turned", "copied"))
    cmp_turned, windows_ready, hidden_done, hidden_ready, cmp_done = (
        core.sem(f"nsa_cmp_{n}") for n in ("turned", "windows_ready", "hidden_done", "hidden_ready", "done"))
    vc_copied, kc_ready, kc_turned, kc_squared, kc_rooted = (
        core.sem(f"nsa_{n}") for n in ("vc_copied", "kc_ready", "kc_turned", "kc_squared", "kc_rooted"))
    gates_ready = core.sem("nsa_gates_ready")
    dve_chain, pool_chain = core.sem("nsa_dve_chain"), core.sem("nsa_pool_chain")

    with nc.Block() as block:
        @block.sync
        def _(sp):
            sp.dma_start(m.nsa_small[:], small_dram.rearrange("a p c -> (a p) c")).then_inc(small_loaded, 16)
            sp.dma_start(m.w[:, 0:2 * HID], w1_dram.rearrange("a p c -> (a p) c")).then_inc(w1_loaded, 16)
            core.zero_past(sp)

        @block.scalar
        def _(act):
            for t in range(TB):
                if t >= 1:
                    act.wait_ge(summed, t)
                nc.scalar.activation(squares[:, 0:HW], tok(m, "nq")[:, t, :], ACT.Square)
                nc.scalar.activation(squares[:, HW:HW + KV_W], tok(m, "sk")[:, t, :], ACT.Square)
                nc.scalar.activation(squares[:, HW + KV_W:HW + 2 * KV_W], tok(m, "wk")[:, t, :], ACT.Square)\
                    .then_inc(squared, 1)
            act.wait_ge(mean_ready, 1)
            nc.scalar.activation(sums, sums, ACT.Sqrt).then_inc(rooted, 1)
            nc.scalar.activation(tok(m, "gate"), tok(m, "gate"), ACT.Sigmoid).then_inc(gates_ready, 1)
            act.wait_ge(hidden_done, 2)
            for g in range(GROUPS):
                nc.scalar.activation(hidden[:, 2 * g:2 * g + 2, :],
                                     m.bank[:, 6 + g, 0:2 * N_CMP].rearrange("p (kv n) -> p kv n", kv=2),
                                     ACT.Gelu_apprx_tanh).then_inc(hidden_ready, 1)
            act.wait_ge(cmp_done, 1)
            nc.scalar.copy(m.v_cmp, m.bank[0:N_CMP, 4, 2 * HD:4 * HD].rearrange("p (g c) -> p g c", g=GROUPS))\
                .then_inc(vc_copied, 1)
            for t in range(TB):
                act.wait_ge(turned, 2 * t + 1)
                tokens = slice(t * P, (t + 1) * P)
                nc.scalar.copy(m.nsa_q[:, :, tokens], m.bank[:, 2 * (t % 2), :].rearrange("p (c t) -> p c t", c=4))\
                    .then_inc(copied, 1)
                act.wait_ge(turned, 2 * t + 2)
                nc.scalar.copy(m.nsa_k[:, :, tokens], m.bank[:, 2 * (t % 2) + 1, :].rearrange("p (c t) -> p c t", c=4))\
                    .then_inc(copied, 1)
            act.wait_ge(kc_squared, 1)
            nc.scalar.activation(kc_sums, kc_sums, ACT.Sqrt).then_inc(kc_rooted, 1)
            act.wait_ge(kc_turned, 1)
            nc.scalar.copy(m.k_cmp, m.bank[:, 5, 0:GROUPS * N_CMP].rearrange("p (g n) -> p g n", g=GROUPS))

        @block.tensor
        def _(pe):
            for i, name in enumerate(("ck", "cv")):
                for t in range(TB):
                    last = nc.tensor.transpose(m.bank[:, 4 + i, t * P:(t + 1) * P], tok(m, name)[:, t, :], m.ident[:])
            last.then_inc(cmp_turned, 1)
            pe.wait_ge(w1_loaded, 16)
            pe.wait_ge(windows_ready, 4)
            for kv in range(2):
                for l in range(CMP_LEN):
                    for g in range(GROUPS):
                        half = slice(g * HD, (g + 1) * HD)
                        last = nc.tensor.matmul(m.bank[:, 6 + g, kv * N_CMP:(kv + 1) * N_CMP], w1[half, kv, l, :],
                                                windows[half, kv, :, l], start=l == 0, stop=l == CMP_LEN - 1)
                last.then_inc(hidden_done, 1)
            pe.wait_ge(hidden_ready, 2)
            for kv in range(2):
                for g in range(GROUPS):
                    last = nc.tensor.matmul(m.bank[0:N_CMP, 4, (kv * 2 + g) * HD:(kv * 2 + g + 1) * HD],
                                            hidden[:, 2 * g + kv, :], w2[:, kv, :], start=True, stop=True)
            last.then_inc(cmp_done, 1)
            for t in range(TB):
                pe.wait_ge(q_ready, t + 1)
                if t >= 2:
                    pe.wait_ge(copied, 2 * (t - 1))
                for c in range(4):
                    last = nc.tensor.transpose(m.bank[:, 2 * (t % 2), c * P:(c + 1) * P], q_tok[:, c * P:(c + 1) * P],
                                               m.ident[:])
                last.then_inc(turned, 1)
                pe.wait_ge(k_ready, t + 1)
                for c in range(4):
                    last = nc.tensor.transpose(m.bank[:, 2 * (t % 2) + 1, c * P:(c + 1) * P], k_twice[:, c * P:(c + 1) * P],
                                               m.ident[:])
                last.then_inc(turned, 1)
            pe.wait_ge(kc_ready, 1)
            for g in range(GROUPS):
                last = nc.tensor.transpose(m.bank[:, 5, g * N_CMP:(g + 1) * N_CMP], kc_twice[:, g * P:(g + 1) * P],
                                           m.ident[0:N_CMP, 0:N_CMP])
            last.then_inc(kc_turned, 1)

        def rotate(eng, link, x, cos, sin, tmp, heads):
            link(eng.tensor_tensor(tmp[:, 0], x, spread(cos, heads), ALU.mult))
            link(eng.tensor_tensor(tmp[:, 1].rearrange("p h (two c) -> p h two c", two=2), swapped(x, heads, HD),
                                   spread(sin, heads).rearrange("p h (two c) -> p h two c", two=2), ALU.mult))

        @block.vector
        def _(dve):
            link = chained(dve, dve_chain)
            for t in range(TB):
                dve.wait_ge(squared, t + 1)
                nc.vector.tensor_reduce(sums[:, t, :], squares[:, 0:NH * HD].rearrange("p (h c) -> p h c", h=NH), AX.X,
                                        ALU.add).then_inc(summed, 1)
            dve.wait_ge(summed, TB)
            nc.vector.tensor_scalar(sums, sums, 1.0 / HD, EPS, ALU.mult, ALU.add).then_inc(mean_ready, 1)
            dve.wait_ge(cmp_turned, 1)
            dve.wait_ge(small_loaded, 16)
            half = CMP_STRIDE
            for kv in range(2):
                for part in range(2):
                    src = m.bank[:, 4 + kv, part * half:part * half + N_CMP * half].rearrange("p (n l) -> p n l", l=half)
                    pos = place[:, kv, part * half:(part + 1) * half]
                    nc.vector.tensor_tensor(windows[:, kv, :, part * half:(part + 1) * half], src, spread(pos, N_CMP),
                                            ALU.add).then_inc(windows_ready, 1)
            dve.wait_ge(rooted, 1)
            link(nc.vector.reciprocal(sums, sums))
            nc.vector.tensor_scalar(sums[:, :, 0:HEADS], sums[:, :, 0:HEADS], HD ** -0.5, None, ALU.mult)\
                .then_inc(scales_ready, 1)
            dve.wait_ge(scales_ready, 1)
            q = q_tok.rearrange("p (h c) -> p h c", h=HEADS)
            for t in range(TB):
                if t >= 1:
                    dve.wait_ge(turned, 2 * t - 1)
                src = tok(m, "nq")[:, t, :].rearrange("p (h c) -> p h c", h=HEADS)
                link(nc.vector.tensor_tensor(q, src, per_head(sums[:, t, 0:HEADS], HD), ALU.mult))
                link(nc.vector.tensor_tensor(q, q, spread(gains[:, 0:HD], HEADS), ALU.mult))
                rotate(nc.vector, link, q, m.nsa_cos[:, t, :], m.nsa_sin[:, t, :], turn_q, HEADS)
                nc.vector.tensor_tensor(q, turn_q[:, 0], turn_q[:, 1], ALU.add).then_inc(q_ready, 1)
                dve.wait_ge(q_ready, t + 1)
            dve.wait_ge(cmp_done, 1)
            link(nc.vector.tensor_copy(kc_tok, m.bank[0:N_CMP, 4, 0:2 * HD].rearrange("p (g c) -> p g c", g=GROUPS)))
            link(nc.vector.tensor_tensor(kc_turn[:, 0], kc_tok, kc_tok, ALU.mult))
            link(nc.vector.tensor_reduce(kc_sums, kc_turn[:, 0], AX.X, ALU.add))
            nc.vector.tensor_scalar(kc_sums, kc_sums, 1.0 / HD, EPS, ALU.mult, ALU.add).then_inc(kc_squared, 1)
            dve.wait_ge(kc_rooted, 1)
            link(nc.vector.reciprocal(kc_sums, kc_sums))
            link(nc.vector.tensor_tensor(kc_tok, kc_tok, per_head(kc_sums, HD), ALU.mult))
            link(nc.vector.tensor_tensor(kc_tok, kc_tok, spread(gains[0:N_CMP, HD:2 * HD], GROUPS), ALU.mult))
            rotate(nc.vector, link, kc_tok, m.end_cos[0:N_CMP, :], m.end_sin[0:N_CMP, :], kc_turn, GROUPS)
            twice = kc_twice.rearrange("p (h two c) -> p h two c", two=2, c=HD)
            for i in range(2):
                last = nc.vector.tensor_tensor(twice[:, :, i, :], kc_turn[:, 0], kc_turn[:, 1], ALU.add)
            last.then_inc(kc_ready, 1)

        @block.gpsimd
        def _(pool):
            link = chained(pool, pool_chain)
            pool.wait_ge(scales_ready, 1)
            pool.wait_ge(small_loaded, 16)
            k = k_tok.rearrange("p (h c) -> p h c", h=KH)
            twice = k_twice.rearrange("p (h two c) -> p h two c", two=2, c=HD)
            for t in range(TB):
                for i, name in enumerate(("sk", "wk")):
                    src = tok(m, name)[:, t, :].rearrange("p (h c) -> p h c", h=GROUPS)
                    g0 = HEADS + i * GROUPS
                    link(nc.gpsimd.tensor_tensor(k[:, i * GROUPS:(i + 1) * GROUPS, :], src,
                                                 per_head(sums[:, t, g0:g0 + GROUPS], HD), ALU.mult))
                link(nc.gpsimd.tensor_tensor(k, k, spread(gains[:, HD:2 * HD], KH), ALU.mult))
                rotate(nc.gpsimd, link, k, m.nsa_cos[:, t, :], m.nsa_sin[:, t, :], turn_k, KH)
                if t >= 1:
                    pool.wait_ge(turned, 2 * t)
                for i in range(2):
                    last = nc.gpsimd.tensor_tensor(twice[:, :, i, :], turn_k[:, 0], turn_k[:, 1], ALU.add)
                last.then_inc(k_ready, 1)
                pool.wait_ge(k_ready, t + 1)


def pair_half(h):
    return slice((h % 2) * HD, (h % 2 + 1) * HD)


def compressed_attention(core, m):
    nc = core.nc
    HH = HEADS // 2
    WIDE = TB * HH * N_CMP
    scores = m.z[:, 0:2 * WIDE].rearrange("p (e x) -> p e x", e=2)
    groups = m.z[:, 0:2 * WIDE].rearrange("p (g n) -> p g n", n=N_CMP)
    turned_p = m.z[0:N_CMP, 1024:1024 + TB * HEADS * P].rearrange("p (i t) -> p i t", t=P)
    top = m.small[:, 0:2 * TB * HH]
    total = m.small[:, 32:32 + 2 * TB * HH]
    factor = m.small[:, 64:64 + TB * HEADS].rearrange("p (t h) -> p t h", t=TB)
    score_done, less_max, exp_done, weighed = (core.sem(f"cmp_{n}") for n in ("score_done", "less_max", "exp_done", "weighed"))
    turned, copied, pv_done, chain = (core.sem(f"cmp_{n}") for n in ("turned", "copied", "pv_done", "chain"))

    with nc.Block() as block:
        @block.sync
        def _(sp):
            core.zero_past(sp)

        @block.tensor
        def _(pe):
            for b in range(TB):
                for h in range(HEADS):
                    at_ = (b * HH + h // 2) * N_CMP
                    last = nc.tensor.matmul(m.bank[:, h % 2, at_:at_ + N_CMP], m.nsa_q[pair_half(h), h // 2, b * P:(b + 1) * P],
                                            m.k_cmp[pair_half(h), h // HH, :], start=True, stop=True)
            last.then_inc(score_done, 1)
            pe.wait_ge(weighed, 2)
            for b in range(TB):
                for e in range(2):
                    if b >= 2:
                        pe.wait_ge(copied, 2 * (b - 2) + e + 1)
                    for j in range(HH):
                        at_ = (b * HH + j) * N_CMP
                        last = nc.tensor.transpose(m.bank[0:N_CMP, 2 * (b % 2) + e, j * P:(j + 1) * P],
                                                   scores[:, e, at_:at_ + N_CMP], m.ident[:])
                    last.then_inc(turned, 1)
            for b in range(TB):
                pe.wait_ge(copied, 2 * b + 2)
                for h in range(HEADS):
                    i = (b * 2 + h % 2) * HH + h // 2
                    last = nc.tensor.matmul(m.bank[:, 4 + b, h * HD:(h + 1) * HD], turned_p[:, i, :],
                                            m.v_cmp[:, h // HH, :], start=True, stop=True)
                last.then_inc(pv_done, 1)

        @block.scalar
        def _(act):
            act.wait_ge(less_max, 1)
            nc.scalar.activation(m.z[:, 0:2 * WIDE], m.z[:, 0:2 * WIDE], ACT.Exp).then_inc(exp_done, 1)
            for b in range(TB):
                for e in range(2):
                    act.wait_ge(turned, 2 * b + e + 1)
                    i = (b * 2 + e) * HH
                    nc.scalar.copy(turned_p[:, i:i + HH, :], m.bank[0:N_CMP, 2 * (b % 2) + e, :]
                                   .rearrange("p (h t) -> p h t", h=HH)).then_inc(copied, 1)

        @block.vector
        def _(dve):
            link = chained(dve, chain)

            def windows_of(table):
                return table.rearrange("p t (one n) -> p t one n", one=1).broadcast_to([P, TB, HH, N_CMP])

            def by_head(x):
                return x.rearrange("p (t h n) -> p t h n", t=TB, h=HH)

            dve.wait_ge(score_done, 1)
            for e in range(2):
                link(nc.vector.tensor_tensor(by_head(scores[:, e]), by_head(m.bank[:, e, 0:WIDE]), windows_of(m.cmp_fill),
                                             ALU.add))
            link(nc.vector.tensor_reduce(top, groups, AX.X, ALU.max))
            nc.vector.tensor_tensor(groups, groups, per_head(top, N_CMP), ALU.subtract).then_inc(less_max, 1)
            dve.wait_ge(exp_done, 1)
            for e in range(2):
                nc.vector.tensor_tensor(by_head(scores[:, e]), by_head(scores[:, e]), windows_of(m.cmp_seen), ALU.mult)\
                    .then_inc(weighed, 1)
            dve.wait_ge(weighed, 2)
            link(nc.vector.tensor_reduce(total, groups, AX.X, ALU.add))
            link(nc.vector.tensor_scalar(total, total, 1e-30, None, ALU.max))
            link(nc.vector.reciprocal(total, total))
            gate = tok(m, "gate")[:, :, 0:HEADS]
            for e in range(2):
                link(nc.vector.tensor_tensor(factor[:, :, e::2], total[:, e * TB * HH:(e + 1) * TB * HH]
                                             .rearrange("p (t h) -> p t h", t=TB), gate[:, :, e::2], ALU.mult))
            for b in range(TB):
                dve.wait_ge(pv_done, b + 1)
                nc.vector.tensor_tensor(m.otok[:, b, :].rearrange("p (h c) -> p h c", h=HEADS),
                                        m.bank[:, 4 + b, :].rearrange("p (h c) -> p h c", h=HEADS),
                                        per_head(factor[:, b, :], HD), ALU.mult)


def merge(core, m, gate_dram, out_dram):
    nc = core.nc
    SLOTS, OUT_SLOTS = 2, 3
    OC = HW // P
    GATE_W, SLOT_W = BRANCHES * D, BRANCHES * (D + OC * P)
    gate_w = [m.w[:, i * SLOT_W:i * SLOT_W + GATE_W].rearrange("p (b k c) -> p b k c", b=BRANCHES, k=DK) for i in range(SLOTS)]
    proj_w = [m.w[:, i * SLOT_W + GATE_W:(i + 1) * SLOT_W].rearrange("p (b k c) -> p b k c", b=BRANCHES, k=OC) for i in range(SLOTS)]
    out_w = m.w[:, SLOTS * SLOT_W:SLOTS * SLOT_W + OUT_SLOTS * D].rearrange("p (s c) -> p s c", s=OUT_SLOTS)
    y = m.sbqk
    opened = m.z[:, 0:BRANCHES * SEQ].rearrange("p (b t) -> p b t", b=BRANCHES)
    part = m.z[:, BRANCHES * SEQ:2 * BRANCHES * SEQ].rearrange("p (b t) -> p b t", b=BRANCHES)
    loaded = [core.sem(f"merge_loaded{i}") for i in range(SLOTS)]
    out_loaded = [core.sem(f"out_loaded{i}") for i in range(OUT_SLOTS)]
    out_used, out_done = core.sem("out_used"), core.sem("out_done")
    gate_done, proj_done, opened_ready, part_ready = (
        [core.sem(f"{n}{b}") for b in range(BRANCHES)] for n in ("gate_done", "proj_done", "opened", "part_ready"))
    y_ready, chain = core.sem("y_ready"), core.sem("merge_chain")
    rounds = DK // SLOTS

    with nc.Block() as block:
        @block.sync
        def _(sp):
            gate_in = gate_dram.rearrange("a j p c -> (a j) p c")
            out_in = out_dram.rearrange("a k p c -> (a k) p c")

            def load(r, i):
                sp.dma_start(m.w[:, i * SLOT_W:(i + 1) * SLOT_W], one(gate_in, r * SLOTS + i)).then_inc(loaded[i], 16)

            for i in range(SLOTS):
                load(0, i)
            for k in range(OUT_SLOTS):
                sp.dma_start(out_w[:, k, :], out_in[k]).then_inc(out_loaded[k], 16)
            with sp.Fori(1, rounds) as r:
                for i in range(SLOTS):
                    sp.wait_ge(proj_done[BRANCHES - 1], r * SLOTS + i - SLOTS + 1)
                    load(r, i)
            for k in range(OUT_SLOTS, DK):
                sp.wait_ge(out_used, k - OUT_SLOTS + 1)
                sp.dma_start(out_w[:, k % OUT_SLOTS, :], out_in[k]).then_inc(out_loaded[k % OUT_SLOTS], 16)
            core.zero_past(sp)

        @block.tensor
        def _(pe):
            def chunk(r, i, first):
                pe.wait_ge(loaded[i], r * 16 + 16)
                for b in range(BRANCHES):
                    if not (first and i == 0):
                        pe.wait_ge(part_ready[b], r * SLOTS + i)
                    for k in range(DK):
                        last = nc.tensor.matmul(m.bank[:, 2 * b, :], gate_w[i][:, b, k, :], m.h[:, k, :], start=k == 0,
                                                stop=k == DK - 1)
                    last.then_inc(gate_done[b], 1)
                    for k in range(OC):
                        last = nc.tensor.matmul(m.bank[:, 2 * b + 1, :], proj_w[i][:, b, k, :], m.o[:, b * OC + k, :],
                                                start=k == 0, stop=k == OC - 1)
                    last.then_inc(proj_done[b], 1)

            for i in range(SLOTS):
                chunk(0, i, True)
            with pe.Fori(1, rounds) as r:
                for i in range(SLOTS):
                    chunk(r, i, False)
            pe.wait_ge(y_ready, DK)
            for k in range(DK):
                pe.wait_ge(out_loaded[k % OUT_SLOTS], 16 * (k // OUT_SLOTS) + 16)
                for c in range(DK):
                    last = nc.tensor.matmul(m.bank[:, c, :], out_w[:, k % OUT_SLOTS, c * P:(c + 1) * P], y[:, k, :],
                                            start=k == 0, stop=k == DK - 1)
                    if k == DK - 1:
                        last.then_inc(out_done, 1)
                if k < DK - 1:
                    last.then_inc(out_used, 1)

        @block.scalar
        def _(act):
            def open_gates(n, first):
                for b in range(BRANCHES):
                    act.wait_ge(gate_done[b], n + 1)
                    if not first:
                        act.wait_ge(part_ready[b], n)
                    nc.scalar.activation(opened[:, b, :], m.bank[:, 2 * b, :], ACT.Sigmoid).then_inc(opened_ready[b], 1)

            open_gates(0, True)
            with act.Fori(1, DK) as n:
                open_gates(n, False)

        @block.vector
        def _(dve):
            with dve.Fori(0, DK) as n:
                for b in range(BRANCHES):
                    dve.wait_ge(opened_ready[b], n + 1)
                    dve.wait_ge(proj_done[b], n + 1)
                    nc.vector.tensor_tensor(part[:, b, :], opened[:, b, :], m.bank[:, 2 * b + 1, :], ALU.mult)\
                        .then_inc(part_ready[b], 1)
                dve.wait_ge(part_ready[1], n + 1)
                nc.vector.tensor_tensor(part[:, 0, :], part[:, 0, :], part[:, 1, :], ALU.add).then_inc(chain, 1)
                dve.wait_ge(part_ready[2], n + 1)
                dve.wait_ge(chain, n + 1)
                nc.vector.tensor_tensor(column(y, n), part[:, 0, :], part[:, 2, :], ALU.add).then_inc(y_ready, 1)
                dve.wait_ge(y_ready, n + 1)
            for c in range(DK):
                dve.wait_ge(out_done, c + 1)
                nc.vector.tensor_tensor(m.x[:, c, :], m.bank[:, c, :], m.x[:, c, :], ALU.add)


LAYERS = 2


def first_block(core, m, a):
    nc = core.nc
    m.tok = m.arena[:, 0:TB * TOK_W].rearrange("p (t c) -> p t c", t=TB)
    m.o = m.arena[:, 8928:8928 + 12 * SEQ].rearrange("p (c t) -> p c t", c=12)
    m.sbqk = m.arena[:, 15072:15072 + 8 * SEQ].rearrange("p (c t) -> p c t", c=8)
    m.z = m.arena[:, 19168:19168 + 7168]
    m.late = m.arena[:, 8928:8928 + 12 * SEQ]
    m.otok = m.scratch.rearrange("p (t c) -> p t c", t=TB)
    m.probs = m.z[:, 4096:5632].rearrange("p (n k) -> p n k", n=3)
    m.turned_p = m.z[:, 5632:7168].rearrange("p (n k) -> p n k", n=3)
    m.part = m.z[:, 0:SEQ]
    m.sums = m.small[:, 128:160].rearrange("p (t h) -> p t h", t=TB)
    m.neg_max = m.small[:, 160:163]
    m.mla_q = m.w[0:QK_MLA, 0:4096].rearrange("p (h t) -> p h t", h=HEADS)
    m.mla_k = m.w[0:QK_MLA, 4096:8192].rearrange("p (h t) -> p h t", h=HEADS)
    m.mla_kv = m.z[:, 0:4096].rearrange("p (t c) -> p t c", t=TB)
    m.nsa_q = m.w[:, 8192:10240].rearrange("p (c t) -> p c t", c=4)
    m.nsa_k = m.w[:, 10240:12288].rearrange("p (c t) -> p c t", c=4)
    m.odds = m.w[:, 0:1536].rearrange("p (n k) -> p n k", n=3)
    m.rest = m.w[:, 1536:3072].rearrange("p (n k) -> p n k", n=3)
    m.left = m.w[:, 3072:3072 + 3 * (SEQ + 1)].rearrange("p (n k) -> p n k", n=3)
    m.ones_row = m.w[:, 4611:4611 + SEQ]

    def keys_of(name):
        base = {"sk": 0, "wk": 2}[name]
        return lambda h, keys: m.nsa_k[pair_half(h), base + h // 4, 0:keys]

    def values_of(name):
        return lambda h, kb: tok(m, name)[:, kb, h // 4 * HD:(h // 4 + 1) * HD]

    def queries(h, b):
        return m.nsa_q[pair_half(h), h // 2, b * P:(b + 1) * P]

    core.zero_all()
    with nc.Fori(0, LAYERS) as l:
        ffn(core, m, "ffn1", at(a["ffn1_norm"], l), at(a["ffn1_wi"], l), at(a["ffn1_wo"], l))
        core.next_stage()
        in_projection(core, m, at(a["mix_norm"], l), at(a["w_in_qk"], l), at(a["w_in_tok"], l))
        core.next_stage()
        mla_prepare(core, m, at(a["mla_w_uq"], l), at(a["mla_w_ukv"], l), at(a["mla_norms"], l), at(a["mla_gains"], l))
        core.next_stage()
        attention(core, m, "mla", lambda h, b: m.mla_q[:, h, b * P:(b + 1) * P], lambda h, keys: m.mla_k[:, h, 0:keys],
                  lambda h, kb: m.mla_kv[:, kb, h * 2 * HD + HD:(h + 1) * 2 * HD], m.causal_bf, out=m.o[:, 4:8])
        core.next_stage()
        nsa_prepare(core, m, at(a["cmp_w1"], l), at(a["nsa_small"], l), None)
        core.next_stage()
        compressed_attention(core, m)
        core.next_stage()
        attention(core, m, "slc", queries, keys_of("sk"), values_of("sv"), m.causal_bf, add=True,
                  gate=lambda b: tok(m, "gate")[:, b, HEADS:2 * HEADS])
        core.next_stage()
        attention(core, m, "win", queries, keys_of("wk"), values_of("wv"), m.causal_bf, add=True,
                  gate=lambda b: tok(m, "gate")[:, b, 2 * HEADS:3 * HEADS], out=m.o[:, 8:12])
        core.next_stage()
        attention(core, m, "stick", lambda h, b: m.sbqk[pair_half(h), h // 2, b * P:(b + 1) * P],
                  lambda h, keys: m.sbqk[pair_half(h), 4 + h // 2, 0:keys],
                  lambda h, kb: tok(m, "sb_v")[:, kb, h * HD:(h + 1) * HD], m.strict_bf, stick=True, out=m.o[:, 0:4])
        core.next_stage()
        merge(core, m, at(a["merge_w"], l), at(a["w_out"], l))
        core.next_stage()
        ffn(core, m, "ffn2", at(a["ffn2_norm"], l), at(a["ffn2_wi"], l), at(a["ffn2_wo"], l))
        core.zero_all()


def allocate(core, m):
    nc = core.nc
    m.x = core.sbuf("x_t", [P, DK, SEQ])
    m.h = core.sbuf("h_t", [P, DK, SEQ])
    m.w = core.sbuf("weights", [P, 12288])
    m.arena = core.sbuf("arena", [P, 26336])
    m.scratch = core.sbuf("scratch", [P, 2048])
    m.square = m.scratch[:, 0:2 * SEQ].rearrange("p (n t) -> p n t", n=2)
    m.root = m.scratch[:, 2 * SEQ:3 * SEQ]
    m.mean = m.scratch[:, 3 * SEQ:4 * SEQ]
    m.gain = core.sbuf("gain", [P, DK])
    m.ones = core.sbuf("ones", [P, P])
    m.small = core.sbuf("small", [P, 256])
    m.nsa_small = core.sbuf("nsa_small_sb", [P, 320])
    cmp_ = core.sbuf("cmp_kv", [P, 2 * N_CMP + KV_W])
    m.k_cmp = cmp_[:, 0:2 * N_CMP].rearrange("p (g n) -> p g n", g=GROUPS)
    m.v_cmp = cmp_[0:N_CMP, 2 * N_CMP:].rearrange("p (g c) -> p g c", g=GROUPS)
    m.ident_bf, m.causal_bf, m.strict_bf = (core.sbuf(n, [P, P], BF16) for n in ("ident_bf", "causal_bf", "strict_bf"))
    places, width = const_places()
    m.const = core.sbuf("const_sb", [P, width])
    c = {name: m.const[:, i:j] for name, (i, j) in places.items()}
    m.ident, m.causal, m.strict = c["ident"], c["causal"], c["strict"]
    m.mla_cos, m.mla_sin, m.nsa_cos, m.nsa_sin, m.cmp_fill, m.cmp_seen = (
        c[n].rearrange("p (t c) -> p t c", t=TB) for n in ("mla_cos", "mla_sin", "nsa_cos", "nsa_sin", "cmp_fill", "cmp_seen"))
    m.end_cos, m.end_sin = c["end_cos"], c["end_sin"]
    m.ident_neg = core.sbuf("ident_neg", [P, P], BF16)
    m.tail = core.sbuf("tail", [P, 680])
    m.bank = core.ctx.enter_context(nc.psum_tensor("bank", [P, 8, SEQ], F32))


def load_start(core, m, a):
    nc = core.nc
    loaded = core.sem("start_loaded")
    with nc.Block() as block:
        @block.sync
        def _(sp):
            sp.dma_start(m.x[:], a["x"]).then_inc(loaded, 16)
            sp.dma_start(m.const[:], a["const"]).then_inc(loaded, 16)
            sp.wait_ge(loaded, 32)

        @block.vector
        def _(dve):
            nc.vector.memset(m.ones[:], 1.0)
            dve.wait_ge(loaded, 32)
            nc.vector.tensor_copy(m.ident_bf[:], m.ident)
            nc.vector.tensor_scalar(m.ident_neg[:], m.ident, -1.0, None, ALU.mult)
            nc.vector.tensor_copy(m.causal_bf[:], m.causal)
            nc.vector.tensor_copy(m.strict_bf[:], m.strict)


def lay_out_first(i):
    f = lambda n: np.asarray(i[n])
    L = LAYERS

    def gain(n):
        return f(n).reshape(L, DK, P).transpose(0, 2, 1)

    def chunks(w, c):
        return w.reshape(L, DK, P, -1, c).transpose(0, 3, 2, 1, 4).reshape(L, -1, P, DK * c)

    def up(w):
        return w.reshape(L, DK, P, 2, D_FF // P, P).transpose(0, 4, 2, 3, 1, 5).reshape(L, D_FF // P, P, 2 * D)

    def rows(v):
        return np.broadcast_to(v[:, None, :], (L, P, v.shape[-1]))

    w_in = f("w_in")
    n_tok = 2 * HW + TOK_W
    gates = w_in[:, :, n_tok:].reshape(L, DK, P, BRANCHES, DK, P).transpose(0, 4, 2, 3, 1, 5).reshape(L, DK, P, -1)
    proj = np.stack([f(n) for n in ("proj_sb", "proj_mla", "proj_nsa")], 1)
    proj = proj.reshape(L, BRANCHES, HW // P, P, DK, P).transpose(0, 4, 3, 1, 2, 5).reshape(L, DK, P, -1)
    w1 = np.stack([f("cmp_wk1"), f("cmp_wv1")], 1).reshape(L, 2, CMP_LEN, HD, CMP_HIDDEN).transpose(0, 3, 1, 2, 4)
    w1 = w1.reshape(L, HD, -1)
    place = np.stack([f("cmp_pos_k"), f("cmp_pos_v")], 1).transpose(0, 3, 1, 2).reshape(L, HD, -1)
    w2 = np.stack([f("cmp_wk2"), f("cmp_wv2")], 1).transpose(0, 2, 1, 3).reshape(L, CMP_HIDDEN, -1)
    out = {
        "x": f("x")[0].T.reshape(DK, P, SEQ).transpose(1, 0, 2),
        "const": const_array(),
        "mix_norm": gain("mix_norm"),
        "w_in_qk": chunks(w_in[:, :, 0:2 * HW], P),
        "w_in_tok": chunks(w_in[:, :, 2 * HW:n_tok], TOK_C),
        "mla_w_uq": f("mla_w_uq").reshape(L, 2, P, -1).transpose(0, 2, 1, 3).reshape(L, P, -1),
        "mla_w_ukv": f("mla_w_ukv"),
        "mla_norms": np.concatenate([f("mla_q_norm").reshape(L, 2, P).transpose(0, 2, 1), f("mla_kv_norm")[:, :, None]], 2),
        "mla_gains": rows(np.concatenate([f("mla_qk_gain_q"), f("mla_qk_gain_k")], 1)),
        "cmp_w1": np.concatenate([w1, w1], 1),
        "nsa_small": np.concatenate([rows(np.concatenate([f("nsa_q_gain"), f("nsa_k_gain")], 1)),
                                     np.concatenate([place, place], 1), w2], 2),
        "merge_w": np.concatenate([gates, proj], 3),
        "w_out": f("w_out").reshape(L, DK, P, D),
    }
    for n in ("ffn1", "ffn2"):
        out[f"{n}_norm"] = gain(f"{n}_norm")
        out[f"{n}_wi"] = up(f(f"{n}_wi"))
        out[f"{n}_wo"] = f(f"{n}_wo").reshape(L, D_FF // P, P, D)
    return {n: np.ascontiguousarray(v) for n, v in out.items()}


GH = 4
CONV_K = 5
N_FM = 28
FM_AT = dict(gq=0, gk=4, gv=8, gz=12, mo=16, mq=20, mk=24)
KINDS = dict(a=0, b=1, i=2, f=3)
GATE_ROWS = 36
BACK = 32
DIRS = 2
GATE_C = len(KINDS) * GATE_ROWS


def gate_row(d, h):
    return d * BACK + h


def second_projection(core, m, a):
    nc = core.nc
    SLOTS = 2
    fm_w = m.w[:, 0:SLOTS * D].rearrange("p (s k c) -> p s k c", s=SLOTS, k=DK)
    v_w = m.w[:, 2048:2048 + DK * SEQ].rearrange("p (k c) -> p k c", k=DK)
    gate_w = m.w[:, 6144:6144 + DK * GATE_C].rearrange("p (k c) -> p k c", k=DK)
    s = norm_steps(core, "second")
    loaded = [core.sem(f"fm_loaded{i}") for i in range(SLOTS)]
    done = [core.sem(f"fm_done{i}") for i in range(SLOTS)]
    copied = [core.sem(f"fm_copied{i}") for i in range(SLOTS)]
    tok_loaded, v_done, gates_done, ones_set = (core.sem(n) for n in ("tok_loaded", "v_done", "gates_done", "ones_set"))
    rounds = N_FM // SLOTS

    with nc.Block() as block:
        @block.sync
        def _(sp):
            sp.dma_start(m.gain[:], a["norm1_2"]).then_inc(s["gain_loaded"], 16)

            def load(r, i):
                sp.dma_start(m.w[:, i * D:(i + 1) * D], one(a["w_in_fm_2"], r * SLOTS + i)).then_inc(loaded[i], 16)

            for i in range(SLOTS):
                load(0, i)
            sp.dma_start(m.w[:, 2048:2048 + DK * SEQ], a["w_in_v_2"]).then_inc(tok_loaded, 16)
            sp.dma_start(m.w[:, 6144:6144 + DK * GATE_C], a["w_in_gates_2"]).then_inc(tok_loaded, 16)
            sp.dma_start(m.const[:, P:P + m.const_2_width], a["const_2"]).then_inc(tok_loaded, 16)
            sp.dma_start(m.gdn_small, a["gdn_small_2"]).then_inc(tok_loaded, 16)
            with sp.Fori(1, rounds) as r:
                for i in range(SLOTS):
                    sp.wait_ge(done[i], r)
                    load(r, i)
            core.zero_past(sp)

        @block.tensor
        def _(pe):
            norm_tensor(nc, pe, m, s)
            pe.wait_ge(s["normed"], DK)

            def chunk(r, i, first):
                pe.wait_ge(loaded[i], r * 16 + 16)
                if not first:
                    pe.wait_ge(copied[i], r)
                for k in range(DK):
                    last = nc.tensor.matmul(m.bank[:, i, :], fm_w[:, i, k, :], m.h[:, k, :], start=k == 0, stop=k == DK - 1)
                last.then_inc(done[i], 1)

            for i in range(SLOTS):
                chunk(0, i, True)
            with pe.Fori(1, rounds) as r:
                for i in range(SLOTS):
                    chunk(r, i, False)
            pe.wait_ge(tok_loaded, 64)
            for t in range(TB):
                for k in range(DK):
                    last = nc.tensor.matmul(m.bank[:, 2 + t, :], m.h[:, k, t * P:(t + 1) * P], v_w[:, k, :], start=k == 0,
                                            stop=k == DK - 1)
                last.then_inc(v_done, 1)
            for t in range(TB):
                for k in range(DK):
                    last = nc.tensor.matmul(m.bank[:, 6 + t // 2, t % 2 * GATE_C:(t % 2 + 1) * GATE_C],
                                            m.h[:, k, t * P:(t + 1) * P], gate_w[:, k, :], start=k == 0, stop=k == DK - 1)
            last.then_inc(gates_done, 1)

        @block.scalar
        def _(act):
            norm_scalar(nc, act, m, s)
            with act.Fori(0, rounds) as r:
                for i in range(SLOTS):
                    act.wait_ge(done[i], r + 1)
                    nc.scalar.copy(column(m.fm, r * SLOTS + i), m.bank[:, i, :]).then_inc(copied[i], 1)

        @block.vector
        def _(dve):
            norm_vector(nc, dve, m, s, m.gain)
            dve.wait_ge(tok_loaded, 64)
            nc.vector.tensor_copy(m.strict_bf[:], m.anti)
            nc.vector.memset(m.mv[:, :, :, P:P + 1], 1.0)
            for t in range(TB):
                dve.wait_ge(v_done, t + 1)
                nc.vector.tensor_copy(m.mv[:, t, :, 0:P], m.bank[:, 2 + t, :].rearrange("p (h c) -> p h c", h=GH))
            dve.wait_ge(gates_done, 1)
            for i in range(2):
                nc.vector.tensor_copy(m.gates[:, 2 * i:2 * i + 2, :],
                                      m.bank[:, 6 + i, 0:2 * GATE_C].rearrange("p (t c) -> p t c", t=2))


def gate_rows(core, m):
    nc = core.nc
    row = [m.rows[:, i * SEQ:(i + 1) * SEQ] for i in range(6)]
    xa, G, xf, B, shift, neg_m = row
    soft = [m.scratch[0:GATE_ROWS, i * SEQ:(i + 1) * SEQ] for i in range(2)]
    ones = m.scratch[0:GATE_ROWS, 2 * SEQ:3 * SEQ]
    less = m.scratch[0:GATE_ROWS, 3 * SEQ:4 * SEQ]
    dt_bias, a_log, i_bias, f_bias = (m.gdn_small[0:GATE_ROWS, i:i + 1] for i in range(4))
    turned, biased, rate, soft_done = (core.sem(f"rows_{n}") for n in ("turned", "biased", "rate", "soft_done"))
    act_chain, chain, ready, back, selected = (core.sem(f"rows_{n}") for n in ("act_chain", "chain", "ready", "back", "selected"))
    ways = ((slice(0, GH), 1), (slice(BACK, BACK + GH), -1))

    with nc.Block() as block:
        @block.sync
        def _(sp):
            core.zero_past(sp)

        @block.tensor
        def _(pe):
            for bank, kind in enumerate(("a", "i", "f")):
                for t in range(TB):
                    last = nc.tensor.transpose(m.bank[0:GATE_ROWS, bank, t * P:(t + 1) * P],
                                               m.gates[:, t, KINDS[kind] * GATE_ROWS:(KINDS[kind] + 1) * GATE_ROWS], m.ident)
                last.then_inc(turned, 1)
            pe.wait_ge(ready, 3)
            for kind, src in enumerate((G, shift, xf)):
                for t in range(TB):
                    last = nc.tensor.transpose(m.bank[:, 3 + kind, t * GATE_ROWS:(t + 1) * GATE_ROWS],
                                               src[:, t * P:(t + 1) * P], m.ident[0:GATE_ROWS, 0:GATE_ROWS])
            last.then_inc(back, 1)

        @block.scalar
        def _(act):
            link = chained(act, act_chain)
            for i, x in enumerate((xa, xf)):
                act.wait_ge(biased, i + 1)
                link(nc.scalar.activation(soft[i], x, ACT.Abs))
                link(nc.scalar.activation(soft[i], soft[i], ACT.Exp, scale=-1.0))
                nc.scalar.activation(soft[i], soft[i], ACT.Ln, bias=1.0).then_inc(soft_done, 1)
            nc.scalar.activation(m.rate[0:GATE_ROWS, :], a_log, ACT.Exp).then_inc(rate, 1)
            nc.scalar.activation(m.beta, m.gates[:, :, GATE_ROWS:2 * GATE_ROWS], ACT.Sigmoid)

        @block.vector
        def _(dve):
            link = chained(dve, chain)
            link(nc.vector.memset(ones, 1.0))
            for i, (x, bank, bias) in enumerate(((xa, 0, dt_bias), (xf, 2, f_bias))):
                dve.wait_ge(turned, bank + 1)
                nc.vector.tensor_scalar(x, m.bank[0:GATE_ROWS, bank, :], bias, None, ALU.add).then_inc(biased, 1)
            link(nc.vector.tensor_scalar(shift, m.bank[0:GATE_ROWS, 1, :], i_bias, None, ALU.add))
            dve.wait_ge(soft_done, 1)
            dve.wait_ge(rate, 1)
            dve.wait_ge(biased, 2)
            link(nc.vector.scalar_tensor_tensor(soft[0], xa, 0.0, soft[0], ALU.max, ALU.add))
            link(nc.vector.tensor_scalar(xa, soft[0], m.rate[0:GATE_ROWS, :], -1.0, ALU.mult, ALU.mult))
            link(nc.vector.memset(G, 0.0))
            for rows, way in ways:
                for t in range(TB):
                    part = slice(t * P, (t + 1) * P)
                    last = nc.vector.tensor_tensor_scan(G[rows, part][:, ::way], ones[rows, part], xa[rows, part][:, ::way],
                                                        0.0, ALU.mult, ALU.add)
            last.then_inc(ready, 1)
            dve.wait_ge(soft_done, 2)
            link(nc.vector.scalar_tensor_tensor(xf, xf, 0.0, soft[1], ALU.min, ALU.subtract))
            link(nc.vector.memset(B, 0.0))
            for rows, way in ways:
                link(nc.vector.tensor_tensor_scan(B[rows, ::way], ones[rows, :], xf[rows, ::way], 0.0, ALU.mult, ALU.add))
            link(nc.vector.tensor_tensor(less, B, shift, ALU.subtract))
            nc.vector.tensor_tensor(shift, shift, B, ALU.subtract).then_inc(ready, 1)
            link(nc.vector.memset(neg_m, 0.0))
            for rows, way in ways:
                link(nc.vector.tensor_tensor_scan(neg_m[rows, ::way], less[rows, ::way], less[rows, ::way], 0.0, ALU.min, ALU.min))
            nc.vector.tensor_tensor(xf, B, neg_m, ALU.subtract).then_inc(ready, 1)
            dve.wait_ge(back, 1)
            for kind, to in enumerate((m.g_tok, m.shift_tok, m.bm_tok)):
                nc.vector.tensor_copy(to, m.bank[:, 3 + kind, 0:TB * GATE_ROWS].rearrange("p (t r) -> p t r", t=TB))
            sel = m.select.rearrange("p (r c) -> p r c", c=P)
            for d in range(DIRS):
                rows = m.ident[0:GATE_ROWS, d * BACK:d * BACK + GH]
                nc.vector.tensor_copy(sel[:, d * GH:(d + 1) * GH, :],
                                      rows.rearrange("p (r one) -> p r one", one=1).broadcast_to([GATE_ROWS, GH, P]))


def mlstm(core, m):
    nc = core.nc
    select = m.select.rearrange("p (r c) -> p r c", c=P)
    decay = m.w[:, 0:2 * SEQ].rearrange("p (n t) -> p n t", n=2)
    weights = m.w[:, 1024:1024 + 2 * TB * SEQ].rearrange("p (n s t) -> p n s t", n=2, s=TB)
    least = m.w[:, 5120:5120 + TB * GATE_ROWS].rearrange("p (t r) -> p t r", t=TB)
    den = m.w[:, 5376:5376 + 2 * DIRS * GH * TB].rearrange("p (n t) -> p n t", t=TB)
    part = m.w[:, 5632:5632 + 2 * P].rearrange("p (t c) -> p t c", t=2)
    spread_done, score_done, decay_done, weighed, read_m = (
        core.sem(f"ml_{n}") for n in ("spread_done", "score_done", "decay_done", "weighed", "read_m"))
    pv_done, out_read, least_done, chain = (core.sem(f"ml_{n}") for n in ("pv_done", "out_read", "least_done", "chain"))
    units = [(h, d) for h in range(GH) for d in range(DIRS)]
    MBANK, SBANK, OBANK = 0, 2, 4

    def queries(d, sb):
        return slice(sb * P, SEQ) if d == 0 else slice(0, (sb + 1) * P)

    with nc.Block() as block:
        @block.sync
        def _(sp):
            core.zero_past(sp)

        @block.tensor
        def _(pe):
            def products(n):
                h, d = units[n]
                pe.wait_ge(weighed, (n + 1) * TB)
                for pair in range(2):
                    if n >= 2:
                        pe.wait_ge(out_read, 2 * (n - 2) + pair + 1)
                    for j in range(2):
                        t = 2 * pair + j
                        keys = range(t + 1) if d == 0 else range(t, TB)
                        for sb in keys:
                            last = nc.tensor.matmul(m.bank[:, OBANK + 2 * (n % 2) + pair, j * (P + 1):(j + 1) * (P + 1)],
                                                    weights[:, n % 2, sb, t * P:(t + 1) * P], m.mv[:, sb, h, :],
                                                    start=sb == keys[0], stop=sb == keys[-1])
                    last.then_inc(pv_done, 1)

            for n, (h, d) in enumerate(units):
                if n >= 1:
                    pe.wait_ge(decay_done, n * TB)
                mask = m.strict_bf if d == 0 else m.causal_bf
                nc.tensor.matmul(m.bank[:, MBANK, :], select[:, d * GH + h, :], m.rows[:, 5 * SEQ:6 * SEQ], start=True, stop=True)
                nc.tensor.matmul(m.bank[:, MBANK + 1, :], select[:, d * GH + h, :], m.rows[:, 5 * SEQ:6 * SEQ], start=True,
                                 stop=False)
                for t in range(TB):
                    last = nc.tensor.matmul(m.bank[:, MBANK + 1, t * P:(t + 1) * P], m.ident_bf[:], mask[:], start=False,
                                            stop=t == TB - 1)
                last.then_inc(spread_done, 1)
                for sb in range(TB):
                    i = n * TB + sb
                    if i >= 2:
                        pe.wait_ge(weighed, i - 1)
                    q = queries(d, sb)
                    nc.tensor.matmul(m.bank[:, SBANK + i % 2, q], m.fm[:, FM_AT["mk"] + h, sb * P:(sb + 1) * P],
                                     m.fm[:, FM_AT["mq"] + h, q], start=True, stop=True).then_inc(score_done, 1)
                if n >= 1:
                    products(n - 1)
            products(len(units) - 1)

        @block.scalar
        def _(act):
            nc.scalar.activation(least, m.bm_tok, ACT.Exp, scale=-1.0).then_inc(least_done, 1)
            for n, (h, d) in enumerate(units):
                act.wait_ge(spread_done, n + 1)
                for sb in range(TB):
                    i = n * TB + sb
                    if i >= 2:
                        act.wait_ge(weighed, i - 1)
                    shift = m.shift_tok[:, sb, gate_row(d, h):gate_row(d, h) + 1]
                    own = slice(sb * P, (sb + 1) * P)
                    rest = slice((sb + 1) * P, SEQ) if d == 0 else slice(0, sb * P)
                    last = nc.scalar.activation(decay[:, i % 2, own], m.bank[:, MBANK + 1, own], ACT.Exp, bias=shift)
                    if rest.stop > rest.start:
                        last = nc.scalar.activation(decay[:, i % 2, rest], m.bank[:, MBANK, rest], ACT.Exp, bias=shift)
                    last.then_inc(decay_done, 1)

        @block.vector
        def _(dve):
            link = chained(dve, chain)
            dve.wait_ge(least_done, 1)

            def divide(n):
                h, d = units[n]
                for pair in range(2):
                    dve.wait_ge(pv_done, 2 * n + pair + 1)
                    bank = m.bank[:, OBANK + 2 * (n % 2) + pair, 0:2 * (P + 1)].rearrange("p (t c) -> p t c", t=2)
                    x = den[:, n, 2 * pair:2 * pair + 2]
                    low = least[:, 2 * pair:2 * pair + 2, gate_row(d, h)]
                    out = m.o_tok[:, 2 * pair:2 * pair + 2, h * P:(h + 1) * P]
                    link(nc.vector.scalar_tensor_tensor(x, bank[:, :, P], -1.0, low, ALU.mult, ALU.max))
                    link(nc.vector.tensor_tensor(x, bank[:, :, P], x, ALU.max))
                    link(nc.vector.reciprocal(x, x))
                    to = out if d == 0 else part
                    nc.vector.tensor_tensor(to, bank[:, :, 0:P], per_head(x, P), ALU.mult).then_inc(out_read, 1)
                    if d == 1:
                        dve.wait_ge(out_read, 2 * n + pair + 1)
                        link(nc.vector.tensor_tensor(out, out, part, ALU.add))

            for n, (h, d) in enumerate(units):
                for sb in range(TB):
                    i = n * TB + sb
                    dve.wait_ge(score_done, i + 1)
                    dve.wait_ge(decay_done, i + 1)
                    if n >= 2 and sb == 0:
                        dve.wait_ge(pv_done, 2 * (n - 1))
                    q = queries(d, sb)
                    nc.vector.scalar_tensor_tensor(weights[:, n % 2, sb, q], m.bank[:, SBANK + i % 2, q], P ** -0.5,
                                                   decay[:, i % 2, q], ALU.mult, ALU.mult).then_inc(weighed, 1)
                if n >= 1:
                    divide(n - 1)
            divide(len(units) - 1)


def gated_norm(core, m, name, at_chunk, func, gain):
    nc = core.nc
    sums = m.small[:, 0:TB * GH].rearrange("p (t h) -> p t h", t=TB)
    squares = m.w[:, 0:TB * SEQ].rearrange("p (t c) -> p t c", t=TB)
    gates = m.w[:, 2048:2048 + GH * SEQ].rearrange("p (h t) -> p h t", h=GH)
    squared, mean_ready, rooted, scaled = (core.sem(f"{name}_{n}") for n in ("squared", "mean_ready", "rooted", "scaled"))
    gated, turned, chain = (core.sem(f"{name}_{n}") for n in ("gated", "turned", "chain"))

    with nc.Block() as block:
        @block.sync
        def _(sp):
            core.zero_past(sp)

        @block.scalar
        def _(act):
            nc.scalar.activation(squares, m.o_tok, ACT.Square).then_inc(squared, 1)
            act.wait_ge(mean_ready, 1)
            nc.scalar.activation(sums, sums, ACT.Sqrt).then_inc(rooted, 1)
            nc.scalar.activation(gates, m.fm[:, at_chunk:at_chunk + GH, :], func).then_inc(gated, 1)

        @block.vector
        def _(dve):
            link = chained(dve, chain)
            dve.wait_ge(squared, 1)
            link(nc.vector.tensor_reduce(sums, squares.rearrange("p t (h c) -> p t h c", h=GH), AX.X, ALU.add))
            nc.vector.tensor_scalar(sums, sums, 1.0 / P, EPS, ALU.mult, ALU.add).then_inc(mean_ready, 1)
            dve.wait_ge(rooted, 1)
            link(nc.vector.reciprocal(sums, sums))
            for t in range(TB):
                o = m.o_tok[:, t, :].rearrange("p (h c) -> p h c", h=GH)
                nc.vector.tensor_tensor(o, o, per_head(sums[:, t, :], P), ALU.mult).then_inc(scaled, 1)
            dve.wait_ge(gated, 1)
            for h in range(GH):
                dve.wait_ge(turned, h + 1)
                nc.vector.scalar_tensor_tensor(m.fm[:, at_chunk + h, :], m.bank[:, h, :], gain(h), gates[:, h, :], ALU.mult,
                                               ALU.mult)

        @block.tensor
        def _(pe):
            pe.wait_ge(scaled, TB)
            for h in range(GH):
                for t in range(TB):
                    last = nc.tensor.transpose(m.bank[:, h, t * P:(t + 1) * P], m.o_tok[:, t, h * P:(h + 1) * P], m.ident)
                last.then_inc(turned, 1)


def conv_and_turn(core, m):
    nc = core.nc
    N = 3 * GH
    taps = m.gdn_small[:, 16:16 + N * CONV_K].rearrange("p (c j) -> p c j", c=N)
    conv_done, silu_done, squared, summed, mean_ready, rooted = (
        core.sem(f"conv_{n}") for n in ("done", "silu_done", "squared", "summed", "mean_ready", "rooted"))
    unit, turned, turned_read, products_done, products_read, chain = (
        core.sem(f"conv_{n}") for n in ("unit", "turned", "turned_read", "products_done", "products_read", "chain"))
    square = m.scratch.rearrange("p (n t) -> p n t", n=4)[:, 0:2]
    root = m.scratch.rearrange("p (n t) -> p n t", n=4)[:, 2:4]
    mid = CONV_K // 2

    with nc.Block() as block:
        @block.sync
        def _(sp):
            core.zero_past(sp)

        @block.vector
        def _(dve):
            link = chained(dve, chain)
            for c in range(N):
                link(nc.vector.tensor_scalar(m.cv[:, c, :], m.fm[:, c, :], taps[:, c, mid:mid + 1], None, ALU.mult))
                for j in [j for j in range(CONV_K) if j != mid]:
                    off = j - mid
                    to = slice(max(0, -off), SEQ - max(0, off))
                    of = slice(max(0, off), SEQ - max(0, -off))
                    last = nc.vector.scalar_tensor_tensor(m.cv[:, c, to], m.fm[:, c, of], taps[:, c, j:j + 1], m.cv[:, c, to],
                                                          ALU.mult, ALU.add)
                    if j != CONV_K - 1:
                        link(last)
                last.then_inc(conv_done, 1)
            for c in range(2 * GH):
                dve.wait_ge(summed, c + 1)
                nc.vector.tensor_scalar(root[:, c % 2, :], m.bank[:, c % 2, :], EPS, None, ALU.add).then_inc(mean_ready, 1)
                dve.wait_ge(rooted, c + 1)
                link(nc.vector.reciprocal(root[:, c % 2, :], root[:, c % 2, :]))
                scale = P ** -0.5 if c < GH else 1.0
                nc.vector.scalar_tensor_tensor(m.cv[:, c, :], m.cv[:, c, :], scale, root[:, c % 2, :], ALU.mult, ALU.mult)\
                    .then_inc(unit, 1)
            for t in range(TB):
                dve.wait_ge(products_done, 2 * t + 1)
                nc.vector.tensor_copy(m.kk[:, t, :], m.bank[:, 4 + 2 * (t % 2), :]).then_inc(products_read, 1)

        @block.scalar
        def _(act):
            for c in range(N):
                act.wait_ge(conv_done, c + 1)
                nc.scalar.activation(m.cv[:, c, :], m.cv[:, c, :], ACT.Silu).then_inc(silu_done, 1)
            act.wait_ge(silu_done, 2 * GH)
            for c in range(2 * GH):
                if c >= 2:
                    act.wait_ge(summed, c - 1)
                nc.scalar.activation(square[:, c % 2, :], m.cv[:, c, :], ACT.Square).then_inc(squared, 1)
                act.wait_ge(mean_ready, c + 1)
                nc.scalar.activation(root[:, c % 2, :], root[:, c % 2, :], ACT.Sqrt).then_inc(rooted, 1)
            for i in range(2 * TB):
                act.wait_ge(turned, i + 1)
                to = m.k_tok if i < TB else m.v_tok
                nc.scalar.copy(to[:, i % TB, :], m.bank[:, 2 + i % 2, :]).then_inc(turned_read, 1)
            for t in range(TB):
                act.wait_ge(products_done, 2 * t + 2)
                nc.scalar.copy(m.qk[:, t, :], m.bank[:, 5 + 2 * (t % 2), :]).then_inc(turned_read, 1)

        @block.tensor
        def _(pe):
            for c in range(2 * GH):
                pe.wait_ge(squared, c + 1)
                if c >= 2:
                    pe.wait_ge(mean_ready, c - 1)
                nc.tensor.matmul(m.bank[:, c % 2, :], m.ones[:], square[:, c % 2, :], start=True, stop=True).then_inc(summed, 1)
            pe.wait_ge(unit, 2 * GH)
            pe.wait_ge(silu_done, N)
            for i in range(2 * TB):
                if i >= 2:
                    pe.wait_ge(turned_read, i - 1)
                for h in range(GH):
                    c = GH + h if i < TB else 2 * GH + h
                    t = i % TB
                    last = nc.tensor.transpose(m.bank[:, 2 + i % 2, h * P:(h + 1) * P], m.cv[:, c, t * P:(t + 1) * P], m.ident)
                last.then_inc(turned, 1)
            for t in range(TB):
                tokens = slice(t * P, (t + 1) * P)
                if t >= 2:
                    pe.wait_ge(products_read, t - 1)
                    pe.wait_ge(turned_read, 2 * TB + t - 1)
                for i, left in enumerate((GH, 0)):
                    for h in range(GH):
                        last = nc.tensor.matmul(m.bank[:, 4 + 2 * (t % 2) + i, h * P:(h + 1) * P], m.cv[:, left + h, tokens],
                                                m.cv[:, GH + h, tokens], start=True, stop=True)
                    last.then_inc(products_done, 1)


def delta_inverse(core, m):
    nc = core.nc
    W = GH * P
    names = ("E", "N", "D", "Dt", "D2", "D2t", "D4", "D4t", "D8", "Y", "X", "Z")
    buf = [{n: m.w[:, (d * len(names) + i) * W:(d * len(names) + i + 1) * W] for i, n in enumerate(names)} for d in range(DIRS)]
    select = m.select.rearrange("p (r c) -> p r c", c=P)
    heads = lambda x: x.rearrange("p (h c) -> p h c", h=GH)
    masked = core.sem("inv_masked")
    act_done = [core.sem(f"inv_act_done{d}") for d in range(DIRS)]
    dve_done = [core.sem(f"inv_dve_done{d}") for d in range(DIRS)]
    pe_done = [core.sem(f"inv_pe_done{d}") for d in range(DIRS)]
    links = [core.sem(f"inv_link{d}") for d in range(DIRS)]

    def lane(b, d):
        return b if d == 0 else TB - 1 - b

    with nc.Block() as block:
        @block.sync
        def _(sp):
            core.zero_past(sp)

        steps = ["exponents", "turned_qk", "turned_D", "D2", "D2t", "D4", "D4t", "D8", "Y1", "Y2", "Y3"]
        for b_ in (16, 32, 64):
            steps += [f"X{b_}", f"Z{b_}", f"J{b_}"]
        at_step = {n: i for i, n in enumerate(steps)}
        per_block = len(steps)

        def bank(step, d):
            return 4 * d + at_step[step] % 4

        by_dve = ("turned_D", "Y1", "Y2", "Y3", "J16", "J32", "J64", "D2t", "D4t")
        by_act = [n for n in steps if n not in by_dve]
        dve_at = {n: i for i, n in enumerate([n for n in steps if n in by_dve])}
        act_at = {n: i for i, n in enumerate(by_act)}

        def wait_read(eng, n, d, b):
            if n in dve_at:
                eng.wait_ge(dve_done[d], b * len(dve_at) + dve_at[n] + 1)
            else:
                eng.wait_ge(act_done[d], b * len(act_at) + act_at[n] + 1)

        def wait_made(eng, n, d, b):
            eng.wait_ge(pe_done[d], b * per_block + at_step[n] + 1)

        @block.tensor
        def _(pe):
            def product(n, d, b, left, right, needs):
                for x in needs:
                    wait_read(pe, x, d, b)
                last_user = steps[at_step[n] - 4] if at_step[n] >= 4 else None
                if last_user:
                    wait_read(pe, last_user, d, b)
                to = heads(m.bank[:, bank(n, d), :])
                for h in range(GH):
                    last = nc.tensor.matmul(to[:, h, :], heads(buf[d][left])[:, h, :], heads(buf[d][right])[:, h, :],
                                            start=True, stop=True)
                last.then_inc(pe_done[d], 1)

            def turn(n, d, b, src, needs):
                for x in needs:
                    wait_read(pe, x, d, b)
                last_user = steps[at_step[n] - 4] if at_step[n] >= 4 else None
                if last_user:
                    wait_read(pe, last_user, d, b)
                for h in range(GH):
                    last = nc.tensor.transpose(m.bank[:, bank(n, d), h * P:(h + 1) * P], heads(src)[:, h, :], m.ident)
                last.then_inc(pe_done[d], 1)

            for b in range(TB):
                for d in range(DIRS):
                    t = lane(b, d)
                    if b >= 1:
                        for n in steps[-4:]:
                            wait_read(pe, n, d, b - 1)
                    mask = m.causal_bf if d == 0 else m.strict_bf
                    for h in range(GH):
                        to = m.bank[:, bank("exponents", d), h * P:(h + 1) * P]
                        nc.tensor.matmul(to, select[:, d * GH + h, :], m.rows[:, SEQ + t * P:SEQ + (t + 1) * P], start=True,
                                         stop=False)
                        last = nc.tensor.matmul(to, m.ident_neg[:], mask[:], start=False, stop=True)
                    last.then_inc(pe_done[d], 1)
                for d in range(DIRS):
                    pe.wait_ge(masked, 2 * (b * DIRS + d) + 1)
                    turn("turned_qk", d, b, buf[d]["Z"], ())
                for d in range(DIRS):
                    pe.wait_ge(masked, 2 * (b * DIRS + d) + 2)
                    turn("turned_D", d, b, buf[d]["D"], ())
                for n, left, right, needs in (
                        ("D2", "Dt", "D", ("turned_D",)), ("D2t", "D", "Dt", ()),
                        ("D4", "D2t", "D2", ("D2", "D2t")), ("D4t", "D2", "D2t", ()),
                        ("D8", "D4t", "D4", ("D4", "D4t")),
                        ("Y1", "D2", "Y", ()), ("Y2", "D4", "Y", ("Y1",)), ("Y3", "D8", "Y", ("D8", "Y2"))):
                    for d in range(DIRS):
                        product(n, d, b, left, right, needs)
                for size, before in ((16, "Y3"), (32, "J16"), (64, "J32")):
                    for d in range(DIRS):
                        turn(f"X{size}", d, b, buf[d]["Y"], (before,))
                    for d in range(DIRS):
                        off = {16: "D", 32: "D2", 64: "D4"}[size]
                        product(f"Z{size}", d, b, off, "Y", ())
                    for d in range(DIRS):
                        product(f"J{size}", d, b, "X", "Z", (f"X{size}", f"Z{size}"))

        @block.scalar
        def _(act):
            for b in range(TB):
                for d in range(DIRS):
                    t = lane(b, d)
                    wait_made(act, "exponents", d, b)
                    e = heads(buf[d]["E"])
                    if b >= 1:
                        act.wait_ge(masked, 2 * ((b - 1) * DIRS + d) + 2)
                    for h in range(GH):
                        r = gate_row(d, h)
                        last = nc.scalar.activation(e[:, h, :], m.bank[:, bank("exponents", d), h * P:(h + 1) * P], ACT.Exp,
                                                    bias=m.g_tok[:, t, r:r + 1], scale=-1.0)
                    last.then_inc(act_done[d], 1)
                for n, to in (("turned_qk", None), ("D2", "D2"), ("D4", "D4"), ("D8", "D8"), ("X16", "X"), ("Z16", "Z"),
                              ("X32", "X"), ("Z32", "Z"), ("X64", "X"), ("Z64", "Z")):
                    for d in range(DIRS):
                        wait_made(act, n, d, b)
                        dst = m.qk_t[:, d * TB + lane(b, d), :] if to is None else buf[d][to]
                        nc.scalar.copy(dst, m.bank[:, bank(n, d), :]).then_inc(act_done[d], 1)

        @block.vector
        def _(dve):
            link = [chained(dve, s) for s in links]
            mask = [{n: spread(m.block_mask[:, (d * 4 + i) * P:(d * 4 + i + 1) * P], GH) for i, n in enumerate((16, "16", "32", "64"))}
                    for d in range(DIRS)]
            ident = spread(m.ident, GH)
            for b in range(TB):
                for d in range(DIRS):
                    t = lane(b, d)
                    w = buf[d]
                    wait_read(dve, "exponents", d, b)
                    nc.vector.tensor_tensor(w["Z"], m.qk[:, t, :], w["E"], ALU.mult).then_inc(masked, 1)
                    link[d](nc.vector.tensor_tensor(w["N"], m.kk[:, t, :], w["E"], ALU.mult))
                    beta = m.beta[:, t, d * BACK:d * BACK + GH]
                    link[d](nc.vector.tensor_tensor(heads(w["N"]), heads(w["N"]), per_head(beta, P), ALU.mult))
                    link[d](nc.vector.tensor_scalar(w["N"], w["N"], -1.0, None, ALU.mult))
                    nc.vector.tensor_tensor(heads(w["D"]), heads(w["N"]), mask[d][16], ALU.mult).then_inc(masked, 1)
                    dve.wait_ge(masked, 2 * (b * DIRS + d) + 2)

                def copied(n, d, instruction):
                    instruction.then_inc(dve_done[d], 1)
                    wait_read(dve, n, d, b)

                for d in range(DIRS):
                    wait_made(dve, "turned_D", d, b)
                    w = buf[d]
                    link[d](nc.vector.tensor_tensor(heads(w["Y"]), heads(m.bank[:, bank("turned_D", d), :]), ident, ALU.add))
                    copied("turned_D", d, nc.vector.tensor_copy(w["Dt"], m.bank[:, bank("turned_D", d), :]))
                for d in range(DIRS):
                    wait_made(dve, "D2t", d, b)
                    copied("D2t", d, nc.vector.tensor_copy(buf[d]["D2t"], m.bank[:, bank("D2t", d), :]))
                for d in range(DIRS):
                    wait_made(dve, "D4t", d, b)
                    copied("D4t", d, nc.vector.tensor_copy(buf[d]["D4t"], m.bank[:, bank("D4t", d), :]))
                for n, off in (("Y1", None), ("Y2", None), ("Y3", "16"), ("J16", "32"), ("J32", "64"), ("J64", None)):
                    for d in range(DIRS):
                        w = buf[d]
                        wait_made(dve, n, d, b)
                        if n == "Y3":
                            link[d](nc.vector.tensor_tensor(heads(w["D"]), heads(w["N"]), mask[d]["16"], ALU.mult))
                            link[d](nc.vector.tensor_tensor(heads(w["D2"]), heads(w["N"]), mask[d]["32"], ALU.mult))
                            link[d](nc.vector.tensor_tensor(heads(w["D4"]), heads(w["N"]), mask[d]["64"], ALU.mult))
                        if n == "J64":
                            t = lane(b, d)
                            out = m.inverse[:, d * TB + t, :]
                            link[d](nc.vector.tensor_tensor(w["Y"], w["Y"], m.bank[:, bank(n, d), :], ALU.add))
                            beta = m.beta[:, t, d * BACK:d * BACK + GH]
                            copied(n, d, nc.vector.tensor_tensor(heads(out), heads(w["Y"]), per_head(beta, P), ALU.mult))
                        else:
                            copied(n, d, nc.vector.tensor_tensor(w["Y"], w["Y"], m.bank[:, bank(n, d), :], ALU.add))


def delta_rule(core, m):
    nc = core.nc
    W = GH * P
    heads = lambda x: x.rearrange("p (h c) -> p h c", h=GH)
    k_dec = m.w[:, 0:2 * TB * W].rearrange("p (n c) -> p n c", c=W)
    state = [m.w[:, (8 + d) * W:(9 + d) * W] for d in range(DIRS)]
    rest = [m.w[:, (10 + d) * W:(11 + d) * W] for d in range(DIRS)]
    new = [m.w[:, (12 + d) * W:(13 + d) * W] for d in range(DIRS)]
    from_state = [m.w[:, (14 + d) * W:(15 + d) * W] for d in range(DIRS)]
    kept = [m.w[:, (16 + d) * W:(17 + d) * W] for d in range(DIRS)]
    GW = TB * DIRS * GH
    grown = m.w[:, 18 * W:18 * W + GW].rearrange("p (t r) -> p t r", t=TB)
    left = m.w[:, 18 * W + GW:18 * W + 2 * GW].rearrange("p (t r) -> p t r", t=TB)
    whole = m.w[:, 18 * W + 2 * GW:18 * W + 3 * GW].rearrange("p (t r) -> p t r", t=TB)
    factors, exponents, decayed = (core.sem(f"rule_{n}") for n in ("factors", "exponents", "decayed"))
    ks_done, qs_done, new_done, out_done, add_done = (
        [core.sem(f"rule_{n}{d}") for d in range(DIRS)] for n in ("ks_done", "qs_done", "new_done", "out_done", "add_done"))
    rest_ready, new_ready, state_ready, out_ready, qs_read = (
        [core.sem(f"rule_{n}{d}") for d in range(DIRS)] for n in ("rest_ready", "new_ready", "state_ready", "out_ready", "qs_read"))
    links, ends_done = core.sem("rule_link"), core.sem("rule_ends_done")
    select = m.select.rearrange("p (r c) -> p r c", c=P)
    ends = m.bank[:, 2, 0:DIRS * GH * TB].rearrange("p (r t) -> p t r", t=TB)

    def lane(i, d):
        return i if d == 0 else TB - 1 - i

    def rows_of(x, d):
        return x[:, d * GH:(d + 1) * GH]

    with nc.Block() as block:
        @block.sync
        def _(sp):
            core.zero_past(sp)

        @block.tensor
        def _(pe):
            for r in range(DIRS * GH):
                end = P - 1 if r < GH else 0
                last = nc.tensor.matmul(m.bank[:, 2, r * TB:(r + 1) * TB], select[:, r, :], m.rows[:, SEQ + end:2 * SEQ:P],
                                        start=True, stop=True)
            last.then_inc(ends_done, 1)
            for i in range(TB):
                for d in range(DIRS):
                    t = lane(i, d)
                    tokens = slice(t * P, (t + 1) * P)
                    pe.wait_ge(state_ready[d], i + 1)
                    for left_at, bank, done in ((GH, 0, ks_done), (0, 1, qs_done)):
                        for h in range(GH):
                            last = nc.tensor.matmul(heads(m.bank[:, 4 * d + bank, :])[:, h, :], m.cv[:, left_at + h, tokens],
                                                    heads(state[d])[:, h, :], start=True, stop=True)
                        last.then_inc(done[d], 1)
                for d in range(DIRS):
                    t = lane(i, d)
                    pe.wait_ge(rest_ready[d], i + 1)
                    for h in range(GH):
                        last = nc.tensor.matmul(heads(m.bank[:, 4 * d, :])[:, h, :], heads(m.inverse[:, d * TB + t, :])[:, h, :],
                                                heads(rest[d])[:, h, :], start=True, stop=True)
                    last.then_inc(new_done[d], 1)
                for d in range(DIRS):
                    t = lane(i, d)
                    pe.wait_ge(new_ready[d], i + 1)
                    if i == 0:
                        pe.wait_ge(decayed, TB * DIRS)
                    for h in range(GH):
                        last = nc.tensor.matmul(heads(m.bank[:, 4 * d + 3, :])[:, h, :], heads(k_dec[:, d * TB + t, :])[:, h, :],
                                                heads(new[d])[:, h, :], start=True, stop=True)
                    last.then_inc(add_done[d], 1)
                    if i >= 1:
                        pe.wait_ge(out_ready[d], i)
                    for h in range(GH):
                        last = nc.tensor.matmul(heads(m.bank[:, 4 * d + 2, :])[:, h, :], heads(m.qk_t[:, d * TB + t, :])[:, h, :],
                                                heads(new[d])[:, h, :], start=True, stop=True)
                    last.then_inc(out_done[d], 1)

        @block.scalar
        def _(act):
            act.wait_ge(exponents, 1)
            nc.scalar.activation(left, left, ACT.Exp).then_inc(factors, 1)
            nc.scalar.activation(grown, grown, ACT.Exp).then_inc(factors, 1)
            nc.scalar.activation(whole, whole, ACT.Exp).then_inc(factors, 1)
            for i in range(TB):
                for d in range(DIRS):
                    act.wait_ge(new_done[d], i + 1)
                    if i >= 1:
                        act.wait_ge(out_done[d], i)
                    nc.scalar.copy(new[d], m.bank[:, 4 * d, :]).then_inc(new_ready[d], 1)

        @block.gpsimd
        def _(pool):
            pool.wait_ge(factors, 1)
            for i in range(TB):
                for d in range(DIRS):
                    t = lane(i, d)
                    nc.gpsimd.tensor_tensor(heads(k_dec[:, d * TB + t, :]), heads(m.k_tok[:, t, :]),
                                            per_head(rows_of(left[:, t, :], d), P), ALU.mult).then_inc(decayed, 1)

        @block.vector
        def _(dve):
            link = chained(dve, links)
            for d in range(DIRS):
                last = nc.vector.memset(state[d], 0.0).then_inc(state_ready[d], 1)
            dve.wait_ge(ends_done, 1)
            for d in range(DIRS):
                g = m.g_tok[:, :, d * BACK:d * BACK + GH]
                part = slice(d * GH, (d + 1) * GH)
                link(nc.vector.tensor_tensor(left[:, :, part], ends[:, :, part], g, ALU.subtract))
                link(nc.vector.tensor_copy(grown[:, :, part], g))
            nc.vector.tensor_copy(whole, ends).then_inc(exponents, 1)
            dve.wait_ge(factors, 3)
            for i in range(TB):
                for d in range(DIRS):
                    t = lane(i, d)
                    dve.wait_ge(ks_done[d], i + 1)
                    up = per_head(rows_of(grown[:, t, :], d), P)
                    if i >= 1:
                        dve.wait_ge(new_done[d], i)
                    link(nc.vector.tensor_tensor(heads(rest[d]), heads(m.bank[:, 4 * d, :]), up, ALU.mult))
                    nc.vector.tensor_tensor(rest[d], m.v_tok[:, t, :], rest[d], ALU.subtract).then_inc(rest_ready[d], 1)
                for d in range(DIRS):
                    t = lane(i, d)
                    dve.wait_ge(qs_done[d], i + 1)
                    up = per_head(rows_of(grown[:, t, :], d), P)
                    link(nc.vector.tensor_tensor(heads(from_state[d]), heads(m.bank[:, 4 * d + 1, :]), up, ALU.mult))
                    if i < TB - 1:
                        link(nc.vector.tensor_tensor(heads(kept[d]), heads(state[d]), per_head(rows_of(whole[:, t, :], d), P),
                                                     ALU.mult))
                        dve.wait_ge(add_done[d], i + 1)
                        nc.vector.tensor_tensor(state[d], kept[d], m.bank[:, 4 * d + 3, :], ALU.add).then_inc(state_ready[d], 1)
                        dve.wait_ge(state_ready[d], i + 2)
                for d in range(DIRS):
                    t = lane(i, d)
                    dve.wait_ge(out_done[d], i + 1)
                    o = m.o_tok[:, t, :]
                    if i > lane(t, 1 - d):
                        link(nc.vector.tensor_tensor(o, o, from_state[d], ALU.add))
                        nc.vector.tensor_tensor(o, o, m.bank[:, 4 * d + 2, :], ALU.add).then_inc(out_ready[d], 1)
                    else:
                        nc.vector.tensor_tensor(o, from_state[d], m.bank[:, 4 * d + 2, :], ALU.add).then_inc(out_ready[d], 1)
                    dve.wait_ge(out_ready[d], i + 1)


def out_projection(core, m, w_dram):
    nc = core.nc
    w = m.w[:, 0:DK * D].rearrange("p (k c) -> p k c", k=DK)
    y = m.fm[:, FM_AT["gz"]:FM_AT["gz"] + DK, :]
    loaded = [core.sem(f"out2_loaded{k}") for k in range(DK)]
    done = core.sem("out2_done")
    with nc.Block() as block:
        @block.sync
        def _(sp):
            for k in range(DK):
                sp.dma_start(w[:, k, :], w_dram[k]).then_inc(loaded[k], 16)
            core.zero_past(sp)

        @block.tensor
        def _(pe):
            for k in range(DK):
                pe.wait_ge(loaded[k], 16)
                for c in range(DK):
                    last = nc.tensor.matmul(m.bank[:, c, :], w[:, k, c * P:(c + 1) * P], y[:, k, :], start=k == 0,
                                            stop=k == DK - 1)
                    if k == DK - 1:
                        last.then_inc(done, 1)

        @block.vector
        def _(dve):
            for c in range(DK):
                dve.wait_ge(done, c + 1)
                nc.vector.tensor_tensor(m.x[:, c, :], m.bank[:, c, :], m.x[:, c, :], ALU.add)


PH, KEYS, TOP = 8, 128, 16
PAIRS = 2 * PH
PICKS = PH * TOP
RING = 8


def expert_queries(core, m, a):
    nc = core.nc
    SLOTS = 2
    w = m.w[:, 0:SLOTS * D].rearrange("p (s k c) -> p s k c", s=SLOTS, k=DK)
    s = norm_steps(core, "peer")
    loaded = [core.sem(f"wq_loaded{i}") for i in range(SLOTS)]
    done = [core.sem(f"wq_done{i}") for i in range(SLOTS)]
    copied = [core.sem(f"wq_copied{i}") for i in range(SLOTS)]
    rest_loaded = core.sem("peer_rest_loaded")
    rounds = PAIRS // SLOTS

    with nc.Block() as block:
        @block.sync
        def _(sp):
            sp.dma_start(m.gain[:], a["norm2_2"]).then_inc(s["gain_loaded"], 16)

            def load(r, i):
                sp.dma_start(m.w[:, i * D:(i + 1) * D], one(a["peer_wq_2"], r * SLOTS + i)).then_inc(loaded[i], 16)

            for i in range(SLOTS):
                load(0, i)
            sp.dma_start(m.keys, a["peer_keys_2"]).then_inc(rest_loaded, 16)
            sp.dma_start(m.final_gain, a["normf_2"]).then_inc(rest_loaded, 16)
            sp.dma_start(m.iota, a["iota"]).then_inc(rest_loaded, 16)
            with sp.Fori(1, rounds) as r:
                for i in range(SLOTS):
                    sp.wait_ge(done[i], r)
                    load(r, i)
            sp.wait_ge(rest_loaded, 48)
            core.zero_past(sp)

        @block.tensor
        def _(pe):
            norm_tensor(nc, pe, m, s)
            pe.wait_ge(s["normed"], DK)

            def chunk(r, i, first):
                pe.wait_ge(loaded[i], r * 16 + 16)
                if not first:
                    pe.wait_ge(copied[i], r)
                for k in range(DK):
                    last = nc.tensor.matmul(m.bank[:, i, :], w[:, i, k, :], m.h[:, k, :], start=k == 0, stop=k == DK - 1)
                last.then_inc(done[i], 1)

            for i in range(SLOTS):
                chunk(0, i, True)
            with pe.Fori(1, rounds) as r:
                for i in range(SLOTS):
                    chunk(r, i, False)

        @block.scalar
        def _(act):
            norm_scalar(nc, act, m, s)
            with act.Fori(0, rounds) as r:
                for i in range(SLOTS):
                    act.wait_ge(done[i], r + 1)
                    nc.scalar.copy(column(m.queries, r * SLOTS + i), m.bank[:, i, :]).then_inc(copied[i], 1)

        @block.vector
        def _(dve):
            norm_vector(nc, dve, m, s, m.gain)


def top_16(vector, link, values, left, top, index, width):
    link(vector.max(top[:, 0:8], values))
    vector.max_index(index[:, 0:8], top[:, 0:8], values)
    link(vector.match_replace(left, top[:, 0:8], values, NEG))
    link(vector.max(top[:, 8:16], left))
    return vector.max_index(index[:, 8:16], top[:, 8:16], left)


def choose_experts(core, m):
    nc = core.nc
    NS = PAIRS * KEYS
    z = m.choose
    scores, left = z[:, 0:NS], z[:, NS:2 * NS]
    halves = z[:, 2 * NS:2 * NS + PAIRS * TOP]
    where = z[:, 4352:4352 + PAIRS * TOP].bitcast(U32)
    where_f = z[:, 4608:4608 + PAIRS * TOP]
    best = z[:, 4864:4864 + PICKS]
    place = z[:, 4992:4992 + PICKS].bitcast(U32)
    part = z[:, 5120:5120 + PICKS].bitcast(U32)
    part_f = z[:, 5248:5248 + PICKS]
    rows = [z[:, 5376 + i * PICKS:5376 + (i + 1) * PICKS] for i in range(2)]
    total = z[:, 5632:5632 + PH]
    score_done, score_read, exp_ready, exp_done, chain = (
        core.sem(f"choose_{n}") for n in ("score_done", "score_read", "exp_ready", "exp_done", "chain"))

    with nc.Block() as block:
        @block.sync
        def _(sp):
            core.zero_past(sp)

        @block.tensor
        def _(pe):
            for t in range(TB):
                for q in range(4):
                    if t >= 2:
                        pe.wait_ge(score_read, 4 * (t - 2) + q + 1)
                    for j in range(4):
                        i = 4 * q + j
                        last = nc.tensor.matmul(m.bank[:, 4 * (t % 2) + q, j * KEYS:(j + 1) * KEYS],
                                                m.queries[:, i, t * P:(t + 1) * P],
                                                m.keys[:, i * KEYS:(i + 1) * KEYS], start=True, stop=True)
                    last.then_inc(score_done, 1)

        @block.scalar
        def _(act):
            for t in range(TB):
                if t >= 1:
                    act.wait_ge(exp_ready, t)
                for q in range(4):
                    act.wait_ge(score_done, 4 * t + q + 1)
                    nc.scalar.copy(scores[:, q * SEQ:(q + 1) * SEQ], m.bank[:, 4 * (t % 2) + q, :]).then_inc(score_read, 1)
                act.wait_ge(exp_ready, t + 1)
                nc.scalar.activation(m.picked[:, t, :], m.picked[:, t, :], ACT.Exp).then_inc(exp_done, 1)

        @block.vector
        def _(dve):
            link = chained(dve, chain)
            v = nc.vector
            pairs = lambda x: x.rearrange("p (h k j) -> p h k j", h=PH, k=TOP)
            inner = lambda x: x.rearrange("p (h k one) -> p h k one", h=PH, one=1).broadcast_to([P, PH, TOP, TOP])
            outer = lambda x: x.rearrange("p (h one j) -> p h one j", h=PH, one=1).broadcast_to([P, PH, TOP, TOP])
            half = lambda x, i: x.rearrange("p (h two k) -> p two h k", h=PH, two=2)[:, i]
            for t in range(TB):
                dve.wait_ge(score_read, 4 * t + 4)
                for i in range(PAIRS):
                    last = top_16(v, link, scores[:, i * KEYS:(i + 1) * KEYS], left[:, i * KEYS:(i + 1) * KEYS],
                                  halves[:, i * TOP:(i + 1) * TOP], where[:, i * TOP:(i + 1) * TOP], KEYS)
                link(last)
                link(v.tensor_copy(where_f, where))
                first = half(halves, 0).rearrange("p h (k one) -> p h k one", one=1).broadcast_to([P, PH, TOP, TOP])
                second = half(halves, 1).rearrange("p h (one j) -> p h one j", one=1).broadcast_to([P, PH, TOP, TOP])
                link(v.tensor_tensor(pairs(scores), first, second, ALU.add))
                C = TOP * TOP
                for h in range(PH):
                    last = top_16(v, link, scores[:, h * C:(h + 1) * C], left[:, h * C:(h + 1) * C],
                                  best[:, h * TOP:(h + 1) * TOP], place[:, h * TOP:(h + 1) * TOP], C)
                link(last)
                for i in range(2):
                    if i == 0:
                        link(v.tensor_scalar(part, place, 4, None, ALU.logical_shift_right))
                    else:
                        link(v.tensor_scalar(part, place, TOP - 1, None, ALU.bitwise_and))
                    link(v.tensor_copy(part_f, part))
                    link(v.tensor_tensor(pairs(scores), inner(part_f), m.iota.rearrange("p (a j) -> p a j", a=1)
                                         .rearrange("p a (b j) -> p a b j", b=1).broadcast_to([P, PH, TOP, TOP]), ALU.is_equal))
                    keys = half(where_f, i).rearrange("p h (one j) -> p h one j", one=1).broadcast_to([P, PH, TOP, TOP])
                    link(v.tensor_tensor(pairs(scores), pairs(scores), keys, ALU.mult))
                    link(v.tensor_reduce(rows[i], scores.rearrange("p (k j) -> p k j", j=TOP), AX.X, ALU.add))
                link(v.scalar_tensor_tensor(rows[0], rows[0], float(KEYS), rows[1], ALU.mult, ALU.add))
                v.tensor_copy(m.index[:, t, :], rows[0])
                heads = best.rearrange("p (h k) -> p h k", h=PH)
                top = heads[:, :, 0:1].broadcast_to([P, PH, TOP])
                gates = m.picked[:, t, :].rearrange("p (h k) -> p h k", h=PH)
                v.tensor_tensor(gates, heads, top, ALU.subtract).then_inc(exp_ready, 1)
                dve.wait_ge(exp_done, t + 1)
                link(v.tensor_reduce(total, gates, AX.X, ALU.add))
                link(v.reciprocal(total, total))
                link(v.tensor_tensor(gates, gates, per_head(total, TOP), ALU.mult))


def experts(core, m, a, out):
    nc = core.nc
    GROUPS_ = PICKS // RING
    ring = m.w[:, 0:RING * D].rearrange("p (n c) -> p n c", n=RING)
    junk = m.w[:, RING * D:(RING + 1) * D]
    total = m.w[:, 9 * D:10 * D]
    squares = m.w[:, 10 * D:11 * D]
    result = m.w[:, 11 * D:12 * D]
    stage_index = [m.staged[:, i * RING:(i + 1) * RING] for i in range(2)]
    dots = m.dots
    loaded = [core.sem(f"row_loaded{i}") for i in range(RING)]
    used = [core.sem(f"row_used{i}") for i in range(RING)]
    granted, index_staged, turned, acts_ready, gelu_done, weights_ready = (
        core.sem(f"experts_{n}") for n in ("granted", "index_staged", "turned", "acts_ready", "gelu_done", "weights_ready"))
    summed, x_turned, squared, mean_ready, rooted, result_ready, stored, chain = (
        core.sem(f"experts_{n}") for n in ("summed", "x_turned", "squared", "mean_ready", "rooted", "result_ready", "stored",
                                            "chain"))
    sums = m.small[:, 0:1]
    H_BANK, ACC_BANK, X_BANK = 0, 2, 4

    def wide(b):
        return m.bank[:, b:b + 2, :].rearrange("p b c -> p (b c)")

    with nc.Block() as block:
        @block.gpsimd
        def _(pool):
            for t in range(TB):
                for part, table in enumerate((a["peer_u_2"], a["peer_v_2"])):
                    before = (2 * t + part) * GROUPS_
                    with pool.Fori(0, GROUPS_ // 2) as g:
                        for i in range(2):
                            cols = bass.ds((g * 2 + i) * RING, RING)
                            nc.gpsimd.tensor_copy(stage_index[i], m.index[:, t, cols]).then_inc(index_staged, 1)
                            pool.wait_ge(index_staged, before + g * 2 + i + 1)
                            for n in range(RING):
                                pool.wait_ge(used[n], before + g * 2 + i + 1)
                                pool.sem_inc(granted, 1)
                                nc.gpsimd.indirect_dma_start(
                                    ring[:, n, :], None, table,
                                    bass.IndirectOffsetOnAxis(ap=stage_index[i][:, n:n + 1], axis=0)).then_inc(loaded[n], 16)

        @block.tensor
        def _(pe):
            for t in range(TB):
                tokens = slice(t * P, (t + 1) * P)
                if t >= 1:
                    pe.wait_ge(acts_ready, t)
                for k in range(DK):
                    last = nc.tensor.transpose(wide(H_BANK)[:, k * P:(k + 1) * P], m.h[:, k, tokens], m.ident)
                last.then_inc(turned, 1)
                if t >= 1:
                    pe.wait_ge(squared, t)
                for k in range(DK):
                    last = nc.tensor.transpose(wide(X_BANK)[:, k * P:(k + 1) * P], m.x[:, k, tokens], m.ident)
                last.then_inc(x_turned, 1)

        @block.scalar
        def _(act):
            for t in range(TB):
                act.wait_ge(acts_ready, t + 1)
                nc.scalar.activation(m.acts, m.acts, ACT.Gelu).then_inc(gelu_done, 1)
                act.wait_ge(summed, t + 1)
                nc.scalar.activation(squares, total, ACT.Square, accum_out=sums).then_inc(squared, 1)
                act.wait_ge(mean_ready, t + 1)
                nc.scalar.activation(sums, sums, ACT.Sqrt).then_inc(rooted, 1)

        @block.vector
        def _(dve):
            link = chained(dve, chain)
            v = nc.vector
            for n in range(RING):
                dve.sem_inc(used[n], 1)
            for t in range(TB):
                dve.wait_ge(turned, t + 1)
                before = 2 * t * GROUPS_
                with dve.Fori(0, GROUPS_ // 2) as g:
                    for i in range(2):
                        for n in range(RING):
                            dve.wait_ge(loaded[n], (g * 2 + (before + i + 1)) * 16)
                            v.tensor_tensor_reduce(out=junk, in0=ring[:, n, :], in1=wide(H_BANK), scale=1.0, scalar=0.0,
                                                   op0=ALU.mult, op1=ALU.add, accum_out=dots[:, n:n + 1]).then_inc(used[n], 1)
                            dve.wait_ge(used[n], g * 2 + (before + i + 2))
                        v.tensor_copy(m.acts[:, bass.ds((g * 2 + i) * RING, RING)], dots[:, 0:RING]).then_inc(weights_ready, 1)
                        dve.wait_ge(weights_ready, g * 2 + (t * GROUPS_ + i + 1))
                dve.sem_inc(acts_ready, 1)
                dve.wait_ge(gelu_done, t + 1)
                link(v.tensor_tensor(m.acts, m.acts, m.picked[:, t, :], ALU.mult))
                link(v.memset(wide(ACC_BANK), 0.0))
                before += GROUPS_
                with dve.Fori(0, GROUPS_ // 2) as g:
                    for i in range(2):
                        for n in range(RING):
                            dve.wait_ge(loaded[n], (g * 2 + (before + i + 1)) * 16)
                            weight = m.acts[:, bass.ds((g * 2 + i) * RING + n, 1)]
                            v.scalar_tensor_tensor(wide(ACC_BANK), ring[:, n, :], weight, wide(ACC_BANK), ALU.mult, ALU.add)\
                                .then_inc(used[n], 1)
                            dve.wait_ge(used[n], g * 2 + (before + i + 2))
                if t >= 1:
                    dve.wait_ge(stored, 16 * t)
                link(v.tensor_copy(result, wide(ACC_BANK)))
                dve.wait_ge(x_turned, t + 1)
                if t >= 1:
                    dve.wait_ge(squared, t)
                v.tensor_tensor(total, result, wide(X_BANK), ALU.add).then_inc(summed, 1)
                dve.wait_ge(squared, t + 1)
                v.tensor_scalar(sums, sums, 1.0 / D, EPS, ALU.mult, ALU.add).then_inc(mean_ready, 1)
                dve.wait_ge(rooted, t + 1)
                link(v.reciprocal(sums, sums))
                v.scalar_tensor_tensor(result, total, sums, m.final_gain, ALU.mult, ALU.mult).then_inc(result_ready, 1)

        @block.sync
        def _(sp):
            for t in range(TB):
                sp.wait_ge(result_ready, t + 1)
                sp.dma_start(out[t * P:(t + 1) * P, :], result).then_inc(stored, 16)
            sp.wait_ge(stored, 16 * TB)
            core.zero_past(sp)


def second_block(core, m, a, out):
    m.fm = m.arena[:, 0:N_FM * SEQ].rearrange("p (c t) -> p c t", c=N_FM)
    m.cv = m.arena[:, 14336:14336 + 12 * SEQ].rearrange("p (c t) -> p c t", c=12)
    m.mv = m.arena[:, 20480:20480 + TB * GH * (P + 1)].rearrange("p (t h c) -> p t h c", t=TB, h=GH)
    m.gates = m.arena[:, 22544:22544 + TB * GATE_C].rearrange("p (t c) -> p t c", t=TB)
    m.rows = m.arena[0:GATE_ROWS, 23120:23120 + 6 * SEQ]
    m.select = m.rows[:, 2 * SEQ:4 * SEQ]
    m.o_tok = m.scratch.rearrange("p (t c) -> p t c", t=TB)
    m.k_tok, m.v_tok, m.kk = (m.arena[:, i * 2048:(i + 1) * 2048].rearrange("p (t c) -> p t c", t=TB) for i in range(3))
    m.qk = m.arena[:, 14336 + 8 * SEQ:14336 + 12 * SEQ].rearrange("p (t c) -> p t c", t=TB)
    m.qk_t = m.arena[:, 20 * SEQ:28 * SEQ].rearrange("p (n c) -> p n c", n=8)
    m.inverse = m.h.rearrange("p k t -> p (k t)").rearrange("p (n c) -> p n c", n=8)
    tok4 = [m.tail[:, i * 144:(i + 1) * 144].rearrange("p (t r) -> p t r", t=TB) for i in range(4)]
    m.g_tok, m.shift_tok, m.bm_tok, m.beta = tok4
    m.rate = m.tail[:, 576:577]
    m.gdn_small = m.tail[:, 580:580 + 96]
    m.anti = m.const[:, P:2 * P]
    m.block_mask = m.const[:, 2 * P:10 * P]
    m.const_2_width = 9 * P
    m.queries = m.arena[:, 0:PAIRS * SEQ].rearrange("p (n t) -> p n t", n=PAIRS)
    m.keys = m.arena[:, 8192:8192 + PAIRS * KEYS]
    m.final_gain = m.arena[:, 10240:10240 + D]
    m.picked = m.arena[:, 11264:11264 + TB * PICKS].rearrange("p (t c) -> p t c", t=TB)
    m.index = m.arena[:, 11776:11776 + TB * PICKS].bitcast(U32).rearrange("p (t c) -> p t c", t=TB)
    m.acts = m.arena[:, 12288:12288 + PICKS]
    m.iota = m.arena[:, 12416:12416 + TOP]
    m.staged = m.arena[:, 12432:12432 + 2 * RING].bitcast(U32)
    m.dots = m.arena[:, 12448:12448 + RING]
    m.choose = m.arena[:, 12800:12800 + 5760]

    second_projection(core, m, a)
    core.next_stage()
    gate_rows(core, m)
    core.next_stage()
    mlstm(core, m)
    core.next_stage()
    gated_norm(core, m, "ml_norm", FM_AT["mo"], ACT.Sigmoid, lambda h: m.gdn_small[:, 77 + h:78 + h])
    core.next_stage()
    conv_and_turn(core, m)
    core.next_stage()
    delta_inverse(core, m)
    core.next_stage()
    delta_rule(core, m)
    core.next_stage()
    gated_norm(core, m, "gdn_norm", FM_AT["gz"], ACT.Silu, lambda h: m.gdn_small[:, 76:77])
    core.next_stage()
    out_projection(core, m, a["w_out_2"])
    core.next_stage()
    expert_queries(core, m, a)
    core.next_stage()
    choose_experts(core, m)
    core.next_stage()
    experts(core, m, a, out)
    core.zero_all()


def lay_out_second(i):
    f = lambda n: np.asarray(i[n])[0] if n != "normf_g_2" else np.asarray(i[n])

    def gain(n):
        return f(n).reshape(DK, P).T

    def chunks(w, c):
        return w.reshape(DK, P, -1, c).transpose(2, 1, 0, 3).reshape(-1, P, DK * c)

    sizes = (512, 512, 512, 512, 8, 8, 512, 512, 512, 512, 8, 8)
    names = ("gq", "gk", "gv", "gz", "a", "b", "mq", "mk", "mv", "mo", "i", "f")
    ends = np.cumsum(sizes)
    w_in = f("w_in_2")
    part = {n: w_in[:, e - s:e] for n, s, e in zip(names, sizes, ends)}
    gates = np.zeros((D, GATE_C), w_in.dtype)
    small = np.zeros((P, 96), w_in.dtype)
    for kind, at_ in KINDS.items():
        for d in range(DIRS):
            gates[:, at_ * GATE_ROWS + d * BACK:][:, :GH] = part[kind][:, d * GH:(d + 1) * GH]
    for n, name in enumerate(("gdn_dt_bias_2", "gdn_a_log_2", "mlstm_i_bias_2", "mlstm_f_bias_2")):
        for d in range(DIRS):
            small[d * BACK:d * BACK + GH, n] = f(name)[d]
    small[:, 16:76] = f("conv_w_2").reshape(12, P, CONV_K).transpose(1, 0, 2).reshape(P, -1)
    small[:, 76] = f("gdn_norm_g_2")
    small[:, 77:81] = f("mlstm_norm_g_2").reshape(GH, P).T
    t = np.arange(P)
    lower = []
    lower.append((t[:, None] // 16 == t[None, :] // 16) & (t[:, None] > t[None, :]))
    for size in (16, 32, 64):
        lower.append((t[:, None] // (2 * size) == t[None, :] // (2 * size)) & (t[:, None] // size > t[None, :] // size))
    masks = [x.astype(np.float32) for x in lower] + [x.T.astype(np.float32) for x in lower]
    anti = np.where(t[None, :] >= t[:, None], 0.0, NEG).astype(np.float32)
    keys = f("peer_keys_2").reshape(PAIRS, KEYS, P).transpose(2, 0, 1).reshape(P, -1)
    out = {
        "norm1_2": gain("norm1_g_2"), "norm2_2": gain("norm2_g_2"),
        "w_in_fm_2": chunks(np.concatenate([part[n] for n in ("gq", "gk", "gv", "gz", "mo", "mq", "mk")], 1), P),
        "w_in_v_2": chunks(part["mv"], SEQ)[0],
        "w_in_gates_2": chunks(gates, GATE_C)[0],
        "const_2": np.concatenate([anti] + masks, 1),
        "gdn_small_2": small,
        "w_out_2": f("w_out_2").reshape(DK, P, D),
        "peer_wq_2": chunks(f("peer_wq_2"), P),
        "peer_keys_2": keys,
        "normf_2": np.broadcast_to(f("normf_g_2")[None, :], (P, D)),
        "iota": np.broadcast_to(np.arange(TOP, dtype=np.float32)[None, :], (P, TOP)),
        "peer_u_2": f("peer_u_2"), "peer_v_2": f("peer_v_2"),
    }
    return {n: np.ascontiguousarray(v) for n, v in out.items()}


class Memory:
    pass


def program(nc, arrays, out):
    with ExitStack() as ctx:
        core, m = Core(nc, ctx), Memory()
        allocate(core, m)
        load_start(core, m, arrays)
        first_block(core, m, arrays)
        second_block(core, m, arrays, out)


def kernel(**inputs):
    import concourse.bacc as bacc
    from concourse.bass_utils import run_bass_kernel_spmd

    arrays = lay_out_first(inputs) | lay_out_second(inputs)
    nc = bacc.Bacc("TRN2", target_bir_lowering=False, num_devices=1)
    ins = {n: nc.dram_tensor(n, v.shape, mybir.dt.from_np(v.dtype), kind="ExternalInput").ap() for n, v in arrays.items()}
    out = nc.dram_tensor("out", (SEQ, D), F32, kind="ExternalOutput").ap()
    program(nc, ins, out)
    result = run_bass_kernel_spmd(nc, [arrays], core_ids=[0])
    return result.results[0]["out"].reshape(1, SEQ, D)
```

```python
from contextlib import ExitStack

import concourse.bass as bass
import numpy as np
from concourse import mybir

F32 = mybir.dt.float32
BF16 = mybir.dt.bfloat16
F32R = mybir.dt.float32r
U32 = mybir.dt.uint32
ALU = mybir.AluOpType
ACT = mybir.ActivationFunctionType
AX = mybir.AxisListType

P = 128
SEQ = 512
TB = SEQ // P
D = 1024
DK = D // P
D_FF = 2816
EPS = 1e-6


def at(ap, i, n=1):
    return ap[i:i + n] if isinstance(i, int) else ap[bass.ds(i, n)]


def one(ap, i):
    return ap[i] if isinstance(i, int) else ap[bass.ds(i, 1)].rearrange("a p c -> (a p) c")


def column(ap, i):
    return ap[:, i, :] if isinstance(i, int) else ap[:, bass.ds(i, 1), :].rearrange("p a t -> p (a t)")


class Core:

    def __init__(self, nc, ctx):
        self.nc, self.ctx = nc, ctx
        self.taken, self.past = (ExitStack(), []), (ExitStack(), [])

    def sbuf(self, name, shape, dtype=F32):
        return self.ctx.enter_context(self.nc.sbuf_tensor(name, shape, dtype))

    def rounded_name(self, tensor):
        begin = self.nc.sbuf_base - 4 * int(np.prod(tensor.shape[1:]))
        return self.nc.alloc_sbuf_tensor_at(tensor.name + "_rounded", list(tensor.shape), F32R, offset=begin)

    def sem(self, name):
        s = self.taken[0].enter_context(self.nc.semaphore(name))
        self.taken[1].append(s)
        return s

    def zero_past(self, engine):
        for s in self.past[1]:
            engine.sem_clear(s)

    def next_stage(self):
        self.past[0].close()
        self.past, self.taken = self.taken, (ExitStack(), [])

    def zero_all(self):
        self.next_stage()
        with self.nc.Block() as block:
            @block.sync
            def _(sp):
                self.zero_past(sp)
        self.next_stage()


def chained(engine, sem):
    count = [0]

    def link(instruction):
        count[0] += 1
        instruction.then_inc(sem, 1)
        engine.wait_ge(sem, count[0])

    return link


def rounded(m, ap):
    return bass.AP(tensor=m.rounded[ap.tensor.name], offset=ap.offset, ap=ap.ap)


def parts(m, ap):
    n = ap.shape[-1] // 2
    return rounded(m, ap[:, 0:n]), rounded(m, ap[:, n:2 * n])


def split_product(nc, out, left, right, start, stop):
    nc.tensor.matmul(out, left[0], right[0], start=start, stop=False)
    nc.tensor.matmul(out, left[0], right[1], start=False, stop=False)
    return nc.tensor.matmul(out, left[1], right[0], start=False, stop=stop)


def norm_steps(core, name):
    return {k: core.sem(f"{name}_{k}") for k in ("gain_loaded", "square_ready", "square_used", "mean_ready",
                                                  "root_ready", "scaled", "hi_ready", "normed")}


def norm_scalar(nc, act, m, s, meanwhile):
    for k in range(DK):
        if k >= 2:
            act.wait_ge(s["square_used"], k - 1)
        nc.scalar.activation(m.square[:, k % 2, :], m.x[:, k, :], ACT.Square).then_inc(s["square_ready"], 1)
    meanwhile()
    act.wait_ge(s["mean_ready"], 1)
    nc.scalar.activation(m.root, m.mean, ACT.Sqrt).then_inc(s["root_ready"], 1)


def norm_tensor(nc, pe, m, s):
    for k in range(DK):
        pe.wait_ge(s["square_ready"], k + 1)
        nc.tensor.matmul(m.bank[:, 0, :], m.ones[:], m.square[:, k % 2, :], start=k == 0,
                         stop=k == DK - 1).then_inc(s["square_used"], 1)


def norm_hi(nc, act, m, s, hi):
    for k in range(DK):
        act.wait_ge(s["scaled"], k + 1)
        nc.scalar.copy(hi[:, k, :], m.h[:, k, :]).then_inc(s["hi_ready"], 1)


def norm_vector(nc, dve, m, s, gain, hi, lo, meanwhile):
    dve.wait_ge(s["square_used"], DK)
    nc.vector.tensor_scalar(m.mean, m.bank[:, 0, :], 1.0 / D, EPS, ALU.mult, ALU.add).then_inc(s["mean_ready"], 1)
    meanwhile()
    dve.wait_ge(s["root_ready"], 1)
    nc.vector.reciprocal(m.mean, m.root).then_inc(s["mean_ready"], 1)
    dve.wait_ge(s["mean_ready"], 2)
    dve.wait_ge(s["gain_loaded"], 16)
    for k in range(DK + 1):
        if k < DK:
            nc.vector.scalar_tensor_tensor(m.h[:, k, :], m.x[:, k, :], gain[:, k:k + 1], m.mean,
                                           ALU.mult, ALU.mult).then_inc(s["scaled"], 1)
        if k >= 1:
            dve.wait_ge(s["hi_ready"], k)
            nc.vector.tensor_tensor(lo[:, k - 1, :], m.h[:, k - 1, :], hi[:, k - 1, :], ALU.subtract).then_inc(s["normed"], 1)


def ffn(core, m, name, gain_dram, wi_dram, wo_dram):
    nc = core.nc
    FK = D_FF // P
    UP = 2
    DOWN = 4
    up_hi, up_lo = ([v.rearrange("p (h k c) -> p h k c", h=2, k=DK) for v in part] for part in
                    zip(*(parts(m, m.w[:, i * 4 * D:(i + 1) * 4 * D]) for i in range(UP))))
    down_hi, down_lo = zip(*(parts(m, m.w[:, i * 2 * D:(i + 1) * 2 * D]) for i in range(DOWN)))
    raw = m.w[:, UP * 4 * D:]
    up_raw = [raw[:, i * 2 * D:(i + 1) * 2 * D] for i in range(UP)]
    down_raw = [raw[:, i * D:(i + 1) * D] for i in range(DOWN)]
    hidden = m.arena[:, 0:2 * FK * SEQ]
    hidden_hi, hidden_lo = (v.rearrange("p (k t) -> p k t", k=FK) for v in parts(m, hidden))
    product = hidden[:, FK * SEQ:].rearrange("p (k t) -> p k t", k=FK)
    h_hi = rounded(m, m.arena[:, 2 * FK * SEQ:2 * FK * SEQ + DK * SEQ]).rearrange("p (k t) -> p k t", k=DK)
    h_lo = rounded(m, m.h[:])
    silu = m.square
    wi = wi_dram.rearrange("a j p c -> (a j) p c")
    wo = wo_dram.rearrange("a k p c -> (a k) p c")

    def flat(ap):
        return ap.rearrange("p h k c -> p (h k c)")

    s = norm_steps(core, name)
    up_loaded, up_hi_ready, up_ready, a_done, b_done, silu_done, product_ready, hidden_hi_ready, hidden_ready = (
        [core.sem(f"{name}_{n}{i}") for i in range(UP)] for n in (
            "up_loaded", "up_hi_ready", "up_ready", "a_done", "b_done", "silu_done", "product_ready", "hidden_hi_ready",
            "hidden_ready"))
    down_loaded, down_hi_ready, down_ready, down_used = (
        [core.sem(f"{name}_{n}{i}") for i in range(DOWN)] for n in ("down_loaded", "down_hi_ready", "down_ready", "down_used"))
    down_done = core.sem(f"{name}_down_done")
    rounds = FK // UP
    tail = range(FK - FK % DOWN, FK)

    with nc.Block() as block:

        @block.sync
        def _(sp):
            sp.dma_start(m.gain[:], gain_dram.rearrange("a p k -> (a p) k")).then_inc(s["gain_loaded"], 16)

            def load_up(r, i):
                sp.dma_start(up_raw[i], one(wi, r * UP + i)).then_inc(up_loaded[i], 16)

            def load_down(k, i):
                sp.dma_start(down_raw[i], one(wo, k)).then_inc(down_loaded[i], 16)

            for i in range(UP):
                load_up(0, i)
            with sp.Fori(1, rounds) as r:
                for i in range(UP):
                    sp.wait_ge(up_ready[i], r)
                    load_up(r, i)
            for i in range(DOWN):
                sp.wait_ge(up_ready[i * UP // DOWN], rounds)
                load_down(i, i)
            with sp.Fori(1, FK // DOWN) as r:
                for i in range(DOWN):
                    sp.wait_ge(down_ready[i], r)
                    load_down(r * DOWN + i, i)
            for k in tail:
                sp.wait_ge(down_ready[k % DOWN], k // DOWN)
                load_down(k, k % DOWN)
            core.zero_past(sp)

        @block.tensor
        def _(pe):
            norm_tensor(nc, pe, m, s)

            def up(r, i, first):
                pe.wait_ge(up_ready[i], r + 1)
                if not first:
                    pe.wait_ge(product_ready[i], r)
                for half, done in ((0, a_done[i]), (1, b_done[i])):
                    for k in range(DK):
                        if first and i == 0 and half == 0:
                            pe.wait_ge(s["normed"], k + 1)
                        last = split_product(nc, m.bank[:, 2 * i + half, :], (up_hi[i][:, half, k, :], up_lo[i][:, half, k, :]),
                                             (h_hi[:, k, :], h_lo[:, k, :]), start=k == 0, stop=k == DK - 1)
                    last.then_inc(done, 1)

            pe.wait_ge(s["mean_ready"], 1)
            for i in range(UP):
                up(0, i, True)
            with pe.Fori(1, rounds) as r:
                for i in range(UP):
                    up(r, i, False)
            for i in range(UP):
                pe.wait_ge(hidden_ready[i], rounds)

            def down(k, i, r, start=False, stop=False):
                pe.wait_ge(down_ready[i], r + 1)
                for c in range(DK):
                    part = slice(c * P, (c + 1) * P)
                    last = split_product(nc, m.bank[:, c, :], (down_hi[i][:, part], down_lo[i][:, part]),
                                         (column(hidden_hi, k), column(hidden_lo, k)), start=start, stop=stop)
                    if stop:
                        last.then_inc(down_done, 1)
                if not stop:
                    last.then_inc(down_used[i], 1)

            for k in range(DOWN):
                down(k, k, 0, start=k == 0)
            with pe.Fori(1, FK // DOWN) as r:
                for i in range(DOWN):
                    down(r * DOWN + i, i, r)
            for k in tail:
                down(k, k % DOWN, k // DOWN, stop=k == FK - 1)

        @block.scalar
        def _(act):
            def split_up(r, i, first):
                act.wait_ge(up_loaded[i], r * 16 + 16)
                if not first:
                    act.wait_ge(b_done[i], r)
                nc.scalar.copy(flat(up_hi[i]), up_raw[i]).then_inc(up_hi_ready[i], 1)

            def gate(r, i, first):
                act.wait_ge(a_done[i], r + 1)
                if not first:
                    act.wait_ge(product_ready[i], r)
                nc.scalar.activation(silu[:, i, :], m.bank[:, 2 * i, :], ACT.Silu).then_inc(silu_done[i], 1)

            def split_hidden(r, i):
                act.wait_ge(product_ready[i], r + 1)
                nc.scalar.copy(column(hidden_hi, r * UP + i), column(product, r * UP + i)).then_inc(hidden_hi_ready[i], 1)

            def split_down(r, i):
                act.wait_ge(down_loaded[i], r * 16 + 16)
                nc.scalar.copy(down_hi[i], down_raw[i]).then_inc(down_hi_ready[i], 1)

            norm_scalar(nc, act, m, s, lambda: split_up(0, 0, True))
            norm_hi(nc, act, m, s, h_hi)
            split_up(0, 1, True)
            for i in range(UP):
                gate(0, i, True)
                split_up(1, i, False)
                split_hidden(0, i)
            with act.Fori(1, rounds - 1) as r:
                for i in range(UP):
                    gate(r, i, False)
                    split_up(r + 1, i, False)
                    split_hidden(r, i)
            for i in range(UP):
                gate(rounds - 1, i, False)
                split_hidden(rounds - 1, i)
            for i in range(DOWN):
                act.wait_ge(b_done[i * UP // DOWN], rounds)
                split_down(0, i)
            with act.Fori(1, FK // DOWN) as r:
                for i in range(DOWN):
                    act.wait_ge(down_used[i], r)
                    split_down(r, i)
            for k in tail:
                act.wait_ge(down_used[k % DOWN], k // DOWN)
                split_down(k // DOWN, k % DOWN)

        @block.vector
        def _(dve):
            def split_up(r, i):
                dve.wait_ge(up_hi_ready[i], r + 1)
                nc.vector.tensor_tensor(flat(up_lo[i]), up_raw[i], flat(up_hi[i]), ALU.subtract).then_inc(up_ready[i], 1)

            def multiply(r, i):
                dve.wait_ge(silu_done[i], r + 1)
                dve.wait_ge(b_done[i], r + 1)
                nc.vector.tensor_tensor(column(product, r * UP + i), silu[:, i, :], m.bank[:, 2 * i + 1, :], ALU.mult)\
                    .then_inc(product_ready[i], 1)

            def split_hidden(r, i):
                dve.wait_ge(hidden_hi_ready[i], r + 1)
                k = r * UP + i
                nc.vector.tensor_tensor(column(hidden_lo, k), column(product, k), column(hidden_hi, k), ALU.subtract)\
                    .then_inc(hidden_ready[i], 1)

            def split_down(r, i):
                dve.wait_ge(down_hi_ready[i], r + 1)
                nc.vector.tensor_tensor(down_lo[i], down_raw[i], down_hi[i], ALU.subtract).then_inc(down_ready[i], 1)

            norm_vector(nc, dve, m, s, m.gain, h_hi, h_lo, lambda: split_up(0, 0))
            split_up(0, 1)
            with dve.Fori(0, rounds - 1) as r:
                for i in range(UP):
                    multiply(r, i)
                    split_up(r + 1, i)
                    split_hidden(r, i)
            for i in range(UP):
                multiply(rounds - 1, i)
                split_hidden(rounds - 1, i)
            for i in range(DOWN):
                split_down(0, i)
            with dve.Fori(1, FK // DOWN) as r:
                for i in range(DOWN):
                    split_down(r, i)
            for k in tail:
                split_down(k // DOWN, k % DOWN)
            for c in range(DK):
                dve.wait_ge(down_done, c + 1)
                nc.vector.scalar_tensor_tensor(m.x[:, c, :], m.bank[:, c, :], 0.5, m.x[:, c, :], ALU.mult, ALU.add)


HEADS, HD, GROUPS = 8, 64, 2
HW = HEADS * HD
Q_LORA, KV_LORA, ROPE = 256, 128, 32
QK_MLA = HD + ROPE
KV_W = GROUPS * HD
BRANCHES = 3
TOK_SIZES = dict(sb_v=HW, cq=Q_LORA, ckv=KV_LORA, kr=ROPE, nq=HW, ck=KV_W, cv=KV_W, sk=KV_W, sv=KV_W, wk=KV_W,
                 wv=KV_W, gate=BRANCHES * HEADS)
TOK_W = sum(TOK_SIZES.values())
TOK_AT = {}
for _name, _size in TOK_SIZES.items():
    TOK_AT[_name] = sum(TOK_SIZES[n] for n in TOK_AT)
TOK_STEPS = 6
TOK_C = TOK_W // TOK_STEPS
assert TOK_C * TOK_STEPS == TOK_W and TOK_C <= SEQ
CMP_LEN, CMP_STRIDE, CMP_HIDDEN = 32, 16, 128
N_CMP = (SEQ - CMP_LEN) // CMP_STRIDE + 1
NEG = -1e30


def tok(m, name):
    return m.tok[:, :, TOK_AT[name]:TOK_AT[name] + TOK_SIZES[name]]


def in_projection(core, m, gain_dram, qk_dram, tok_dram):
    nc = core.nc
    SLOTS = 2
    QK_STEPS = 2 * HW // P
    TOK_N = DK * TOK_C
    late, z = m.late, m.z
    h_hi, h_lo = (rounded(m, v[:, 0:DK * SEQ]).rearrange("p (k t) -> p k t", k=DK) for v in (late, z))
    qk_slot = [v[:, DK * SEQ:DK * SEQ + 2 * D] for v in (late, z)]
    qk_raw = [v[:, D:] for v in qk_slot]
    qk_hi, qk_lo = zip(*(parts(m, v) for v in qk_slot))
    tok_slot = [m.w[:, i * 2 * TOK_N:(i + 1) * 2 * TOK_N] for i in range(SLOTS)]
    tok_raw = [v[:, TOK_N:] for v in tok_slot]
    tok_hi, tok_lo = zip(*(parts(m, v) for v in tok_slot))
    s = norm_steps(core, "mix")
    qk_loaded, qk_hi_ready, qk_ready, qk_done, qk_copied, tok_loaded, tok_hi_ready, tok_ready, tok_done, tok_copied_act, tok_copied_dve = (
        [core.sem(f"{n}{i}") for i in range(SLOTS)] for n in (
            "qk_loaded", "qk_hi_ready", "qk_ready", "qk_done", "qk_copied", "tok_loaded", "tok_hi_ready", "tok_ready", "tok_done",
            "tok_copied_act", "tok_copied_dve"))
    qk_rounds, tok_rounds = QK_STEPS // SLOTS, TOK_STEPS // SLOTS

    with nc.Block() as block:
        @block.sync
        def _(sp):
            sp.dma_start(m.gain[:], gain_dram.rearrange("a p k -> (a p) k")).then_inc(s["gain_loaded"], 16)
            qk_in = qk_dram.rearrange("a j p c -> (a j) p c")
            tok_in = tok_dram.rearrange("a j p c -> (a j) p c")

            def load_qk(r, i):
                sp.dma_start(qk_raw[i], one(qk_in, r * SLOTS + i)).then_inc(qk_loaded[i], 16)

            def load_tok(r, i):
                sp.dma_start(tok_raw[i], one(tok_in, r * SLOTS + i)).then_inc(tok_loaded[i], 16)

            for i in range(SLOTS):
                load_qk(0, i)
            for i in range(SLOTS):
                load_tok(0, i)
            with sp.Fori(1, qk_rounds) as r:
                for i in range(SLOTS):
                    sp.wait_ge(qk_done[i], r)
                    load_qk(r, i)
            with sp.Fori(1, tok_rounds) as r:
                for i in range(SLOTS):
                    sp.wait_ge(tok_done[i], r)
                    load_tok(r, i)
            core.zero_past(sp)

        @block.tensor
        def _(pe):
            norm_tensor(nc, pe, m, s)
            pe.wait_ge(s["mean_ready"], 1)

            def qk(r, i, first):
                pe.wait_ge(qk_ready[i], r + 1)
                if not first:
                    pe.wait_ge(qk_copied[i], r)
                for k in range(DK):
                    if first and i == 0:
                        pe.wait_ge(s["normed"], k + 1)
                    part = slice(k * P, (k + 1) * P)
                    last = split_product(nc, m.bank[:, i, :], (qk_hi[i][:, part], qk_lo[i][:, part]),
                                         (h_hi[:, k, :], h_lo[:, k, :]), start=k == 0, stop=k == DK - 1)
                last.then_inc(qk_done[i], 1)

            for i in range(SLOTS):
                qk(0, i, True)
            with pe.Fori(1, qk_rounds) as r:
                for i in range(SLOTS):
                    qk(r, i, False)
            for i in range(SLOTS):
                pe.wait_ge(qk_copied[i], qk_rounds)

            def by_token(r, i, first):
                pe.wait_ge(tok_ready[i], r + 1)
                if not first:
                    pe.wait_ge(tok_copied_act[i], r)
                    pe.wait_ge(tok_copied_dve[i], r)
                for t in range(TB):
                    tokens = slice(t * P, (t + 1) * P)
                    for k in range(DK):
                        part = slice(k * TOK_C, (k + 1) * TOK_C)
                        last = split_product(nc, m.bank[:, i * TB + t, 0:TOK_C], (h_hi[:, k, tokens], h_lo[:, k, tokens]),
                                             (tok_hi[i][:, part], tok_lo[i][:, part]), start=k == 0, stop=k == DK - 1)
                last.then_inc(tok_done[i], 1)

            for i in range(SLOTS):
                by_token(0, i, True)
            with pe.Fori(1, tok_rounds) as r:
                for i in range(SLOTS):
                    by_token(r, i, False)

        def tok_out(r, i, t):
            return m.tok[:, t, bass.ds((r * SLOTS + i) * TOK_C, TOK_C)]

        @block.scalar
        def _(act):
            def split_qk(r, i):
                act.wait_ge(qk_loaded[i], r * 16 + 16)
                nc.scalar.copy(qk_hi[i], qk_raw[i]).then_inc(qk_hi_ready[i], 1)

            def split_tok(r, i):
                act.wait_ge(tok_loaded[i], r * 16 + 16)
                nc.scalar.copy(tok_hi[i], tok_raw[i]).then_inc(tok_hi_ready[i], 1)

            def qk_out(r, i):
                act.wait_ge(qk_done[i], r + 1)
                nc.scalar.copy(column(m.sbqk, r * SLOTS + i), m.bank[:, i, :]).then_inc(qk_copied[i], 1)

            def tok_copy(r, i):
                act.wait_ge(tok_done[i], r + 1)
                for t in (0, 1):
                    last = nc.scalar.copy(tok_out(r, i, t), m.bank[:, i * TB + t, 0:TOK_C])
                last.then_inc(tok_copied_act[i], 1)

            norm_scalar(nc, act, m, s, lambda: split_qk(0, 0))
            norm_hi(nc, act, m, s, h_hi)
            split_qk(0, 1)
            for i in range(SLOTS):
                split_tok(0, i)
            with act.Fori(0, qk_rounds - 1) as r:
                for i in range(SLOTS):
                    qk_out(r, i)
                    split_qk(r + 1, i)
            for i in range(SLOTS):
                qk_out(qk_rounds - 1, i)
            with act.Fori(0, tok_rounds - 1) as r:
                for i in range(SLOTS):
                    tok_copy(r, i)
                    split_tok(r + 1, i)
            for i in range(SLOTS):
                tok_copy(tok_rounds - 1, i)

        @block.vector
        def _(dve):
            def split_qk(r, i):
                dve.wait_ge(qk_hi_ready[i], r + 1)
                nc.vector.tensor_tensor(qk_lo[i], qk_raw[i], qk_hi[i], ALU.subtract).then_inc(qk_ready[i], 1)

            def split_tok(r, i):
                dve.wait_ge(tok_hi_ready[i], r + 1)
                nc.vector.tensor_tensor(tok_lo[i], tok_raw[i], tok_hi[i], ALU.subtract).then_inc(tok_ready[i], 1)

            def tok_copy(r, i):
                dve.wait_ge(tok_done[i], r + 1)
                for t in (2, 3):
                    last = nc.vector.tensor_copy(tok_out(r, i, t), m.bank[:, i * TB + t, 0:TOK_C])
                last.then_inc(tok_copied_dve[i], 1)

            norm_vector(nc, dve, m, s, m.gain, h_hi, h_lo, lambda: split_qk(0, 0))
            split_qk(0, 1)
            for i in range(SLOTS):
                split_tok(0, i)
            with dve.Fori(1, qk_rounds) as r:
                for i in range(SLOTS):
                    split_qk(r, i)
            with dve.Fori(0, tok_rounds - 1) as r:
                for i in range(SLOTS):
                    tok_copy(r, i)
                    split_tok(r + 1, i)
            for i in range(SLOTS):
                tok_copy(tok_rounds - 1, i)


def swapped(ap, heads, width):
    return ap.rearrange("p h (two c) -> p h two c", two=2)[:, :, ::-1, :]


def spread(ap, heads):
    return ap.rearrange("p (one c) -> p one c", one=1).broadcast_to([ap.shape[0], heads, ap.shape[1]])


def per_head(ap, width):
    return ap.rearrange("p (h one) -> p h one", one=1).broadcast_to([ap.shape[0], ap.shape[1], width])


def mla_prepare(core, m, uq_dram, ukv_dram, norm_dram, gain_dram):
    nc = core.nc
    NQ, NKV = HEADS * QK_MLA, HEADS * 2 * HD
    w_uq = m.w[:, 8192:8192 + 2 * NQ].rearrange("p (k c) -> p k c", k=2)
    w_ukv = m.w[:, 8192 + 2 * NQ:8192 + 2 * NQ + NKV]
    latent = m.z[:, 4096:4096 + 1536].rearrange("p (t c) -> p t c", t=TB)
    latent_t = m.late[:, 0:1536].rearrange("p (k t) -> p k t", k=3)
    places = (m.z[:, 4096:4096 + 2 * NQ], m.late[:, 1536:1536 + 2 * NQ])
    q_tok, k_tok = ([place[:, i * NQ:(i + 1) * NQ] for place in places] for i in range(2))
    key_scales = [m.small[:, 240 + 8 * i:248 + 8 * i] for i in range(2)]
    turn = m.z[:, 7168 - 1024:7168 - 1024 + 4 * HEADS * ROPE].rearrange("p (n h c) -> p n h c", n=4, h=HEADS)
    squares = m.square.rearrange("p a b -> p (a b)")
    sums = m.small[:, 0:8]
    head_sums = m.small[:, 8:24]
    gains = m.small[:, 24:27]
    head_gain = m.small[:, 32:32 + 2 * QK_MLA]
    loaded, weights_loaded = core.sem("mla_gains_loaded"), core.sem("mla_weights_loaded")
    squared, root_in, rooted = core.sem("mla_squared"), core.sem("mla_root_in"), core.sem("mla_rooted")
    latent_ready, turned, latent_copied = (core.sem(f"mla_latent_{n}") for n in ("ready", "turned", "copied"))
    up_done, up_copied = core.sem("mla_up_done"), core.sem("mla_up_copied")
    key_ready, key_scale = core.sem("mla_key_ready"), core.sem("mla_key_scale")
    q_ready, k_ready = core.sem("mla_q_ready"), core.sem("mla_k_ready")
    heads_turned, heads_copied = core.sem("mla_heads_turned"), core.sem("mla_heads_copied")
    dve_chain, pool_chain = core.sem("mla_dve_chain"), core.sem("mla_pool_chain")
    cq_ckv = m.tok[:, :, TOK_AT["cq"]:TOK_AT["cq"] + Q_LORA + KV_LORA]

    with nc.Block() as block:
        @block.sync
        def _(sp):
            sp.dma_start(gains, norm_dram.rearrange("a p c -> (a p) c")).then_inc(loaded, 16)
            sp.dma_start(head_gain, gain_dram.rearrange("a p c -> (a p) c")).then_inc(loaded, 16)
            sp.dma_start(m.w[:, 8192:8192 + 2 * NQ], uq_dram.rearrange("a p c -> (a p) c")).then_inc(weights_loaded, 16)
            sp.dma_start(w_ukv, ukv_dram.rearrange("a p c -> (a p) c")).then_inc(weights_loaded, 16)
            core.zero_past(sp)

        @block.scalar
        def _(act):
            for t in range(TB):
                nc.scalar.activation(m.scratch[:, t * 384:t * 384 + Q_LORA], cq_ckv[:, t, 0:Q_LORA], ACT.Square,
                                     accum_out=sums[:, t:t + 1])
                last = nc.scalar.activation(m.scratch[:, t * 384 + Q_LORA:(t + 1) * 384], cq_ckv[:, t, Q_LORA:], ACT.Square,
                                            accum_out=sums[:, TB + t:TB + t + 1])
            last.then_inc(squared, 1)
            act.wait_ge(root_in, 1)
            nc.scalar.activation(sums, sums, ACT.Sqrt).then_inc(rooted, 1)
            act.wait_ge(loaded, 32)
            for c in range(3):
                act.wait_ge(turned, c + 1)
                nc.scalar.activation(latent_t[:, c, :], m.bank[:, c, :], ACT.Copy, scale=gains[:, c:c + 1])\
                    .then_inc(latent_copied, 1)

            def copy_heads(t):
                for i, to in enumerate((m.mla_q, m.mla_q, m.mla_k, m.mla_k)):
                    act.wait_ge(heads_turned, 4 * t + i + 1)
                    h0 = (i % 2) * 4
                    nc.scalar.copy(to[:, h0:h0 + 4, t * P:(t + 1) * P],
                                   m.bank[0:QK_MLA, 4 + i, :].rearrange("p (h t) -> p h t", h=4))\
                        .then_inc(heads_copied, 1)

            for t in range(TB):
                act.wait_ge(up_done, t + 1)
                if t >= 2:
                    act.wait_ge(heads_turned, 4 * (t - 1))
                for i in range(2):
                    nc.scalar.copy(q_tok[t % 2][:, i * 384:(i + 1) * 384], m.bank[:, i, 0:384])
                    last = nc.scalar.copy(m.mla_kv[:, t, i * 512:(i + 1) * 512], m.bank[:, 2 + i, :])
                last.then_inc(up_copied, 1)
                if t >= 1:
                    copy_heads(t - 1)
                act.wait_ge(root_in, t + 2)
                nc.scalar.activation(head_sums, head_sums, ACT.Sqrt).then_inc(rooted, 1)
            copy_heads(TB - 1)

        @block.tensor
        def _(pe):
            pe.wait_ge(latent_ready, 1)
            for c in range(3):
                for t in range(TB):
                    last = nc.tensor.transpose(m.bank[:, c, t * P:(t + 1) * P], latent[:, t, c * P:(c + 1) * P],
                                               m.ident[:])
                last.then_inc(turned, 1)
            pe.wait_ge(weights_loaded, 32)
            pe.wait_ge(latent_copied, 3)

            def up(t):
                if t >= 1:
                    pe.wait_ge(up_copied, t)
                tokens = slice(t * P, (t + 1) * P)
                for i in range(2):
                    for k in range(2):
                        nc.tensor.matmul(m.bank[:, i, 0:384], latent_t[:, k, tokens], w_uq[:, k, i * 384:(i + 1) * 384],
                                         start=k == 0, stop=k == 1)
                for i in range(2):
                    last = nc.tensor.matmul(m.bank[:, 2 + i, :], latent_t[:, 2, tokens], w_ukv[:, i * 512:(i + 1) * 512],
                                            start=True, stop=True)
                last.then_inc(up_done, 1)

            up(0)
            for t in range(TB):
                if t + 1 < TB:
                    up(t + 1)
                q, k = (q_tok[t % 2], q_ready), (k_tok[t % 2], k_ready)
                for i, (src, ready) in enumerate((q, q, k, k)):
                    pe.wait_ge(ready, t + 1)
                    if t >= 1:
                        pe.wait_ge(heads_copied, 4 * (t - 1) + i + 1)
                    for j in range(4):
                        h = (i % 2) * 4 + j
                        last = nc.tensor.transpose(m.bank[0:QK_MLA, 4 + i, j * P:(j + 1) * P],
                                                   src[:, h * QK_MLA:(h + 1) * QK_MLA], m.ident[:])
                    last.then_inc(heads_turned, 1)

        def rotate(eng, link, heads, t, tmp):
            x = heads[:, :, HD:QK_MLA]
            link(eng.tensor_tensor(tmp[:, 0], x, spread(m.mla_cos[:, t, :], HEADS), ALU.mult))
            link(eng.tensor_tensor(tmp[:, 1].rearrange("p h (two c) -> p h two c", two=2), swapped(x, HEADS, ROPE),
                                   spread(m.mla_sin[:, t, :], HEADS).rearrange("p h (two c) -> p h two c", two=2),
                                   ALU.mult))
            return eng.tensor_tensor(x, tmp[:, 0], tmp[:, 1], ALU.add)

        @block.vector
        def _(dve):
            link = chained(dve, dve_chain)
            dve.wait_ge(squared, 1)
            link(nc.vector.tensor_scalar(sums[:, 0:TB], sums[:, 0:TB], 1.0 / Q_LORA, EPS, ALU.mult, ALU.add))
            nc.vector.tensor_scalar(sums[:, TB:], sums[:, TB:], 1.0 / KV_LORA, EPS, ALU.mult, ALU.add).then_inc(root_in, 1)
            dve.wait_ge(rooted, 1)
            link(nc.vector.reciprocal(sums, sums))
            for t in range(TB):
                nc.vector.tensor_scalar(latent[:, t, 0:Q_LORA], cq_ckv[:, t, 0:Q_LORA], sums[:, t:t + 1], None, ALU.mult)
                last = nc.vector.tensor_scalar(latent[:, t, Q_LORA:], cq_ckv[:, t, Q_LORA:], sums[:, TB + t:TB + t + 1],
                                               None, ALU.mult)
            last.then_inc(latent_ready, 1)
            dve.wait_ge(loaded, 32)
            sq = squares[:, 0:NQ]
            for t in range(TB):
                dve.wait_ge(up_copied, t + 1)
                if t >= 2:
                    dve.wait_ge(heads_turned, 4 * (t - 1))
                q, k = (x[t % 2].rearrange("p (h c) -> p h c", h=HEADS) for x in (q_tok, k_tok))
                nc.vector.tensor_copy(k[:, :, 0:HD], m.mla_kv[:, t, :].rearrange("p (h c) -> p h c", h=HEADS)[:, :, 0:HD])
                link(nc.vector.tensor_copy(k[:, :, HD:QK_MLA], spread(tok(m, "kr")[:, t, :], HEADS)))
                link(nc.vector.tensor_tensor(sq, k_tok[t % 2], k_tok[t % 2], ALU.mult))
                link(nc.vector.tensor_reduce(head_sums[:, 8:16], sq.rearrange("p (h c) -> p h c", h=HEADS), AX.X, ALU.add))
                link(nc.vector.tensor_tensor(sq, q_tok[t % 2], q_tok[t % 2], ALU.mult))
                link(nc.vector.tensor_reduce(head_sums[:, 0:8], sq.rearrange("p (h c) -> p h c", h=HEADS), AX.X, ALU.add))
                nc.vector.tensor_scalar(head_sums, head_sums, 1.0 / QK_MLA, EPS, ALU.mult, ALU.add).then_inc(root_in, 1)
                dve.wait_ge(rooted, t + 2)
                link(nc.vector.reciprocal(head_sums, head_sums))
                nc.vector.tensor_copy(key_scales[t % 2], head_sums[:, 8:16]).then_inc(key_scale, 1)
                link(nc.vector.tensor_scalar(head_sums[:, 0:8], head_sums[:, 0:8], QK_MLA ** -0.5, None, ALU.mult))
                link(nc.vector.tensor_tensor(q, q, per_head(head_sums[:, 0:8], QK_MLA), ALU.mult))
                link(nc.vector.tensor_tensor(q, q, spread(head_gain[:, 0:QK_MLA], HEADS), ALU.mult))
                rotate(nc.vector, link, q, t, turn[:, 0:2]).then_inc(q_ready, 1)
                dve.wait_ge(q_ready, t + 1)

        @block.gpsimd
        def _(pool):
            link = chained(pool, pool_chain)
            pool.wait_ge(loaded, 32)
            for t in range(TB):
                k = k_tok[t % 2].rearrange("p (h c) -> p h c", h=HEADS)
                pool.wait_ge(key_scale, t + 1)
                link(nc.gpsimd.tensor_tensor(k, k, per_head(key_scales[t % 2], QK_MLA), ALU.mult))
                link(nc.gpsimd.tensor_tensor(k, k, spread(head_gain[:, QK_MLA:], HEADS), ALU.mult))
                rotate(nc.gpsimd, link, k, t, turn[:, 2:4]).then_inc(k_ready, 1)
                pool.wait_ge(k_ready, t + 1)


def attention(core, m, name, q_of, k_of, v_of, mask, kept, stick=False, gate=None, add=False, out=None):
    nc = core.nc
    UNITS = TB * HEADS
    RING = 3
    TURN, PRODUCT = 2, 4
    COPY, BACK, FINISH = PRODUCT, PRODUCT + 1, PRODUCT + 2
    TURN_OUT, COPY_OUT = FINISH + 2, FINISH + 3
    SBANK, TBANK, OBANK, QBANK = 0, 3, 5, 7
    probs, turned_p = m.probs, m.turned_p
    score_done, max_done, exp_done = (core.sem(f"{name}_{n}") for n in ("score_done", "max_done", "exp_done"))
    p_turned, p_copied, pv_done = (core.sem(f"{name}_{n}") for n in ("p_turned", "p_copied", "pv_done"))
    o_ready, o_turned, o_copied = (core.sem(f"{name}_{n}") for n in ("o_ready", "o_turned", "o_copied"))
    o_kept, o_back = core.sem(f"{name}_o_kept"), core.sem(f"{name}_o_back")
    broken, chain = core.sem(f"{name}_broken"), core.sem(f"{name}_chain")

    def unit(n):
        return n // HEADS, n % HEADS, (n // HEADS + 1) * P

    with nc.Block() as block:
        @block.sync
        def _(sp):
            core.zero_past(sp)

        @block.tensor
        def _(pe):
            def score(n):
                b, h, keys = unit(n)
                if n >= RING:
                    pe.wait_ge(exp_done, n - RING + 1)
                bank = m.bank[:, SBANK + n % RING, 0:keys]
                nc.tensor.matmul(bank, q_of(h, b), k_of(h, keys), start=True, stop=False)
                nc.tensor.matmul(bank[:, b * P:keys], m.ident_bf[:], mask[:], start=False, stop=True)\
                    .then_inc(score_done, 1)

            def turn(n):
                b, h, keys = unit(n)
                pe.wait_ge(broken if stick else exp_done, n + 1)
                if n >= 2:
                    pe.wait_ge(p_copied, n - 1)
                for kb in range(b + 1):
                    last = nc.tensor.transpose(m.bank[:, TBANK + n % 2, kb * P:(kb + 1) * P],
                                               probs[:, n % RING, kb * P:(kb + 1) * P], m.ident[:])
                last.then_inc(p_turned, 1)

            def product(n):
                b, h, keys = unit(n)
                pe.wait_ge(p_copied, n + 1)
                if h == 0 and b >= 2:
                    pe.wait_ge(o_kept if out is None else o_copied, b - 1)
                for kb in range(b + 1):
                    last = nc.tensor.matmul(m.bank[pair_half(h), OBANK + b % 2, h // 2 * P:(h // 2 + 1) * P], v_of(h, kb),
                                            turned_p[:, n % RING, kb * P:(kb + 1) * P], start=kb == 0, stop=kb == b)
                last.then_inc(pv_done, 1)

            def turn_back(b):
                pe.wait_ge(o_kept, b + 1)
                if b >= 1:
                    pe.wait_ge(o_ready, b)
                for c in range(HW // P):
                    last = nc.tensor.transpose(m.bank[:, QBANK, c * P:(c + 1) * P], kept[:, c * P:(c + 1) * P], m.ident[:])
                last.then_inc(o_back, 1)

            def turn_out(b):
                pe.wait_ge(o_ready, b + 1)
                for c in range(HW // P):
                    last = nc.tensor.transpose(m.bank[:, OBANK + b % 2, c * P:(c + 1) * P], m.otok[:, b, c * P:(c + 1) * P],
                                               m.ident[:])
                last.then_inc(o_turned, 1)

            for n in range(UNITS + TURN_OUT + 1):
                if n < UNITS:
                    score(n)
                if 0 <= n - TURN < UNITS:
                    turn(n - TURN)
                if 0 <= n - PRODUCT < UNITS:
                    product(n - PRODUCT)
                b, late = divmod(n - BACK, HEADS)
                if late == 0 and 1 <= b <= TB:
                    turn_back(b - 1)
                b, late = divmod(n - TURN_OUT, HEADS)
                if out is not None and late == 0 and 1 <= b <= TB:
                    turn_out(b - 1)

        @block.scalar
        def _(act):
            def keep(b):
                act.wait_ge(pv_done, (b + 1) * HEADS)
                if b >= 1:
                    act.wait_ge(o_back, b)
                nc.scalar.copy(kept, m.bank[:, OBANK + b % 2, :]).then_inc(o_kept, 1)

            def copy_out(b):
                act.wait_ge(o_turned, b + 1)
                nc.scalar.copy(out[:, :, b * P:(b + 1) * P], m.bank[:, OBANK + b % 2, :].rearrange("p (c t) -> p c t", c=HW // P))\
                    .then_inc(o_copied, 1)

            for n in range(UNITS + COPY_OUT + 1):
                if n < UNITS:
                    b, h, keys = unit(n)
                    bank = m.bank[:, SBANK + n % RING, 0:keys]
                    if stick:
                        act.wait_ge(score_done, n + 1)
                        if n >= RING:
                            act.wait_ge(broken, n - RING + 1)
                        nc.scalar.activation(m.odds[:, n % RING, 0:keys], bank, ACT.Sigmoid, scale=HD ** -0.5)
                        nc.scalar.activation(m.rest[:, n % RING, 0:keys], bank, ACT.Sigmoid, scale=-HD ** -0.5)\
                            .then_inc(exp_done, 1)
                    else:
                        act.wait_ge(max_done, n + 1)
                        if n >= RING:
                            act.wait_ge(p_turned, n - RING + 1)
                        nc.scalar.activation(probs[:, n % RING, 0:keys], bank, ACT.Exp, bias=m.neg_max[:, n % RING:n % RING + 1],
                                             accum_out=m.sums[:, b, h:h + 1]).then_inc(exp_done, 1)
                b, late = divmod(n - COPY, HEADS)
                if late == 0 and 1 <= b <= TB:
                    keep(b - 1)
                b, late = divmod(n - COPY_OUT, HEADS)
                if out is not None and late == 0 and 1 <= b <= TB:
                    copy_out(b - 1)

        @block.vector
        def _(dve):
            link = chained(dve, chain)

            def copy_turned(n):
                b, h, keys = unit(n)
                dve.wait_ge(p_turned, n + 1)
                if n >= RING:
                    dve.wait_ge(pv_done, n - RING + 1)
                nc.vector.tensor_copy(turned_p[:, n % RING, 0:keys], m.bank[:, TBANK + n % 2, 0:keys]).then_inc(p_copied, 1)

            def finish(b):
                dve.wait_ge(o_back, b + 1)
                o = m.bank[:, QBANK, :].rearrange("p (h c) -> p h c", h=HEADS)
                to = m.otok[:, b, :].rearrange("p (h c) -> p h c", h=HEADS)
                if stick:
                    nc.vector.tensor_copy(to, o).then_inc(o_ready, 1)
                    return
                factor = m.sums[:, b, :]
                link(nc.vector.reciprocal(factor, factor))
                if gate is not None:
                    link(nc.vector.tensor_tensor(factor, factor, gate(b), ALU.mult))
                if not add:
                    nc.vector.tensor_tensor(to, o, per_head(factor, HD), ALU.mult).then_inc(o_ready, 1)
                    return
                part = m.part.rearrange("p (h c) -> p h c", h=HEADS)
                link(nc.vector.tensor_tensor(part, o, per_head(factor, HD), ALU.mult))
                nc.vector.tensor_tensor(to, to, part, ALU.add).then_inc(o_ready, 1)
                dve.wait_ge(o_ready, b + 1)

            if stick:
                link(nc.vector.memset(m.ones_row[:], 1.0))
                link(nc.vector.memset(m.left.rearrange("p n k -> p (n k)"), 1.0))
            for n in range(UNITS + FINISH + 1):
                if n < UNITS:
                    b, h, keys = unit(n)
                    slot = n % RING
                    if stick:
                        dve.wait_ge(exp_done, n + 1)
                        if n >= RING:
                            dve.wait_ge(broken, n - RING + 1)
                        nc.vector.tensor_tensor_scan(m.left[:, slot, 0:keys][:, ::-1], m.rest[:, slot, 0:keys][:, ::-1],
                                                     m.ones_row[:, 0:keys], 1.0, ALU.mult, ALU.mult).then_inc(max_done, 1)
                    else:
                        dve.wait_ge(score_done, n + 1)
                        if n >= RING:
                            dve.wait_ge(exp_done, n - RING + 1)
                        nc.vector.tensor_reduce(m.neg_max[:, slot:slot + 1], m.bank[:, SBANK + slot, 0:keys], AX.X, ALU.max,
                                                negate=True).then_inc(max_done, 1)
                if 0 <= n - TURN < UNITS:
                    copy_turned(n - TURN)
                b, late = divmod(n - FINISH, HEADS)
                if late == 0 and 1 <= b <= TB:
                    finish(b - 1)

        if stick:
            @block.gpsimd
            def _(pool):
                for n in range(UNITS):
                    b, h, keys = unit(n)
                    slot = n % RING
                    pool.wait_ge(max_done, n + 1)
                    if n >= RING:
                        pool.wait_ge(p_turned, n - RING + 1)
                    nc.gpsimd.tensor_tensor(probs[:, slot, 0:keys], m.odds[:, slot, 0:keys], m.left[:, slot, 1:keys + 1],
                                            ALU.mult).then_inc(broken, 1)


def constants():
    def angles(width, positions):
        half = width // 2
        inv = np.exp(np.float32(-np.log(10000.0)) * np.arange(half, dtype=np.float32) * np.float32(2.0 / width))
        ang = positions.astype(np.float32)[:, None] * inv.astype(np.float32)[None, :]
        c, s = np.cos(ang), np.sin(ang)
        return np.concatenate([c, c], 1), np.concatenate([-s, s], 1)

    def by_block(table):
        return table.reshape(TB, P, -1).transpose(1, 0, 2).reshape(P, -1)

    def rows(table):
        out = np.zeros((P, table.shape[1]), np.float32)
        out[:len(table)] = table
        return out

    pos = np.arange(SEQ)
    ends = np.arange(N_CMP) * CMP_STRIDE + CMP_LEN - 1
    i = np.arange(P)
    (mla_cos, mla_sin), (nsa_cos, nsa_sin), (end_cos, end_sin) = angles(ROPE, pos), angles(HD, pos), angles(HD, ends)
    seen = ends[None, :] <= pos[:, None]
    return {
        "ident": np.eye(P),
        "causal": np.where(i[None, :] <= i[:, None], 0.0, NEG),
        "strict": np.where(i[None, :] < i[:, None], 0.0, NEG),
        "mla_cos": by_block(mla_cos), "mla_sin": by_block(mla_sin),
        "nsa_cos": by_block(nsa_cos), "nsa_sin": by_block(nsa_sin),
        "end_cos": rows(end_cos), "end_sin": rows(end_sin),
        "cmp_fill": by_block(np.where(seen, 0.0, NEG)), "cmp_seen": by_block(seen.astype(np.float32)),
    }


def const_array():
    return np.concatenate([np.asarray(v, np.float32) for v in constants().values()], axis=1)


def const_places():
    places, n = {}, 0
    for name, table in constants().items():
        places[name] = (n, n + table.shape[1])
        n += table.shape[1]
    return places, n


def nsa_prepare(core, m, w1_dram, small_dram, gain_dram):
    nc = core.nc
    PAIR = CMP_LEN // 2
    HID = PAIR * CMP_HIDDEN
    w1 = m.w[:, 0:2 * HID].rearrange("p (kv l h) -> p kv l h", kv=2, l=PAIR)
    NH = HEADS + 2 * GROUPS
    KH = 2 * GROUPS
    q_tok = m.z[:, 0:HW]
    k_tok = m.z[:, 512:512 + KH * HD]
    k_twice = m.z[:, 768:768 + 2 * KH * HD]
    turn_q = m.z[:, 1280:1280 + 2 * HW].rearrange("p (n h c) -> p n h c", n=2, h=HEADS)
    turn_k = m.z[:, 2304:2304 + 2 * KH * HD].rearrange("p (n h c) -> p n h c", n=2, h=KH)
    windows = m.z[:, 2816:2816 + 2 * GROUPS * N_CMP * PAIR].rearrange("p (kv l g n) -> p kv l g n", kv=2, g=GROUPS, l=PAIR)
    hidden = m.z[:, 4800:4800 + 4 * N_CMP].rearrange("p (g n) -> p g n", g=4)
    kc_tok = m.z[0:N_CMP, 4928:4928 + 128].rearrange("p (h c) -> p h c", h=GROUPS)
    kc_turn = m.z[0:N_CMP, 5056:5056 + 256].rearrange("p (n h c) -> p n h c", n=2, h=GROUPS)
    kc_twice = m.z[0:N_CMP, 5312:5312 + 256]
    cmp_twice = [x.rearrange("p (t g c) -> p t g c", t=TB, g=GROUPS) for x in (m.scratch[:, 1024:2048], m.z[:, 5568:6592])]
    squares = m.square.rearrange("p a b -> p (a b)")
    sums = m.small[:, 0:TB * NH].rearrange("p (t h) -> p t h", t=TB)
    kc_sums = m.small[0:N_CMP, TB * NH:TB * NH + GROUPS]
    gains = m.nsa_small[:, 0:2 * HD]
    place = m.nsa_small[:, 2 * HD:2 * HD + 2 * CMP_LEN].rearrange("p (kv l) -> p kv l", kv=2)
    w2 = m.nsa_small[:, 192:192 + 2 * HD].rearrange("p (kv c) -> p kv c", kv=2)

    w1_loaded, small_loaded = core.sem("nsa_w1_loaded"), core.sem("nsa_small_loaded")
    squared, summed, mean_ready, rooted, scales_ready = (
        core.sem(f"nsa_{n}") for n in ("squared", "summed", "mean_ready", "rooted", "scales_ready"))
    q_ready, k_ready, turned, copied = (core.sem(f"nsa_{n}") for n in ("q_ready", "k_ready", "turned", "copied"))
    cmp_turned, windows_ready, hidden_done, hidden_ready, cmp_done = (
        core.sem(f"nsa_cmp_{n}") for n in ("turned", "windows_ready", "hidden_done", "hidden_ready", "done"))
    vc_copied, kc_ready, kc_turned, kc_squared, kc_rooted = (
        core.sem(f"nsa_{n}") for n in ("vc_copied", "kc_ready", "kc_turned", "kc_squared", "kc_rooted"))
    gates_ready, cmp_copied = core.sem("nsa_gates_ready"), core.sem("nsa_cmp_copied")
    dve_chain, pool_chain = core.sem("nsa_dve_chain"), core.sem("nsa_pool_chain")

    with nc.Block() as block:
        @block.sync
        def _(sp):
            sp.dma_start(m.nsa_small[:], small_dram.rearrange("a p c -> (a p) c")).then_inc(small_loaded, 16)
            sp.dma_start(m.w[:, 0:2 * HID], w1_dram.rearrange("a p c -> (a p) c")).then_inc(w1_loaded, 16)
            core.zero_past(sp)

        @block.scalar
        def _(act):
            for t in range(TB):
                if t >= 1:
                    act.wait_ge(summed, t)
                nc.scalar.activation(squares[:, 0:HW], tok(m, "nq")[:, t, :], ACT.Square)
                nc.scalar.activation(squares[:, HW:HW + KV_W], tok(m, "sk")[:, t, :], ACT.Square)
                nc.scalar.activation(squares[:, HW + KV_W:HW + 2 * KV_W], tok(m, "wk")[:, t, :], ACT.Square)\
                    .then_inc(squared, 1)
            act.wait_ge(mean_ready, 1)
            nc.scalar.activation(sums, sums, ACT.Sqrt).then_inc(rooted, 1)
            nc.scalar.activation(tok(m, "gate"), tok(m, "gate"), ACT.Sigmoid).then_inc(gates_ready, 1)
            act.wait_ge(hidden_done, 1)
            nc.scalar.activation(hidden, m.bank[:, 3, 0:4 * N_CMP].rearrange("p (g n) -> p g n", g=4), ACT.Gelu_apprx_tanh)\
                .then_inc(hidden_ready, 1)
            act.wait_ge(cmp_done, 1)
            nc.scalar.copy(m.v_cmp, m.bank[0:N_CMP, 4, 2 * HD:4 * HD].rearrange("p (g c) -> p g c", g=GROUPS))\
                .then_inc(vc_copied, 1)
            for t in range(TB):
                act.wait_ge(turned, 2 * t + 1)
                tokens = slice(t * P, (t + 1) * P)
                nc.scalar.copy(m.nsa_q[:, :, tokens], m.bank[:, 2 * (t % 2), :].rearrange("p (c t) -> p c t", c=4))\
                    .then_inc(copied, 1)
                act.wait_ge(turned, 2 * t + 2)
                nc.scalar.copy(m.nsa_k[:, :, tokens], m.bank[:, 2 * (t % 2) + 1, :].rearrange("p (c t) -> p c t", c=4))\
                    .then_inc(copied, 1)
            act.wait_ge(kc_squared, 1)
            nc.scalar.activation(kc_sums, kc_sums, ACT.Sqrt).then_inc(kc_rooted, 1)
            act.wait_ge(kc_turned, 1)
            nc.scalar.copy(m.k_cmp, m.bank[:, 5, 0:GROUPS * N_CMP].rearrange("p (g n) -> p g n", g=GROUPS))

        @block.tensor
        def _(pe):
            for i in range(2):
                pe.wait_ge(cmp_copied, i + 1)
                for g in range(GROUPS):
                    for t in range(TB):
                        last = nc.tensor.transpose(m.bank[:, 4 + 2 * i + g, t * P:(t + 1) * P], cmp_twice[i][:, t, g], m.ident[:])
            last.then_inc(cmp_turned, 1)
            pe.wait_ge(w1_loaded, 16)
            pe.wait_ge(windows_ready, 8)
            for kv in range(2):
                to = m.bank[:, 3, kv * GROUPS * N_CMP:(kv + 1) * GROUPS * N_CMP]
                for l in range(PAIR):
                    last = nc.tensor.matmul(to, w1[:, kv, l, :], windows[:, kv, l].rearrange("p g n -> p (g n)"), start=l == 0,
                                            stop=l == PAIR - 1)
            last.then_inc(hidden_done, 1)
            pe.wait_ge(hidden_ready, 1)
            for kv in range(2):
                for g in range(GROUPS):
                    last = nc.tensor.matmul(m.bank[0:N_CMP, 4, (kv * 2 + g) * HD:(kv * 2 + g + 1) * HD],
                                            hidden[:, 2 * kv + g, :], w2[:, kv, :], start=True, stop=True)
            last.then_inc(cmp_done, 1)
            for t in range(TB):
                pe.wait_ge(q_ready, t + 1)
                if t >= 2:
                    pe.wait_ge(copied, 2 * (t - 1))
                for c in range(4):
                    last = nc.tensor.transpose(m.bank[:, 2 * (t % 2), c * P:(c + 1) * P], q_tok[:, c * P:(c + 1) * P],
                                               m.ident[:])
                last.then_inc(turned, 1)
                pe.wait_ge(k_ready, t + 1)
                for c in range(4):
                    last = nc.tensor.transpose(m.bank[:, 2 * (t % 2) + 1, c * P:(c + 1) * P], k_twice[:, c * P:(c + 1) * P],
                                               m.ident[:])
                last.then_inc(turned, 1)
            pe.wait_ge(kc_ready, 1)
            for g in range(GROUPS):
                last = nc.tensor.transpose(m.bank[:, 5, g * N_CMP:(g + 1) * N_CMP], kc_twice[:, g * P:(g + 1) * P],
                                           m.ident[0:N_CMP, 0:N_CMP])
            last.then_inc(kc_turned, 1)

        def rotate(eng, link, x, cos, sin, tmp, heads):
            link(eng.tensor_tensor(tmp[:, 0], x, spread(cos, heads), ALU.mult))
            link(eng.tensor_tensor(tmp[:, 1].rearrange("p h (two c) -> p h two c", two=2), swapped(x, heads, HD),
                                   spread(sin, heads).rearrange("p h (two c) -> p h two c", two=2), ALU.mult))

        @block.vector
        def _(dve):
            link = chained(dve, dve_chain)
            for t in range(TB):
                dve.wait_ge(squared, t + 1)
                nc.vector.tensor_reduce(sums[:, t, :], squares[:, 0:NH * HD].rearrange("p (h c) -> p h c", h=NH), AX.X,
                                        ALU.add).then_inc(summed, 1)
            dve.wait_ge(summed, TB)
            nc.vector.tensor_scalar(sums, sums, 1.0 / HD, EPS, ALU.mult, ALU.add).then_inc(mean_ready, 1)
            dve.wait_ge(cmp_turned, 1)
            dve.wait_ge(small_loaded, 16)
            half = CMP_STRIDE // 2
            for kv in range(2):
                for odd in range(2):
                    rows = slice(odd * HD, (odd + 1) * HD)
                    turned_kv = m.bank[rows, 4 + 2 * kv:6 + 2 * kv, odd::2]
                    for part in range(2):
                        src = turned_kv[:, :, part * half:part * half + N_CMP * half].rearrange("p g (n l) -> p l g n", l=half)
                        pos = place[rows, kv, odd::2][:, part * half:(part + 1) * half]
                        pos = pos.rearrange("p (l g n) -> p l g n", g=1, n=1).broadcast_to([HD, half, GROUPS, N_CMP])
                        nc.vector.tensor_tensor(windows[rows, kv, part * half:(part + 1) * half], src, pos, ALU.add)\
                            .then_inc(windows_ready, 1)
            dve.wait_ge(rooted, 1)
            link(nc.vector.reciprocal(sums, sums))
            nc.vector.tensor_scalar(sums[:, :, 0:HEADS], sums[:, :, 0:HEADS], HD ** -0.5, None, ALU.mult)\
                .then_inc(scales_ready, 1)
            dve.wait_ge(scales_ready, 1)
            q = q_tok.rearrange("p (h c) -> p h c", h=HEADS)
            for t in range(TB):
                if t >= 1:
                    dve.wait_ge(turned, 2 * t - 1)
                src = tok(m, "nq")[:, t, :].rearrange("p (h c) -> p h c", h=HEADS)
                link(nc.vector.tensor_tensor(q, src, per_head(sums[:, t, 0:HEADS], HD), ALU.mult))
                link(nc.vector.tensor_tensor(q, q, spread(gains[:, 0:HD], HEADS), ALU.mult))
                rotate(nc.vector, link, q, m.nsa_cos[:, t, :], m.nsa_sin[:, t, :], turn_q, HEADS)
                nc.vector.tensor_tensor(q, turn_q[:, 0], turn_q[:, 1], ALU.add).then_inc(q_ready, 1)
                dve.wait_ge(q_ready, t + 1)
            dve.wait_ge(cmp_done, 1)
            link(nc.vector.tensor_copy(kc_tok, m.bank[0:N_CMP, 4, 0:2 * HD].rearrange("p (g c) -> p g c", g=GROUPS)))
            link(nc.vector.tensor_tensor(kc_turn[:, 0], kc_tok, kc_tok, ALU.mult))
            link(nc.vector.tensor_reduce(kc_sums, kc_turn[:, 0], AX.X, ALU.add))
            nc.vector.tensor_scalar(kc_sums, kc_sums, 1.0 / HD, EPS, ALU.mult, ALU.add).then_inc(kc_squared, 1)
            dve.wait_ge(kc_rooted, 1)
            link(nc.vector.reciprocal(kc_sums, kc_sums))
            link(nc.vector.tensor_tensor(kc_tok, kc_tok, per_head(kc_sums, HD), ALU.mult))
            link(nc.vector.tensor_tensor(kc_tok, kc_tok, spread(gains[0:N_CMP, HD:2 * HD], GROUPS), ALU.mult))
            rotate(nc.vector, link, kc_tok, m.end_cos[0:N_CMP, :], m.end_sin[0:N_CMP, :], kc_turn, GROUPS)
            twice = kc_twice.rearrange("p (h two c) -> p h two c", two=2, c=HD)
            for i in range(2):
                last = nc.vector.tensor_tensor(twice[:, :, i, :], kc_turn[:, 0], kc_turn[:, 1], ALU.add)
            last.then_inc(kc_ready, 1)

        @block.gpsimd
        def _(pool):
            link = chained(pool, pool_chain)
            for i, name in enumerate(("ck", "cv")):
                src = tok(m, name).rearrange("p t (g c) -> p t g c", g=GROUPS)
                for j in range(2):
                    last = nc.gpsimd.tensor_copy(cmp_twice[i][:, :, :, j * HD:(j + 1) * HD], src)
                last.then_inc(cmp_copied, 1)
            pool.wait_ge(scales_ready, 1)
            pool.wait_ge(small_loaded, 16)
            k = k_tok.rearrange("p (h c) -> p h c", h=KH)
            twice = k_twice.rearrange("p (h two c) -> p h two c", two=2, c=HD)
            for t in range(TB):
                for i, name in enumerate(("sk", "wk")):
                    src = tok(m, name)[:, t, :].rearrange("p (h c) -> p h c", h=GROUPS)
                    g0 = HEADS + i * GROUPS
                    link(nc.gpsimd.tensor_tensor(k[:, i * GROUPS:(i + 1) * GROUPS, :], src,
                                                 per_head(sums[:, t, g0:g0 + GROUPS], HD), ALU.mult))
                link(nc.gpsimd.tensor_tensor(k, k, spread(gains[:, HD:2 * HD], KH), ALU.mult))
                rotate(nc.gpsimd, link, k, m.nsa_cos[:, t, :], m.nsa_sin[:, t, :], turn_k, KH)
                if t >= 1:
                    pool.wait_ge(turned, 2 * t)
                for i in range(2):
                    last = nc.gpsimd.tensor_tensor(twice[:, :, i, :], turn_k[:, 0], turn_k[:, 1], ALU.add)
                last.then_inc(k_ready, 1)
                pool.wait_ge(k_ready, t + 1)


def pair_half(h):
    return slice((h % 2) * HD, (h % 2 + 1) * HD)


def compressed_attention(core, m):
    nc = core.nc
    HH = HEADS // 2
    WIDE = TB * HH * N_CMP
    scores = m.z[:, 0:2 * WIDE].rearrange("p (e x) -> p e x", e=2)
    groups = m.z[:, 0:2 * WIDE].rearrange("p (g n) -> p g n", n=N_CMP)
    turned_p = m.z[0:N_CMP, 1024:1024 + TB * HEADS * P].rearrange("p (i t) -> p i t", t=P)
    top = m.small[:, 0:2 * TB * HH]
    total = m.small[:, 32:32 + 2 * TB * HH]
    factor = m.small[:, 64:64 + TB * HEADS].rearrange("p (t h) -> p t h", t=TB)
    score_done, less_max, exp_done, weighed = (core.sem(f"cmp_{n}") for n in ("score_done", "less_max", "exp_done", "weighed"))
    turned, copied, pv_done, chain = (core.sem(f"cmp_{n}") for n in ("turned", "copied", "pv_done", "chain"))

    with nc.Block() as block:
        @block.sync
        def _(sp):
            core.zero_past(sp)

        @block.tensor
        def _(pe):
            for b in range(TB):
                for h in range(HEADS):
                    at_ = (b * HH + h // 2) * N_CMP
                    last = nc.tensor.matmul(m.bank[:, h % 2, at_:at_ + N_CMP], m.nsa_q[pair_half(h), h // 2, b * P:(b + 1) * P],
                                            m.k_cmp[pair_half(h), h // HH, :], start=True, stop=True)
            last.then_inc(score_done, 1)
            pe.wait_ge(weighed, 2)
            for b in range(TB):
                for e in range(2):
                    if b >= 2:
                        pe.wait_ge(copied, 2 * (b - 2) + e + 1)
                    for j in range(HH):
                        at_ = (b * HH + j) * N_CMP
                        last = nc.tensor.transpose(m.bank[0:N_CMP, 2 * (b % 2) + e, j * P:(j + 1) * P],
                                                   scores[:, e, at_:at_ + N_CMP], m.ident[:])
                    last.then_inc(turned, 1)
            for b in range(TB):
                pe.wait_ge(copied, 2 * b + 2)
                for h in range(HEADS):
                    i = (b * 2 + h % 2) * HH + h // 2
                    last = nc.tensor.matmul(m.bank[:, 4 + b, h * HD:(h + 1) * HD], turned_p[:, i, :],
                                            m.v_cmp[:, h // HH, :], start=True, stop=True)
                last.then_inc(pv_done, 1)

        @block.scalar
        def _(act):
            act.wait_ge(less_max, 1)
            nc.scalar.activation(m.z[:, 0:2 * WIDE], m.z[:, 0:2 * WIDE], ACT.Exp).then_inc(exp_done, 1)
            for b in range(TB):
                for e in range(2):
                    act.wait_ge(turned, 2 * b + e + 1)
                    i = (b * 2 + e) * HH
                    nc.scalar.copy(turned_p[:, i:i + HH, :], m.bank[0:N_CMP, 2 * (b % 2) + e, :]
                                   .rearrange("p (h t) -> p h t", h=HH)).then_inc(copied, 1)

        @block.vector
        def _(dve):
            link = chained(dve, chain)

            def windows_of(table):
                return table.rearrange("p t (one n) -> p t one n", one=1).broadcast_to([P, TB, HH, N_CMP])

            def by_head(x):
                return x.rearrange("p (t h n) -> p t h n", t=TB, h=HH)

            dve.wait_ge(score_done, 1)
            for e in range(2):
                link(nc.vector.tensor_tensor(by_head(scores[:, e]), by_head(m.bank[:, e, 0:WIDE]), windows_of(m.cmp_fill),
                                             ALU.add))
            link(nc.vector.tensor_reduce(top, groups, AX.X, ALU.max))
            nc.vector.tensor_tensor(groups, groups, per_head(top, N_CMP), ALU.subtract).then_inc(less_max, 1)
            dve.wait_ge(exp_done, 1)
            for e in range(2):
                nc.vector.tensor_tensor(by_head(scores[:, e]), by_head(scores[:, e]), windows_of(m.cmp_seen), ALU.mult)\
                    .then_inc(weighed, 1)
            dve.wait_ge(weighed, 2)
            link(nc.vector.tensor_reduce(total, groups, AX.X, ALU.add))
            link(nc.vector.tensor_scalar(total, total, 1e-30, None, ALU.max))
            link(nc.vector.reciprocal(total, total))
            gate = tok(m, "gate")[:, :, 0:HEADS]
            for e in range(2):
                link(nc.vector.tensor_tensor(factor[:, :, e::2], total[:, e * TB * HH:(e + 1) * TB * HH]
                                             .rearrange("p (t h) -> p t h", t=TB), gate[:, :, e::2], ALU.mult))
            for b in range(TB):
                dve.wait_ge(pv_done, b + 1)
                nc.vector.tensor_tensor(m.otok[:, b, :].rearrange("p (h c) -> p h c", h=HEADS),
                                        m.bank[:, 4 + b, :].rearrange("p (h c) -> p h c", h=HEADS),
                                        per_head(factor[:, b, :], HD), ALU.mult)


def merge(core, m, gate_dram, out_dram):
    nc = core.nc
    OC = HW // P
    UNIT = D + OC * P
    SLOTS, RAW = BRANCHES, 2
    OUT_SLOTS = 4
    CHUNKS = BRANCHES * OC
    gate_hi, gate_lo = zip(*(parts(m, m.w[:, i * 2 * UNIT:(i + 1) * 2 * UNIT]) for i in range(SLOTS)))
    raw = [m.w[:, (2 * SLOTS + i) * UNIT:(2 * SLOTS + i + 1) * UNIT] for i in range(RAW)]
    out_hi, out_lo = zip(*(parts(m, m.w[:, i * 2 * D:(i + 1) * 2 * D]) for i in range(OUT_SLOTS)))
    out_raw = [m.w[:, (2 * OUT_SLOTS + i) * D:(2 * OUT_SLOTS + i + 1) * D] for i in range(OUT_SLOTS)]
    chunks = lambda v, n: rounded(m, v[:]).rearrange("p (k t) -> p k t", k=n)
    h_hi, h_lo = chunks(m.arena[:, 0:DK * SEQ], DK), rounded(m, m.h[:])
    y_hi = chunks(m.arena[:, DK * SEQ:2 * DK * SEQ], DK)
    o_hi, o_lo = chunks(m.z[:, 0:CHUNKS * SEQ], CHUNKS), rounded(m, m.o[:])
    y = m.sbqk
    y_lo = rounded(m, y[:])
    opened = m.scratch[:, 0:BRANCHES * SEQ].rearrange("p (b t) -> p b t", b=BRANCHES)
    part = [m.scratch[:, BRANCHES * SEQ:], m.z[:, CHUNKS * SEQ:CHUNKS * SEQ + SEQ], m.z[:, CHUNKS * SEQ + SEQ:CHUNKS * SEQ + 2 * SEQ]]
    loaded, raw_used = ([core.sem(f"merge_{n}{i}") for i in range(RAW)] for n in ("loaded", "raw_used"))
    out_loaded, out_hi_ready, out_ready, out_used = (
        [core.sem(f"{n}{i}") for i in range(OUT_SLOTS)] for n in ("out_loaded", "out_hi_ready", "out_ready", "out_used"))
    out_done = core.sem("out_done")
    weights_hi, weights_ready, gate_done, proj_done, opened_ready, part_ready = (
        [core.sem(f"merge_{n}{b}") for b in range(BRANCHES)] for n in (
            "weights_hi", "weights_ready", "gate_done", "proj_done", "opened", "part_ready"))
    h_hi_ready, h_ready, o_hi_ready, o_ready, y_made, y_hi_ready, y_ready, chain = (
        core.sem(f"merge_{n}") for n in ("h_hi_ready", "h_ready", "o_hi_ready", "o_ready", "y_made", "y_hi_ready", "y_ready",
                                         "chain"))

    def raw_slot(j, b):
        return (j * BRANCHES + b) % RAW

    with nc.Block() as block:
        @block.sync
        def _(sp):
            gate_in = gate_dram.rearrange("a j p c -> (a j) p c")
            out_in = out_dram.rearrange("a k p c -> (a k) p c")

            def load(u, i):
                sp.dma_start(raw[i], one(gate_in, u)).then_inc(loaded[i], 16)

            for i in range(RAW):
                load(i, i)
            with sp.Fori(1, DK * BRANCHES // RAW) as r:
                for i in range(RAW):
                    sp.wait_ge(raw_used[i], r)
                    load(r * RAW + i, i)
            for i in range(OUT_SLOTS):
                for j in range(RAW):
                    sp.wait_ge(raw_used[j], DK * BRANCHES // RAW)
                for b in range(BRANCHES):
                    sp.wait_ge(proj_done[b], DK)
                sp.dma_start(out_raw[i], out_in[i]).then_inc(out_loaded[i], 16)
            for k in range(OUT_SLOTS, DK):
                sp.wait_ge(out_ready[k % OUT_SLOTS], k // OUT_SLOTS)
                sp.dma_start(out_raw[k % OUT_SLOTS], out_in[k]).then_inc(out_loaded[k % OUT_SLOTS], 16)
            core.zero_past(sp)

        @block.tensor
        def _(pe):
            def chunk(n, first):
                for b in range(BRANCHES):
                    pe.wait_ge(weights_ready[b], n + 1)
                    if not first:
                        pe.wait_ge(part_ready[b], n)
                    for k in range(DK):
                        if first and b == 0:
                            pe.wait_ge(h_ready, k + 1)
                        cols = slice(k * P, (k + 1) * P)
                        last = split_product(nc, m.bank[:, 2 * b, :], (gate_hi[b][:, cols], gate_lo[b][:, cols]),
                                             (h_hi[:, k, :], h_lo[:, k, :]), start=k == 0, stop=k == DK - 1)
                    last.then_inc(gate_done[b], 1)
                    for k in range(OC):
                        if first:
                            pe.wait_ge(o_ready, b * OC + k + 1)
                        cols = slice(D + k * P, D + (k + 1) * P)
                        last = split_product(nc, m.bank[:, 2 * b + 1, :], (gate_hi[b][:, cols], gate_lo[b][:, cols]),
                                             (o_hi[:, b * OC + k, :], o_lo[:, b * OC + k, :]), start=k == 0, stop=k == OC - 1)
                    last.then_inc(proj_done[b], 1)

            chunk(0, True)
            with pe.Fori(1, DK) as n:
                chunk(n, False)
            pe.wait_ge(y_made, DK)
            for k in range(DK):
                i = k % OUT_SLOTS
                pe.wait_ge(y_ready, k + 1)
                pe.wait_ge(out_ready[i], k // OUT_SLOTS + 1)
                for c in range(DK):
                    cols = slice(c * P, (c + 1) * P)
                    last = split_product(nc, m.bank[:, c, :], (out_hi[i][:, cols], out_lo[i][:, cols]),
                                         (y_hi[:, k, :], y_lo[:, k, :]), start=k == 0, stop=k == DK - 1)
                    if k == DK - 1:
                        last.then_inc(out_done, 1)
                if k < DK - 1:
                    last.then_inc(out_used[i], 1)

        @block.scalar
        def _(act):
            def split_weights(pair, j, b, first):
                i = raw_slot(j, b)
                act.wait_ge(loaded[i], (pair * BRANCHES + (j * BRANCHES + b) // RAW + 1) * 16)
                if not first:
                    act.wait_ge(proj_done[b], pair * 2 + j)
                nc.scalar.copy(gate_hi[b], raw[i]).then_inc(weights_hi[b], 1)

            def open_gate(n, b, first):
                act.wait_ge(gate_done[b], n + 1)
                if not first:
                    act.wait_ge(part_ready[b], n)
                nc.scalar.activation(opened[:, b, :], m.bank[:, 2 * b, :], ACT.Sigmoid).then_inc(opened_ready[b], 1)

            def split_y(n):
                act.wait_ge(y_made, n + 1)
                nc.scalar.copy(column(y_hi, n), column(y, n)).then_inc(y_hi_ready, 1)

            split_weights(0, 0, 0, True)
            for k in range(DK):
                nc.scalar.copy(h_hi[:, k, :], m.h[:, k, :]).then_inc(h_hi_ready, 1)
            for b in range(BRANCHES):
                if b >= 1:
                    split_weights(0, 0, b, True)
                for k in range(b * OC, (b + 1) * OC):
                    nc.scalar.copy(o_hi[:, k, :], m.o[:, k, :]).then_inc(o_hi_ready, 1)
            for b in range(BRANCHES):
                open_gate(0, b, True)
                split_weights(0, 1, b, False)
            with act.Fori(0, DK // 2 - 1) as pair:
                for j in range(2):
                    split_y(pair * 2 + j)
                    for b in range(BRANCHES):
                        open_gate(pair * 2 + j + 1, b, False)
                        split_weights(pair + 1, j, b, False)
            split_y(DK - 2)
            for b in range(BRANCHES):
                open_gate(DK - 1, b, False)
            split_y(DK - 1)
            for k in range(DK):
                i = k % OUT_SLOTS
                act.wait_ge(out_loaded[i], 16 * (k // OUT_SLOTS) + 16)
                if k >= OUT_SLOTS:
                    act.wait_ge(out_used[i], k // OUT_SLOTS)
                nc.scalar.copy(out_hi[i], out_raw[i]).then_inc(out_hi_ready[i], 1)

        @block.vector
        def _(dve):
            def split_weights(pair, j, b):
                i = raw_slot(j, b)
                dve.wait_ge(weights_hi[b], pair * 2 + j + 1)
                nc.vector.tensor_tensor(gate_lo[b], raw[i], gate_hi[b], ALU.subtract).then_inc(weights_ready[b], 1)

            def count_raw(pair, j, b):
                dve.wait_ge(weights_ready[b], pair * 2 + j + 1)
                dve.sem_inc(raw_used[raw_slot(j, b)], 1)

            def gated(n, b):
                dve.wait_ge(opened_ready[b], n + 1)
                dve.wait_ge(proj_done[b], n + 1)
                nc.vector.tensor_tensor(part[b], opened[:, b, :], m.bank[:, 2 * b + 1, :], ALU.mult).then_inc(part_ready[b], 1)

            def join(n):
                dve.wait_ge(part_ready[1], n + 1)
                nc.vector.tensor_tensor(part[0], part[0], part[1], ALU.add).then_inc(chain, 1)
                dve.wait_ge(part_ready[2], n + 1)
                dve.wait_ge(chain, n + 1)
                nc.vector.tensor_tensor(column(y, n), part[0], part[2], ALU.add).then_inc(y_made, 1)
                dve.wait_ge(y_hi_ready, n + 1)
                nc.vector.tensor_tensor(column(y_lo, n), column(y, n), column(y_hi, n), ALU.subtract).then_inc(y_ready, 1)

            split_weights(0, 0, 0)
            for k in range(DK):
                dve.wait_ge(h_hi_ready, k + 1)
                nc.vector.tensor_tensor(h_lo[:, k, :], m.h[:, k, :], h_hi[:, k, :], ALU.subtract).then_inc(h_ready, 1)
            count_raw(0, 0, 0)
            for b in range(BRANCHES):
                if b >= 1:
                    split_weights(0, 0, b)
                for k in range(b * OC, (b + 1) * OC):
                    dve.wait_ge(o_hi_ready, k + 1)
                    nc.vector.tensor_tensor(o_lo[:, k, :], m.o[:, k, :], o_hi[:, k, :], ALU.subtract).then_inc(o_ready, 1)
                if b >= 1:
                    count_raw(0, 0, b)
            for b in range(BRANCHES):
                gated(0, b)
                split_weights(0, 1, b)
                count_raw(0, 1, b)
            with dve.Fori(0, DK // 2 - 1) as pair:
                for j in range(2):
                    join(pair * 2 + j)
                    for b in range(BRANCHES):
                        gated(pair * 2 + j + 1, b)
                        split_weights(pair + 1, j, b)
                        count_raw(pair + 1, j, b)
            join(DK - 2)
            for b in range(BRANCHES):
                gated(DK - 1, b)
            join(DK - 1)
            for k in range(DK):
                i = k % OUT_SLOTS
                dve.wait_ge(out_hi_ready[i], k // OUT_SLOTS + 1)
                nc.vector.tensor_tensor(out_lo[i], out_raw[i], out_hi[i], ALU.subtract).then_inc(out_ready[i], 1)
            for c in range(DK):
                dve.wait_ge(out_done, c + 1)
                nc.vector.tensor_tensor(m.x[:, c, :], m.bank[:, c, :], m.x[:, c, :], ALU.add)


LAYERS = 2


def first_block(core, m, a):
    nc = core.nc
    m.tok = m.arena[:, 0:TB * TOK_W].rearrange("p (t c) -> p t c", t=TB)
    m.o = m.arena[:, 8928:8928 + 12 * SEQ].rearrange("p (c t) -> p c t", c=12)
    m.sbqk = m.arena[:, 15072:15072 + 8 * SEQ].rearrange("p (c t) -> p c t", c=8)
    m.z = m.arena[:, 19168:26624]
    m.late = m.arena[:, 8928:8928 + 12 * SEQ]
    m.otok = m.scratch.rearrange("p (t c) -> p t c", t=TB)
    m.probs = m.z[:, 4096:5632].rearrange("p (n k) -> p n k", n=3)
    m.turned_p = m.z[:, 5632:7168].rearrange("p (n k) -> p n k", n=3)
    m.part = m.z[:, 0:SEQ]
    m.sums = m.small[:, 128:160].rearrange("p (t h) -> p t h", t=TB)
    m.neg_max = m.small[:, 160:163]
    m.mla_q = m.w[0:QK_MLA, 0:4096].rearrange("p (h t) -> p h t", h=HEADS)
    m.mla_k = m.w[0:QK_MLA, 4096:8192].rearrange("p (h t) -> p h t", h=HEADS)
    m.mla_kv = m.z[:, 0:4096].rearrange("p (t c) -> p t c", t=TB)
    m.nsa_q = m.w[:, 8192:10240].rearrange("p (c t) -> p c t", c=4)
    m.nsa_k = m.w[:, 10240:12288].rearrange("p (c t) -> p c t", c=4)
    m.odds = m.w[:, 0:1536].rearrange("p (n k) -> p n k", n=3)
    m.rest = m.w[:, 1536:3072].rearrange("p (n k) -> p n k", n=3)
    m.left = m.w[:, 3072:3072 + 3 * (SEQ + 1)].rearrange("p (n k) -> p n k", n=3)
    m.ones_row = m.w[:, 4611:4611 + SEQ]

    def keys_of(name):
        base = {"sk": 0, "wk": 2}[name]
        return lambda h, keys: m.nsa_k[pair_half(h), base + h // 4, 0:keys]

    def values_of(name):
        return lambda h, kb: tok(m, name)[:, kb, h // 4 * HD:(h // 4 + 1) * HD]

    def queries(h, b):
        return m.nsa_q[pair_half(h), h // 2, b * P:(b + 1) * P]

    core.zero_all()
    with nc.Fori(0, LAYERS) as l:
        ffn(core, m, "ffn1", at(a["ffn1_norm"], l), at(a["ffn1_wi"], l), at(a["ffn1_wo"], l))
        core.next_stage()
        in_projection(core, m, at(a["mix_norm"], l), at(a["w_in_qk"], l), at(a["w_in_tok"], l))
        core.next_stage()
        mla_prepare(core, m, at(a["mla_w_uq"], l), at(a["mla_w_ukv"], l), at(a["mla_norms"], l), at(a["mla_gains"], l))
        core.next_stage()
        attention(core, m, "mla", lambda h, b: m.mla_q[:, h, b * P:(b + 1) * P], lambda h, keys: m.mla_k[:, h, 0:keys],
                  lambda h, kb: m.mla_kv[:, kb, h * 2 * HD + HD:(h + 1) * 2 * HD], m.causal_bf, m.w[:, 11776:11776 + HW], out=m.o[:, 4:8])
        core.next_stage()
        nsa_prepare(core, m, at(a["cmp_w1"], l), at(a["nsa_small"], l), None)
        core.next_stage()
        compressed_attention(core, m)
        core.next_stage()
        attention(core, m, "slc", queries, keys_of("sk"), values_of("sv"), m.causal_bf, m.w[:, 6144:6144 + HW], add=True,
                  gate=lambda b: tok(m, "gate")[:, b, HEADS:2 * HEADS])
        core.next_stage()
        attention(core, m, "win", queries, keys_of("wk"), values_of("wv"), m.causal_bf, m.w[:, 6144:6144 + HW], add=True,
                  gate=lambda b: tok(m, "gate")[:, b, 2 * HEADS:3 * HEADS], out=m.o[:, 8:12])
        core.next_stage()
        attention(core, m, "stick", lambda h, b: m.sbqk[pair_half(h), h // 2, b * P:(b + 1) * P],
                  lambda h, keys: m.sbqk[pair_half(h), 4 + h // 2, 0:keys],
                  lambda h, kb: tok(m, "sb_v")[:, kb, h * HD:(h + 1) * HD], m.strict_bf, m.w[:, 6144:6144 + HW], stick=True, out=m.o[:, 0:4])
        core.next_stage()
        merge(core, m, at(a["merge_w"], l), at(a["w_out"], l))
        core.next_stage()
        ffn(core, m, "ffn2", at(a["ffn2_norm"], l), at(a["ffn2_wi"], l), at(a["ffn2_wo"], l))
        core.zero_all()


def allocate(core, m):
    nc = core.nc
    m.rounded = {}

    def both(name, shape):
        tensor = core.sbuf(name, shape)
        m.rounded[tensor.name] = core.rounded_name(tensor)
        return tensor

    m.x = core.sbuf("x_t", [P, DK, SEQ])
    m.h = both("h_t", [P, DK, SEQ])
    m.w = both("weights", [P, 12288])
    m.arena = both("arena", [P, 26624])
    m.scratch = core.sbuf("scratch", [P, 2048])
    m.square = m.scratch[:, 0:2 * SEQ].rearrange("p (n t) -> p n t", n=2)
    m.root = m.scratch[:, 2 * SEQ:3 * SEQ]
    m.mean = m.scratch[:, 3 * SEQ:4 * SEQ]
    m.gain = core.sbuf("gain", [P, DK])
    m.ones = core.sbuf("ones", [P, P])
    m.small = core.sbuf("small", [P, 256])
    m.nsa_small = core.sbuf("nsa_small_sb", [P, 320])
    cmp_ = core.sbuf("cmp_kv", [P, 2 * N_CMP + KV_W])
    m.k_cmp = cmp_[:, 0:2 * N_CMP].rearrange("p (g n) -> p g n", g=GROUPS)
    m.v_cmp = cmp_[0:N_CMP, 2 * N_CMP:].rearrange("p (g c) -> p g c", g=GROUPS)
    m.ident_bf, m.causal_bf, m.strict_bf = (core.sbuf(n, [P, P], BF16) for n in ("ident_bf", "causal_bf", "strict_bf"))
    places, width = const_places()
    m.const = core.sbuf("const_sb", [P, width])
    c = {name: m.const[:, i:j] for name, (i, j) in places.items()}
    m.ident, m.causal, m.strict = c["ident"], c["causal"], c["strict"]
    m.mla_cos, m.mla_sin, m.nsa_cos, m.nsa_sin, m.cmp_fill, m.cmp_seen = (
        c[n].rearrange("p (t c) -> p t c", t=TB) for n in ("mla_cos", "mla_sin", "nsa_cos", "nsa_sin", "cmp_fill", "cmp_seen"))
    m.end_cos, m.end_sin = c["end_cos"], c["end_sin"]
    m.ident_neg = core.sbuf("ident_neg", [P, P], BF16)
    m.tail = core.sbuf("tail", [P, 680])
    m.bank = core.ctx.enter_context(nc.psum_tensor("bank", [P, 8, SEQ], F32))


def load_start(core, m, a):
    nc = core.nc
    loaded = core.sem("start_loaded")
    with nc.Block() as block:
        @block.sync
        def _(sp):
            sp.dma_start(m.x[:], a["x"]).then_inc(loaded, 16)
            sp.dma_start(m.const[:], a["const"]).then_inc(loaded, 16)
            sp.wait_ge(loaded, 32)

        @block.vector
        def _(dve):
            nc.vector.memset(m.ones[:], 1.0)
            dve.wait_ge(loaded, 32)
            nc.vector.tensor_copy(m.ident_bf[:], m.ident)
            nc.vector.tensor_scalar(m.ident_neg[:], m.ident, -1.0, None, ALU.mult)
            nc.vector.tensor_copy(m.causal_bf[:], m.causal)
            nc.vector.tensor_copy(m.strict_bf[:], m.strict)


def lay_out_first(i):
    f = lambda n: np.asarray(i[n])
    L = LAYERS

    def gain(n):
        return f(n).reshape(L, DK, P).transpose(0, 2, 1)

    def chunks(w, c):
        return w.reshape(L, DK, P, -1, c).transpose(0, 3, 2, 1, 4).reshape(L, -1, P, DK * c)

    def up(w):
        return w.reshape(L, DK, P, 2, D_FF // P, P).transpose(0, 4, 2, 3, 1, 5).reshape(L, D_FF // P, P, 2 * D)

    def rows(v):
        return np.broadcast_to(v[:, None, :], (L, P, v.shape[-1]))

    w_in = f("w_in")
    n_tok = 2 * HW + TOK_W
    gates = w_in[:, :, n_tok:].reshape(L, DK, P, BRANCHES, DK, P).transpose(0, 4, 3, 2, 1, 5).reshape(L, DK, BRANCHES, P, -1)
    proj = np.stack([f(n) for n in ("proj_sb", "proj_mla", "proj_nsa")], 1)
    proj = proj.reshape(L, BRANCHES, HW // P, P, DK, P).transpose(0, 4, 1, 3, 2, 5).reshape(L, DK, BRANCHES, P, -1)
    w1 = np.stack([f("cmp_wk1"), f("cmp_wv1")], 1).reshape(L, 2, CMP_LEN // 2, 2, HD, CMP_HIDDEN).transpose(0, 3, 4, 1, 2, 5)
    place = np.stack([f("cmp_pos_k"), f("cmp_pos_v")], 1).transpose(0, 3, 1, 2).reshape(L, HD, -1)
    w2 = np.stack([f("cmp_wk2"), f("cmp_wv2")], 1).transpose(0, 2, 1, 3).reshape(L, CMP_HIDDEN, -1)
    out = {
        "x": f("x")[0].T.reshape(DK, P, SEQ).transpose(1, 0, 2),
        "const": const_array(),
        "mix_norm": gain("mix_norm"),
        "w_in_qk": chunks(w_in[:, :, 0:2 * HW], P),
        "w_in_tok": chunks(w_in[:, :, 2 * HW:n_tok], TOK_C),
        "mla_w_uq": f("mla_w_uq").reshape(L, 2, P, -1).transpose(0, 2, 1, 3).reshape(L, P, -1),
        "mla_w_ukv": f("mla_w_ukv"),
        "mla_norms": np.concatenate([f("mla_q_norm").reshape(L, 2, P).transpose(0, 2, 1), f("mla_kv_norm")[:, :, None]], 2),
        "mla_gains": rows(np.concatenate([f("mla_qk_gain_q"), f("mla_qk_gain_k")], 1)),
        "cmp_w1": w1.reshape(L, P, -1),
        "nsa_small": np.concatenate([rows(np.concatenate([f("nsa_q_gain"), f("nsa_k_gain")], 1)),
                                     np.concatenate([place, place], 1), w2], 2),
        "merge_w": np.concatenate([gates, proj], 4).reshape(L, DK * BRANCHES, P, -1),
        "w_out": f("w_out").reshape(L, DK, P, D),
    }
    for n in ("ffn1", "ffn2"):
        out[f"{n}_norm"] = gain(f"{n}_norm")
        out[f"{n}_wi"] = up(f(f"{n}_wi"))
        out[f"{n}_wo"] = f(f"{n}_wo").reshape(L, D_FF // P, P, D)
    return {n: np.ascontiguousarray(v) for n, v in out.items()}


GH = 4
CONV_K = 5
N_FM = 28
FM_AT = dict(gq=0, gk=4, gv=8, gz=12, mo=16, mq=20, mk=24)
KINDS = dict(a=0, b=1, i=2, f=3)
GATE_ROWS = 36
BACK = 32
DIRS = 2
GATE_C = len(KINDS) * GATE_ROWS


def gate_row(d, h):
    return d * BACK + h


def second_projection(core, m, a):
    nc = core.nc
    SLOTS = 2
    slot = [m.w[:, i * 2 * D:(i + 1) * 2 * D] for i in range(SLOTS)]
    w_hi, w_lo = zip(*(parts(m, v) for v in slot))
    raw = [m.w[:, (2 * SLOTS + i) * D:(2 * SLOTS + i + 1) * D] for i in range(SLOTS)]
    gate_slot = m.w[:, 3 * SLOTS * D:3 * SLOTS * D + 2 * DK * GATE_C]
    gate_hi, gate_lo = parts(m, gate_slot)
    gate_raw = gate_slot[:, DK * GATE_C:]
    h_hi = rounded(m, m.cv[:, 0:DK, :])
    h_lo = rounded(m, m.h[:])
    s = norm_steps(core, "second")
    loaded, hi_ready, ready, done, copied = (
        [core.sem(f"fm_{n}{i}") for i in range(SLOTS)] for n in ("loaded", "hi_ready", "ready", "done", "copied"))
    gates_loaded, gates_hi, gates_ready, gates_done, rest_loaded = (
        core.sem(f"gates_{n}") for n in ("loaded", "hi", "ready", "done", "rest_loaded"))
    V_UNITS = DK // 2
    rounds, v_rounds = N_FM // SLOTS, V_UNITS // SLOTS

    with nc.Block() as block:
        @block.sync
        def _(sp):
            sp.dma_start(m.gain[:], a["norm1_2"]).then_inc(s["gain_loaded"], 16)

            def load(r, i):
                sp.dma_start(raw[i], one(a["w_in_fm_2"], r * SLOTS + i)).then_inc(loaded[i], 16)

            for i in range(SLOTS):
                load(0, i)
            sp.dma_start(gate_raw, a["w_in_gates_2"]).then_inc(gates_loaded, 16)
            sp.dma_start(m.const[:, P:P + m.const_2_width], a["const_2"]).then_inc(rest_loaded, 16)
            sp.dma_start(m.gdn_small, a["gdn_small_2"]).then_inc(rest_loaded, 16)
            with sp.Fori(1, rounds + v_rounds) as r:
                for i in range(SLOTS):
                    sp.wait_ge(ready[i], r)
                    load(r, i)
            core.zero_past(sp)

        @block.tensor
        def _(pe):
            norm_tensor(nc, pe, m, s)
            pe.wait_ge(s["mean_ready"], 1)

            def chunk(r, i, first):
                pe.wait_ge(ready[i], r + 1)
                if not first:
                    pe.wait_ge(copied[i], r)
                for k in range(DK):
                    if first and i == 0:
                        pe.wait_ge(s["normed"], k + 1)
                    part = slice(k * P, (k + 1) * P)
                    last = split_product(nc, m.bank[:, i, :], (w_hi[i][:, part], w_lo[i][:, part]), (h_hi[:, k, :], h_lo[:, k, :]),
                                         start=k == 0, stop=k == DK - 1)
                last.then_inc(done[i], 1)

            for i in range(SLOTS):
                chunk(0, i, True)
            with pe.Fori(1, rounds) as r:
                for i in range(SLOTS):
                    chunk(r, i, False)
            for u in range(V_UNITS):
                i = u % SLOTS
                pe.wait_ge(ready[i], rounds + u // SLOTS + 1)
                for j in range(2):
                    k = 2 * u + j
                    part = slice(j * SEQ, (j + 1) * SEQ)
                    for t in range(TB):
                        tokens = slice(t * P, (t + 1) * P)
                        last = split_product(nc, m.bank[:, 2 + t, :], (h_hi[:, k, tokens], h_lo[:, k, tokens]),
                                             (w_hi[i][:, part], w_lo[i][:, part]), start=k == 0, stop=k == DK - 1)
                last.then_inc(done[i], 1)
            pe.wait_ge(gates_ready, 1)
            for t in range(TB):
                tokens = slice(t * P, (t + 1) * P)
                for k in range(DK):
                    part = slice(k * GATE_C, (k + 1) * GATE_C)
                    last = split_product(nc, m.bank[:, 6 + t // 2, t % 2 * GATE_C:(t % 2 + 1) * GATE_C],
                                         (h_hi[:, k, tokens], h_lo[:, k, tokens]), (gate_hi[:, part], gate_lo[:, part]),
                                         start=k == 0, stop=k == DK - 1)
            last.then_inc(gates_done, 1)

        @block.scalar
        def _(act):
            def split(r, i, first):
                act.wait_ge(loaded[i], r * 16 + 16)
                if not first:
                    act.wait_ge(done[i], r)
                nc.scalar.copy(w_hi[i], raw[i]).then_inc(hi_ready[i], 1)

            def store(r, i):
                act.wait_ge(done[i], r + 1)
                nc.scalar.copy(column(m.fm, r * SLOTS + i), m.bank[:, i, :]).then_inc(copied[i], 1)

            norm_scalar(nc, act, m, s, lambda: split(0, 0, True))
            norm_hi(nc, act, m, s, h_hi)
            split(0, 1, True)
            act.wait_ge(gates_loaded, 16)
            nc.scalar.copy(gate_hi, gate_raw).then_inc(gates_hi, 1)
            with act.Fori(0, rounds) as r:
                for i in range(SLOTS):
                    store(r, i)
                    split(r + 1, i, False)
            for r in range(rounds + 1, rounds + v_rounds):
                for i in range(SLOTS):
                    split(r, i, False)

        @block.vector
        def _(dve):
            def split(r, i):
                dve.wait_ge(hi_ready[i], r + 1)
                nc.vector.tensor_tensor(w_lo[i], raw[i], w_hi[i], ALU.subtract).then_inc(ready[i], 1)

            norm_vector(nc, dve, m, s, m.gain, h_hi, h_lo, lambda: split(0, 0))
            split(0, 1)
            dve.wait_ge(gates_hi, 1)
            nc.vector.tensor_tensor(gate_lo, gate_raw, gate_hi, ALU.subtract).then_inc(gates_ready, 1)
            dve.wait_ge(rest_loaded, 32)
            nc.vector.tensor_copy(m.strict_bf[:], m.anti)
            nc.vector.memset(m.mv[:, :, :, P:P + 1], 1.0)
            with dve.Fori(1, rounds + v_rounds) as r:
                for i in range(SLOTS):
                    split(r, i)
            dve.wait_ge(done[SLOTS - 1], rounds + v_rounds)
            for t in range(TB):
                nc.vector.tensor_copy(m.mv[:, t, :, 0:P], m.bank[:, 2 + t, :].rearrange("p (h c) -> p h c", h=GH))
            dve.wait_ge(gates_done, 1)
            for i in range(2):
                nc.vector.tensor_copy(m.gates[:, 2 * i:2 * i + 2, :],
                                      m.bank[:, 6 + i, 0:2 * GATE_C].rearrange("p (t c) -> p t c", t=2))


def gate_rows(core, m):
    nc = core.nc
    row = [m.rows[:, i * SEQ:(i + 1) * SEQ] for i in range(6)]
    xa, G, xf, B, shift, neg_m = row
    soft = [m.scratch[0:GATE_ROWS, i * SEQ:(i + 1) * SEQ] for i in range(2)]
    ones = m.scratch[0:GATE_ROWS, 2 * SEQ:3 * SEQ]
    less = m.scratch[0:GATE_ROWS, 3 * SEQ:4 * SEQ]
    dt_bias, a_log, i_bias, f_bias = (m.gdn_small[0:GATE_ROWS, i:i + 1] for i in range(4))
    turned, biased, rate, soft_done = (core.sem(f"rows_{n}") for n in ("turned", "biased", "rate", "soft_done"))
    act_chain, chain, ready, back, selected = (core.sem(f"rows_{n}") for n in ("act_chain", "chain", "ready", "back", "selected"))
    ways = ((slice(0, GH), 1), (slice(BACK, BACK + GH), -1))

    with nc.Block() as block:
        @block.sync
        def _(sp):
            core.zero_past(sp)

        @block.tensor
        def _(pe):
            for bank, kind in enumerate(("a", "i", "f")):
                for t in range(TB):
                    last = nc.tensor.transpose(m.bank[0:GATE_ROWS, bank, t * P:(t + 1) * P],
                                               m.gates[:, t, KINDS[kind] * GATE_ROWS:(KINDS[kind] + 1) * GATE_ROWS], m.ident)
                last.then_inc(turned, 1)
            pe.wait_ge(ready, 3)
            for kind, src in enumerate((G, shift, xf)):
                for t in range(TB):
                    last = nc.tensor.transpose(m.bank[:, 3 + kind, t * GATE_ROWS:(t + 1) * GATE_ROWS],
                                               src[:, t * P:(t + 1) * P], m.ident[0:GATE_ROWS, 0:GATE_ROWS])
            last.then_inc(back, 1)

        @block.scalar
        def _(act):
            link = chained(act, act_chain)
            for i, x in enumerate((xa, xf)):
                act.wait_ge(biased, i + 1)
                link(nc.scalar.activation(soft[i], x, ACT.Abs))
                link(nc.scalar.activation(soft[i], soft[i], ACT.Exp, scale=-1.0))
                nc.scalar.activation(soft[i], soft[i], ACT.Ln, bias=1.0).then_inc(soft_done, 1)
            nc.scalar.activation(m.rate[0:GATE_ROWS, :], a_log, ACT.Exp).then_inc(rate, 1)
            nc.scalar.activation(m.beta, m.gates[:, :, GATE_ROWS:2 * GATE_ROWS], ACT.Sigmoid)

        @block.vector
        def _(dve):
            link = chained(dve, chain)
            link(nc.vector.memset(ones, 1.0))
            for i, (x, bank, bias) in enumerate(((xa, 0, dt_bias), (xf, 2, f_bias))):
                dve.wait_ge(turned, bank + 1)
                nc.vector.tensor_scalar(x, m.bank[0:GATE_ROWS, bank, :], bias, None, ALU.add).then_inc(biased, 1)
            link(nc.vector.tensor_scalar(shift, m.bank[0:GATE_ROWS, 1, :], i_bias, None, ALU.add))
            dve.wait_ge(soft_done, 1)
            dve.wait_ge(rate, 1)
            dve.wait_ge(biased, 2)
            link(nc.vector.scalar_tensor_tensor(soft[0], xa, 0.0, soft[0], ALU.max, ALU.add))
            link(nc.vector.tensor_scalar(xa, soft[0], m.rate[0:GATE_ROWS, :], -1.0, ALU.mult, ALU.mult))
            link(nc.vector.memset(G, 0.0))
            for rows, way in ways:
                for t in range(TB):
                    part = slice(t * P, (t + 1) * P)
                    last = nc.vector.tensor_tensor_scan(G[rows, part][:, ::way], ones[rows, part], xa[rows, part][:, ::way],
                                                        0.0, ALU.mult, ALU.add)
            last.then_inc(ready, 1)
            dve.wait_ge(soft_done, 2)
            link(nc.vector.scalar_tensor_tensor(xf, xf, 0.0, soft[1], ALU.min, ALU.subtract))
            link(nc.vector.memset(B, 0.0))
            for rows, way in ways:
                link(nc.vector.tensor_tensor_scan(B[rows, ::way], ones[rows, :], xf[rows, ::way], 0.0, ALU.mult, ALU.add))
            link(nc.vector.tensor_tensor(less, B, shift, ALU.subtract))
            nc.vector.tensor_tensor(shift, shift, B, ALU.subtract).then_inc(ready, 1)
            link(nc.vector.memset(neg_m, 0.0))
            for rows, way in ways:
                link(nc.vector.tensor_tensor_scan(neg_m[rows, ::way], less[rows, ::way], less[rows, ::way], 0.0, ALU.min, ALU.min))
            nc.vector.tensor_tensor(xf, B, neg_m, ALU.subtract).then_inc(ready, 1)
            dve.wait_ge(back, 1)
            for kind, to in enumerate((m.g_tok, m.shift_tok, m.bm_tok)):
                nc.vector.tensor_copy(to, m.bank[:, 3 + kind, 0:TB * GATE_ROWS].rearrange("p (t r) -> p t r", t=TB))
            sel = m.select.rearrange("p (r c) -> p r c", c=P)
            for d in range(DIRS):
                rows = m.ident[0:GATE_ROWS, d * BACK:d * BACK + GH]
                nc.vector.tensor_copy(sel[:, d * GH:(d + 1) * GH, :],
                                      rows.rearrange("p (r one) -> p r one", one=1).broadcast_to([GATE_ROWS, GH, P]))


def mlstm(core, m):
    nc = core.nc
    select = m.select.rearrange("p (r c) -> p r c", c=P)
    decay = m.w[:, 0:2 * SEQ].rearrange("p (n t) -> p n t", n=2)
    weights = m.w[:, 1024:1024 + 2 * TB * SEQ].rearrange("p (n s t) -> p n s t", n=2, s=TB)
    least = m.w[:, 5120:5120 + TB * GATE_ROWS].rearrange("p (t r) -> p t r", t=TB)
    den = m.w[:, 5376:5376 + 2 * DIRS * GH * TB].rearrange("p (n t) -> p n t", t=TB)
    part = m.w[:, 5632:5632 + 2 * P].rearrange("p (t c) -> p t c", t=2)
    spread_done, score_done, decay_done, weighed, read_m = (
        core.sem(f"ml_{n}") for n in ("spread_done", "score_done", "decay_done", "weighed", "read_m"))
    pv_done, out_read, least_done, convolved, chain = (
        core.sem(f"ml_{n}") for n in ("pv_done", "out_read", "least_done", "convolved", "chain"))
    units = [(h, d) for h in range(GH) for d in range(DIRS)]
    MBANK, SBANK, OBANK = 0, 2, 4

    def queries(d, sb):
        return slice(sb * P, SEQ) if d == 0 else slice(0, (sb + 1) * P)

    with nc.Block() as block:
        @block.sync
        def _(sp):
            core.zero_past(sp)

        @block.tensor
        def _(pe):
            def products(n):
                h, d = units[n]
                pe.wait_ge(weighed, (n + 1) * TB)
                for pair in range(2):
                    if n >= 2:
                        pe.wait_ge(out_read, 2 * (n - 2) + pair + 1)
                    for j in range(2):
                        t = 2 * pair + j
                        keys = range(t + 1) if d == 0 else range(t, TB)
                        for sb in keys:
                            last = nc.tensor.matmul(m.bank[:, OBANK + 2 * (n % 2) + pair, j * (P + 1):(j + 1) * (P + 1)],
                                                    weights[:, n % 2, sb, t * P:(t + 1) * P], m.mv[:, sb, h, :],
                                                    start=sb == keys[0], stop=sb == keys[-1])
                    last.then_inc(pv_done, 1)

            for n, (h, d) in enumerate(units):
                if n >= 1:
                    pe.wait_ge(decay_done, n * TB)
                mask = m.strict_bf if d == 0 else m.causal_bf
                nc.tensor.matmul(m.bank[:, MBANK, :], select[:, d * GH + h, :], m.rows[:, 5 * SEQ:6 * SEQ], start=True, stop=True)
                nc.tensor.matmul(m.bank[:, MBANK + 1, :], select[:, d * GH + h, :], m.rows[:, 5 * SEQ:6 * SEQ], start=True,
                                 stop=False)
                for t in range(TB):
                    last = nc.tensor.matmul(m.bank[:, MBANK + 1, t * P:(t + 1) * P], m.ident_bf[:], mask[:], start=False,
                                            stop=t == TB - 1)
                last.then_inc(spread_done, 1)
                for sb in range(TB):
                    i = n * TB + sb
                    if i >= 2:
                        pe.wait_ge(weighed, i - 1)
                    q = queries(d, sb)
                    nc.tensor.matmul(m.bank[:, SBANK + i % 2, q], m.fm[:, FM_AT["mk"] + h, sb * P:(sb + 1) * P],
                                     m.fm[:, FM_AT["mq"] + h, q], start=True, stop=True).then_inc(score_done, 1)
                if n >= 1:
                    products(n - 1)
            products(len(units) - 1)

        @block.scalar
        def _(act):
            nc.scalar.activation(least, m.bm_tok, ACT.Exp, scale=-1.0).then_inc(least_done, 1)
            for n, (h, d) in enumerate(units):
                act.wait_ge(spread_done, n + 1)
                for sb in range(TB):
                    i = n * TB + sb
                    if i >= 2:
                        act.wait_ge(weighed, i - 1)
                    shift = m.shift_tok[:, sb, gate_row(d, h):gate_row(d, h) + 1]
                    own = slice(sb * P, (sb + 1) * P)
                    rest = slice((sb + 1) * P, SEQ) if d == 0 else slice(0, sb * P)
                    last = nc.scalar.activation(decay[:, i % 2, own], m.bank[:, MBANK + 1, own], ACT.Exp, bias=shift)
                    if rest.stop > rest.start:
                        last = nc.scalar.activation(decay[:, i % 2, rest], m.bank[:, MBANK, rest], ACT.Exp, bias=shift)
                    last.then_inc(decay_done, 1)

        @block.vector
        def _(dve):
            link = chained(dve, chain)
            dve.wait_ge(least_done, 1)

            def divide(n):
                h, d = units[n]
                for pair in range(2):
                    dve.wait_ge(pv_done, 2 * n + pair + 1)
                    bank = m.bank[:, OBANK + 2 * (n % 2) + pair, 0:2 * (P + 1)].rearrange("p (t c) -> p t c", t=2)
                    x = den[:, n, 2 * pair:2 * pair + 2]
                    low = least[:, 2 * pair:2 * pair + 2, gate_row(d, h)]
                    out = m.o_tok[:, 2 * pair:2 * pair + 2, h * P:(h + 1) * P]
                    link(nc.vector.scalar_tensor_tensor(x, bank[:, :, P], -1.0, low, ALU.mult, ALU.max))
                    link(nc.vector.tensor_tensor(x, bank[:, :, P], x, ALU.max))
                    link(nc.vector.reciprocal(x, x))
                    to = out if d == 0 else part
                    nc.vector.tensor_tensor(to, bank[:, :, 0:P], per_head(x, P), ALU.mult).then_inc(out_read, 1)
                    if d == 1:
                        dve.wait_ge(out_read, 2 * n + pair + 1)
                        link(nc.vector.tensor_tensor(out, out, part, ALU.add))

            for n, (h, d) in enumerate(units):
                for sb in range(TB):
                    i = n * TB + sb
                    dve.wait_ge(score_done, i + 1)
                    dve.wait_ge(decay_done, i + 1)
                    if n >= 2 and sb == 0:
                        dve.wait_ge(pv_done, 2 * (n - 1))
                    q = queries(d, sb)
                    nc.vector.scalar_tensor_tensor(weights[:, n % 2, sb, q], m.bank[:, SBANK + i % 2, q], P ** -0.5,
                                                   decay[:, i % 2, q], ALU.mult, ALU.mult).then_inc(weighed, 1)
                    for tap in range(2 * i, min(2 * i + 2, CONV_CHUNKS * CONV_K)):
                        convolve(nc, dve, m, convolved, tap)
                if n >= 1:
                    divide(n - 1)
            divide(len(units) - 1)


def gated_norm(core, m, name, at_chunk, func, gain):
    nc = core.nc
    sums = m.small[:, 0:TB * GH].rearrange("p (t h) -> p t h", t=TB)
    squares = m.w[:, 0:TB * SEQ].rearrange("p (t c) -> p t c", t=TB)
    gates = m.w[:, 2048:2048 + GH * SEQ].rearrange("p (h t) -> p h t", h=GH)
    squared, mean_ready, rooted, scaled = (core.sem(f"{name}_{n}") for n in ("squared", "mean_ready", "rooted", "scaled"))
    gated, turned, chain = (core.sem(f"{name}_{n}") for n in ("gated", "turned", "chain"))

    with nc.Block() as block:
        @block.sync
        def _(sp):
            core.zero_past(sp)

        @block.scalar
        def _(act):
            nc.scalar.activation(squares, m.o_tok, ACT.Square).then_inc(squared, 1)
            act.wait_ge(mean_ready, 1)
            nc.scalar.activation(sums, sums, ACT.Sqrt).then_inc(rooted, 1)
            nc.scalar.activation(gates, m.fm[:, at_chunk:at_chunk + GH, :], func).then_inc(gated, 1)

        @block.vector
        def _(dve):
            link = chained(dve, chain)
            dve.wait_ge(squared, 1)
            link(nc.vector.tensor_reduce(sums, squares.rearrange("p t (h c) -> p t h c", h=GH), AX.X, ALU.add))
            nc.vector.tensor_scalar(sums, sums, 1.0 / P, EPS, ALU.mult, ALU.add).then_inc(mean_ready, 1)
            dve.wait_ge(rooted, 1)
            link(nc.vector.reciprocal(sums, sums))
            for t in range(TB):
                o = m.o_tok[:, t, :].rearrange("p (h c) -> p h c", h=GH)
                nc.vector.tensor_tensor(o, o, per_head(sums[:, t, :], P), ALU.mult).then_inc(scaled, 1)
            dve.wait_ge(gated, 1)
            for h in range(GH):
                dve.wait_ge(turned, h + 1)
                nc.vector.scalar_tensor_tensor(m.fm[:, at_chunk + h, :], m.bank[:, h, :], gain(h), gates[:, h, :], ALU.mult,
                                               ALU.mult)

        @block.tensor
        def _(pe):
            pe.wait_ge(scaled, TB)
            for h in range(GH):
                for t in range(TB):
                    last = nc.tensor.transpose(m.bank[:, h, t * P:(t + 1) * P], m.o_tok[:, t, h * P:(h + 1) * P], m.ident)
                last.then_inc(turned, 1)


CONV_CHUNKS = 3 * GH


def convolve(nc, dve, m, done, i):
    mid = CONV_K // 2
    taps = m.gdn_small[:, 16:16 + CONV_CHUNKS * CONV_K].rearrange("p (c j) -> p c j", c=CONV_CHUNKS)
    place, c = divmod(i, CONV_CHUNKS)
    if place == 0:
        nc.vector.tensor_scalar(m.cv[:, c, :], m.fm[:, c, :], taps[:, c, mid:mid + 1], None, ALU.mult).then_inc(done, 1)
        return
    j = [j for j in range(CONV_K) if j != mid][place - 1]
    to = slice(max(0, mid - j), SEQ - max(0, j - mid))
    of = slice(max(0, j - mid), SEQ - max(0, mid - j))
    dve.wait_ge(done, i - CONV_CHUNKS + 1)
    nc.vector.scalar_tensor_tensor(m.cv[:, c, to], m.fm[:, c, of], taps[:, c, j:j + 1], m.cv[:, c, to], ALU.mult, ALU.add)\
        .then_inc(done, 1)


def conv_and_turn(core, m):
    nc = core.nc
    N = 3 * GH
    silu_done, squared, summed, mean_ready, rooted = (
        core.sem(f"conv_{n}") for n in ("silu_done", "squared", "summed", "mean_ready", "rooted"))
    unit, turned, turned_read, products_done, products_read, chain = (
        core.sem(f"conv_{n}") for n in ("unit", "turned", "turned_read", "products_done", "products_read", "chain"))
    square = m.scratch.rearrange("p (n t) -> p n t", n=4)[:, 0:2]
    root = m.scratch.rearrange("p (n t) -> p n t", n=4)[:, 2:4]

    with nc.Block() as block:
        @block.sync
        def _(sp):
            core.zero_past(sp)

        @block.vector
        def _(dve):
            link = chained(dve, chain)
            for c in range(2 * GH):
                dve.wait_ge(summed, c + 1)
                nc.vector.tensor_scalar(root[:, c % 2, :], m.bank[:, c % 2, :], EPS, None, ALU.add).then_inc(mean_ready, 1)
                dve.wait_ge(rooted, c + 1)
                link(nc.vector.reciprocal(root[:, c % 2, :], root[:, c % 2, :]))
                scale = P ** -0.5 if c < GH else 1.0
                nc.vector.scalar_tensor_tensor(m.cv[:, c, :], m.cv[:, c, :], scale, root[:, c % 2, :], ALU.mult, ALU.mult)\
                    .then_inc(unit, 1)
            for t in range(TB):
                dve.wait_ge(products_done, 2 * t + 1)
                nc.vector.tensor_copy(m.kk[:, t, :], m.bank[:, 4 + 2 * (t % 2), :]).then_inc(products_read, 1)

        @block.scalar
        def _(act):
            for c in range(N):
                nc.scalar.activation(m.cv[:, c, :], m.cv[:, c, :], ACT.Silu).then_inc(silu_done, 1)
            act.wait_ge(silu_done, 2 * GH)
            for c in range(2 * GH):
                if c >= 2:
                    act.wait_ge(summed, c - 1)
                nc.scalar.activation(square[:, c % 2, :], m.cv[:, c, :], ACT.Square).then_inc(squared, 1)
                act.wait_ge(mean_ready, c + 1)
                nc.scalar.activation(root[:, c % 2, :], root[:, c % 2, :], ACT.Sqrt).then_inc(rooted, 1)
            for i in range(2 * TB):
                act.wait_ge(turned, i + 1)
                to = m.k_tok if i < TB else m.v_tok
                nc.scalar.copy(to[:, i % TB, :], m.bank[:, 2 + i % 2, :]).then_inc(turned_read, 1)
            for t in range(TB):
                act.wait_ge(products_done, 2 * t + 2)
                nc.scalar.copy(m.qk[:, t, :], m.bank[:, 5 + 2 * (t % 2), :]).then_inc(turned_read, 1)

        @block.tensor
        def _(pe):
            for c in range(2 * GH):
                pe.wait_ge(squared, c + 1)
                if c >= 2:
                    pe.wait_ge(mean_ready, c - 1)
                nc.tensor.matmul(m.bank[:, c % 2, :], m.ones[:], square[:, c % 2, :], start=True, stop=True).then_inc(summed, 1)
            pe.wait_ge(unit, 2 * GH)
            pe.wait_ge(silu_done, N)
            for i in range(2 * TB):
                if i >= 2:
                    pe.wait_ge(turned_read, i - 1)
                for h in range(GH):
                    c = GH + h if i < TB else 2 * GH + h
                    t = i % TB
                    last = nc.tensor.transpose(m.bank[:, 2 + i % 2, h * P:(h + 1) * P], m.cv[:, c, t * P:(t + 1) * P], m.ident)
                last.then_inc(turned, 1)
            for t in range(TB):
                tokens = slice(t * P, (t + 1) * P)
                if t >= 2:
                    pe.wait_ge(products_read, t - 1)
                    pe.wait_ge(turned_read, 2 * TB + t - 1)
                for i, left in enumerate((GH, 0)):
                    for h in range(GH):
                        last = nc.tensor.matmul(m.bank[:, 4 + 2 * (t % 2) + i, h * P:(h + 1) * P], m.cv[:, left + h, tokens],
                                                m.cv[:, GH + h, tokens], start=True, stop=True)
                    last.then_inc(products_done, 1)


def delta_inverse(core, m):
    nc = core.nc
    W = GH * P
    PAIR = 2
    LANES = PAIR * DIRS
    ROUNDS = TB // PAIR
    dir_of = lambda s: s % DIRS

    def block_of(r, s):
        i = r * PAIR + s // DIRS
        return i if dir_of(s) == 0 else TB - 1 - i

    names = ("E", "N", "D", "Dt", "D2", "D2t", "D4", "Z")
    room = [m.w[:, i * LANES * W:(i + 1) * LANES * W] for i in range(6)] + [m.arena[:, 20480:20480 + LANES * W], m.scratch[:]]
    buf = [{n: place[:, s * W:(s + 1) * W] for n, place in zip(names, room)} for s in range(LANES)]
    for lane in buf:
        lane["X"], lane["D8"], lane["D4t"] = lane["E"], lane["Dt"], lane["D2t"]

    def result(r, s):
        return m.inverse[:, dir_of(s) * TB + block_of(r, s), :]

    select = m.select.rearrange("p (r c) -> p r c", c=P)
    heads = lambda x: x.rearrange("p (h c) -> p h c", h=GH)
    masked = core.sem("inv_masked")
    act_done = [core.sem(f"inv_act_done{s}") for s in range(LANES)]
    dve_done = [core.sem(f"inv_dve_done{s}") for s in range(LANES)]
    pe_done = [core.sem(f"inv_pe_done{s}") for s in range(LANES)]
    links = [core.sem(f"inv_link{s}") for s in range(LANES)]

    with nc.Block() as block:
        @block.sync
        def _(sp):
            core.zero_past(sp)

        steps = ["exponents", "turned_qk", "turned_D", "D2", "D2t", "D4", "D4t", "D8", "Y1", "Y2", "Y3"]
        for b_ in (16, 32, 64):
            steps += [f"X{b_}", f"Z{b_}", f"J{b_}"]
        at_step = {n: i for i, n in enumerate(steps)}
        per_block = len(steps)

        BANKS = 8 // LANES

        def bank(step, d):
            return BANKS * d + at_step[step] % BANKS

        by_dve = ("turned_D", "Y1", "Y2", "Y3", "J16", "J32", "J64", "D2t", "D4t")
        by_act = [n for n in steps if n not in by_dve]
        dve_at = {n: i for i, n in enumerate([n for n in steps if n in by_dve])}
        act_at = {n: i for i, n in enumerate(by_act)}

        def wait_read(eng, n, d, b):
            if n in dve_at:
                eng.wait_ge(dve_done[d], b * len(dve_at) + dve_at[n] + 1)
            else:
                eng.wait_ge(act_done[d], b * len(act_at) + act_at[n] + 1)

        def wait_made(eng, n, d, b):
            eng.wait_ge(pe_done[d], b * per_block + at_step[n] + 1)

        @block.tensor
        def _(pe):
            def operand(name, d, b):
                return result(b, d) if name == "Y" else buf[d][name]

            def product(n, d, b, left, right, needs):
                for x in needs:
                    wait_read(pe, x, d, b)
                last_user = steps[at_step[n] - BANKS] if at_step[n] >= BANKS else None
                if last_user:
                    wait_read(pe, last_user, d, b)
                to = heads(m.bank[:, bank(n, d), :])
                for h in range(GH):
                    last = nc.tensor.matmul(to[:, h, :], heads(operand(left, d, b))[:, h, :], heads(operand(right, d, b))[:, h, :],
                                            start=True, stop=True)
                last.then_inc(pe_done[d], 1)

            def turn(n, d, b, src, needs):
                for x in needs:
                    wait_read(pe, x, d, b)
                last_user = steps[at_step[n] - BANKS] if at_step[n] >= BANKS else None
                if last_user:
                    wait_read(pe, last_user, d, b)
                for h in range(GH):
                    last = nc.tensor.transpose(m.bank[:, bank(n, d), h * P:(h + 1) * P], heads(src)[:, h, :], m.ident)
                last.then_inc(pe_done[d], 1)

            for b in range(ROUNDS):
                for d in range(LANES):
                    t = block_of(b, d)
                    if b >= 1:
                        for n in steps[-BANKS:]:
                            wait_read(pe, n, d, b - 1)
                    mask = m.causal_bf if dir_of(d) == 0 else m.strict_bf
                    for h in range(GH):
                        to = m.bank[:, bank("exponents", d), h * P:(h + 1) * P]
                        nc.tensor.matmul(to, select[:, dir_of(d) * GH + h, :], m.rows[:, SEQ + t * P:SEQ + (t + 1) * P], start=True,
                                         stop=False)
                        last = nc.tensor.matmul(to, m.ident_neg[:], mask[:], start=False, stop=True)
                    last.then_inc(pe_done[d], 1)
                for d in range(LANES):
                    pe.wait_ge(masked, 2 * (b * LANES + d) + 1)
                    turn("turned_qk", d, b, buf[d]["Z"], ())
                for d in range(LANES):
                    pe.wait_ge(masked, 2 * (b * LANES + d) + 2)
                    turn("turned_D", d, b, buf[d]["D"], ())
                for n, left, right, needs in (
                        ("D2", "Dt", "D", ("turned_D",)), ("D2t", "D", "Dt", ()),
                        ("D4", "D2t", "D2", ("D2", "D2t")), ("D4t", "D2", "D2t", ()),
                        ("D8", "D4t", "D4", ("D4", "D4t")),
                        ("Y1", "D2", "Y", ()), ("Y2", "D4", "Y", ("Y1",)), ("Y3", "D8", "Y", ("D8", "Y2"))):
                    for d in range(LANES):
                        product(n, d, b, left, right, needs)
                for size, before in ((16, "Y3"), (32, "J16"), (64, "J32")):
                    for d in range(LANES):
                        turn(f"X{size}", d, b, result(b, d), (before,))
                    for d in range(LANES):
                        off = {16: "D", 32: "D2", 64: "D4"}[size]
                        product(f"Z{size}", d, b, off, "Y", ())
                    for d in range(LANES):
                        product(f"J{size}", d, b, "X", "Z", (f"X{size}", f"Z{size}"))

        @block.scalar
        def _(act):
            for b in range(ROUNDS):
                for d in range(LANES):
                    t = block_of(b, d)
                    wait_made(act, "exponents", d, b)
                    e = heads(buf[d]["E"])
                    if b >= 1:
                        act.wait_ge(masked, 2 * ((b - 1) * LANES + d) + 2)
                    for h in range(GH):
                        r = gate_row(dir_of(d), h)
                        last = nc.scalar.activation(e[:, h, :], m.bank[:, bank("exponents", d), h * P:(h + 1) * P], ACT.Exp,
                                                    bias=m.g_tok[:, t, r:r + 1], scale=-1.0)
                    last.then_inc(act_done[d], 1)
                for n, to in (("turned_qk", None), ("D2", "D2"), ("D4", "D4"), ("D8", "D8"), ("X16", "X"), ("Z16", "Z"),
                              ("X32", "X"), ("Z32", "Z"), ("X64", "X"), ("Z64", "Z")):
                    for d in range(LANES):
                        wait_made(act, n, d, b)
                        dst = m.qk_t[:, dir_of(d) * TB + block_of(b, d), :] if to is None else buf[d][to]
                        nc.scalar.copy(dst, m.bank[:, bank(n, d), :]).then_inc(act_done[d], 1)

        @block.vector
        def _(dve):
            link = [chained(dve, s) for s in links]
            mask = [{n: spread(m.block_mask[:, (dir_of(d) * 4 + i) * P:(dir_of(d) * 4 + i + 1) * P], GH) for i, n in enumerate((16, "16", "32", "64"))}
                    for d in range(LANES)]
            ident = spread(m.ident, GH)
            for b in range(ROUNDS):
                for d in range(LANES):
                    t = block_of(b, d)
                    w = buf[d]
                    wait_read(dve, "exponents", d, b)
                    nc.vector.tensor_tensor(w["Z"], m.qk[:, t, :], w["E"], ALU.mult).then_inc(masked, 1)
                    link[d](nc.vector.tensor_tensor(w["N"], m.kk[:, t, :], w["E"], ALU.mult))
                    beta = m.beta[:, t, dir_of(d) * BACK:dir_of(d) * BACK + GH]
                    link[d](nc.vector.tensor_tensor(heads(w["N"]), heads(w["N"]), per_head(beta, P), ALU.mult))
                    link[d](nc.vector.tensor_scalar(w["N"], w["N"], -1.0, None, ALU.mult))
                    nc.vector.tensor_tensor(heads(w["D"]), heads(w["N"]), mask[d][16], ALU.mult).then_inc(masked, 1)
                    dve.wait_ge(masked, 2 * (b * LANES + d) + 2)

                def copied(n, d, instruction):
                    instruction.then_inc(dve_done[d], 1)
                    wait_read(dve, n, d, b)

                for d in range(LANES):
                    wait_made(dve, "turned_D", d, b)
                    w = buf[d]
                    link[d](nc.vector.tensor_tensor(heads(result(b, d)), heads(m.bank[:, bank("turned_D", d), :]), ident, ALU.add))
                    copied("turned_D", d, nc.vector.tensor_copy(w["Dt"], m.bank[:, bank("turned_D", d), :]))
                for d in range(LANES):
                    wait_made(dve, "D2t", d, b)
                    copied("D2t", d, nc.vector.tensor_copy(buf[d]["D2t"], m.bank[:, bank("D2t", d), :]))
                for d in range(LANES):
                    wait_made(dve, "D4t", d, b)
                    copied("D4t", d, nc.vector.tensor_copy(buf[d]["D4t"], m.bank[:, bank("D4t", d), :]))
                for n, off in (("Y1", None), ("Y2", None), ("Y3", "16"), ("J16", "32"), ("J32", "64"), ("J64", None)):
                    for d in range(LANES):
                        w = buf[d]
                        wait_made(dve, n, d, b)
                        if n == "Y3":
                            link[d](nc.vector.tensor_tensor(heads(w["D"]), heads(w["N"]), mask[d]["16"], ALU.mult))
                            link[d](nc.vector.tensor_tensor(heads(w["D2"]), heads(w["N"]), mask[d]["32"], ALU.mult))
                            link[d](nc.vector.tensor_tensor(heads(w["D4"]), heads(w["N"]), mask[d]["64"], ALU.mult))
                        if n == "J64":
                            t = block_of(b, d)
                            out = result(b, d)
                            link[d](nc.vector.tensor_tensor(out, out, m.bank[:, bank(n, d), :], ALU.add))
                            beta = m.beta[:, t, dir_of(d) * BACK:dir_of(d) * BACK + GH]
                            copied(n, d, nc.vector.tensor_tensor(heads(out), heads(out), per_head(beta, P), ALU.mult))
                        else:
                            copied(n, d, nc.vector.tensor_tensor(result(b, d), result(b, d), m.bank[:, bank(n, d), :], ALU.add))


def delta_rule(core, m):
    nc = core.nc
    W = GH * P
    heads = lambda x: x.rearrange("p (h c) -> p h c", h=GH)
    k_dec = m.w[:, 0:2 * TB * W].rearrange("p (n c) -> p n c", c=W)
    state = [m.w[:, (8 + d) * W:(9 + d) * W] for d in range(DIRS)]
    rest = [m.w[:, (10 + d) * W:(11 + d) * W] for d in range(DIRS)]
    new = [m.w[:, (12 + d) * W:(13 + d) * W] for d in range(DIRS)]
    from_state = [m.w[:, (14 + d) * W:(15 + d) * W] for d in range(DIRS)]
    kept = [m.w[:, (16 + d) * W:(17 + d) * W] for d in range(DIRS)]
    GW = TB * DIRS * GH
    grown = m.w[:, 18 * W:18 * W + GW].rearrange("p (t r) -> p t r", t=TB)
    left = m.w[:, 18 * W + GW:18 * W + 2 * GW].rearrange("p (t r) -> p t r", t=TB)
    whole = m.w[:, 18 * W + 2 * GW:18 * W + 3 * GW].rearrange("p (t r) -> p t r", t=TB)
    factors, exponents, decayed = (core.sem(f"rule_{n}") for n in ("factors", "exponents", "decayed"))
    ks_done, qs_done, new_done, out_done, add_done = (
        [core.sem(f"rule_{n}{d}") for d in range(DIRS)] for n in ("ks_done", "qs_done", "new_done", "out_done", "add_done"))
    rest_ready, new_ready, state_ready, out_ready, qs_read = (
        [core.sem(f"rule_{n}{d}") for d in range(DIRS)] for n in ("rest_ready", "new_ready", "state_ready", "out_ready", "qs_read"))
    links, ends_done = core.sem("rule_link"), core.sem("rule_ends_done")
    select = m.select.rearrange("p (r c) -> p r c", c=P)
    ends = m.bank[:, 2, 0:DIRS * GH * TB].rearrange("p (r t) -> p t r", t=TB)

    def lane(i, d):
        return i if d == 0 else TB - 1 - i

    def rows_of(x, d):
        return x[:, d * GH:(d + 1) * GH]

    with nc.Block() as block:
        @block.sync
        def _(sp):
            core.zero_past(sp)

        @block.tensor
        def _(pe):
            for r in range(DIRS * GH):
                end = P - 1 if r < GH else 0
                last = nc.tensor.matmul(m.bank[:, 2, r * TB:(r + 1) * TB], select[:, r, :], m.rows[:, SEQ + end:2 * SEQ:P],
                                        start=True, stop=True)
            last.then_inc(ends_done, 1)
            for i in range(TB):
                for d in range(DIRS):
                    t = lane(i, d)
                    tokens = slice(t * P, (t + 1) * P)
                    pe.wait_ge(state_ready[d], i + 1)
                    for left_at, bank, done in ((GH, 0, ks_done), (0, 1, qs_done)):
                        for h in range(GH):
                            last = nc.tensor.matmul(heads(m.bank[:, 4 * d + bank, :])[:, h, :], m.cv[:, left_at + h, tokens],
                                                    heads(state[d])[:, h, :], start=True, stop=True)
                        last.then_inc(done[d], 1)
                for d in range(DIRS):
                    t = lane(i, d)
                    pe.wait_ge(rest_ready[d], i + 1)
                    for h in range(GH):
                        last = nc.tensor.matmul(heads(m.bank[:, 4 * d, :])[:, h, :], heads(m.inverse[:, d * TB + t, :])[:, h, :],
                                                heads(rest[d])[:, h, :], start=True, stop=True)
                    last.then_inc(new_done[d], 1)
                for d in range(DIRS):
                    t = lane(i, d)
                    pe.wait_ge(new_ready[d], i + 1)
                    if i == 0:
                        pe.wait_ge(decayed, TB * DIRS)
                    for h in range(GH):
                        last = nc.tensor.matmul(heads(m.bank[:, 4 * d + 3, :])[:, h, :], heads(k_dec[:, d * TB + t, :])[:, h, :],
                                                heads(new[d])[:, h, :], start=True, stop=True)
                    last.then_inc(add_done[d], 1)
                    if i >= 1:
                        pe.wait_ge(out_ready[d], i)
                    for h in range(GH):
                        last = nc.tensor.matmul(heads(m.bank[:, 4 * d + 2, :])[:, h, :], heads(m.qk_t[:, d * TB + t, :])[:, h, :],
                                                heads(new[d])[:, h, :], start=True, stop=True)
                    last.then_inc(out_done[d], 1)

        @block.scalar
        def _(act):
            act.wait_ge(exponents, 1)
            nc.scalar.activation(left, left, ACT.Exp).then_inc(factors, 1)
            nc.scalar.activation(grown, grown, ACT.Exp).then_inc(factors, 1)
            nc.scalar.activation(whole, whole, ACT.Exp).then_inc(factors, 1)
            for i in range(TB):
                for d in range(DIRS):
                    act.wait_ge(new_done[d], i + 1)
                    if i >= 1:
                        act.wait_ge(out_done[d], i)
                    nc.scalar.copy(new[d], m.bank[:, 4 * d, :]).then_inc(new_ready[d], 1)

        @block.gpsimd
        def _(pool):
            pool.wait_ge(factors, 1)
            for i in range(TB):
                for d in range(DIRS):
                    t = lane(i, d)
                    nc.gpsimd.tensor_tensor(heads(k_dec[:, d * TB + t, :]), heads(m.k_tok[:, t, :]),
                                            per_head(rows_of(left[:, t, :], d), P), ALU.mult).then_inc(decayed, 1)

        @block.vector
        def _(dve):
            link = chained(dve, links)
            for d in range(DIRS):
                last = nc.vector.memset(state[d], 0.0).then_inc(state_ready[d], 1)
            dve.wait_ge(ends_done, 1)
            for d in range(DIRS):
                g = m.g_tok[:, :, d * BACK:d * BACK + GH]
                part = slice(d * GH, (d + 1) * GH)
                link(nc.vector.tensor_tensor(left[:, :, part], ends[:, :, part], g, ALU.subtract))
                link(nc.vector.tensor_copy(grown[:, :, part], g))
            nc.vector.tensor_copy(whole, ends).then_inc(exponents, 1)
            dve.wait_ge(factors, 3)
            for i in range(TB):
                for d in range(DIRS):
                    t = lane(i, d)
                    dve.wait_ge(ks_done[d], i + 1)
                    up = per_head(rows_of(grown[:, t, :], d), P)
                    if i >= 1:
                        dve.wait_ge(new_done[d], i)
                    link(nc.vector.tensor_tensor(heads(rest[d]), heads(m.bank[:, 4 * d, :]), up, ALU.mult))
                    nc.vector.tensor_tensor(rest[d], m.v_tok[:, t, :], rest[d], ALU.subtract).then_inc(rest_ready[d], 1)
                for d in range(DIRS):
                    t = lane(i, d)
                    dve.wait_ge(qs_done[d], i + 1)
                    up = per_head(rows_of(grown[:, t, :], d), P)
                    link(nc.vector.tensor_tensor(heads(from_state[d]), heads(m.bank[:, 4 * d + 1, :]), up, ALU.mult))
                    if i < TB - 1:
                        link(nc.vector.tensor_tensor(heads(kept[d]), heads(state[d]), per_head(rows_of(whole[:, t, :], d), P),
                                                     ALU.mult))
                        dve.wait_ge(add_done[d], i + 1)
                        nc.vector.tensor_tensor(state[d], kept[d], m.bank[:, 4 * d + 3, :], ALU.add).then_inc(state_ready[d], 1)
                        dve.wait_ge(state_ready[d], i + 2)
                for d in range(DIRS):
                    t = lane(i, d)
                    dve.wait_ge(out_done[d], i + 1)
                    o = m.o_tok[:, t, :]
                    if i > lane(t, 1 - d):
                        link(nc.vector.tensor_tensor(o, o, from_state[d], ALU.add))
                        nc.vector.tensor_tensor(o, o, m.bank[:, 4 * d + 2, :], ALU.add).then_inc(out_ready[d], 1)
                    else:
                        nc.vector.tensor_tensor(o, from_state[d], m.bank[:, 4 * d + 2, :], ALU.add).then_inc(out_ready[d], 1)
                    dve.wait_ge(out_ready[d], i + 1)


def out_projection(core, m, w_dram):
    nc = core.nc
    SLOTS = 4
    w_hi, w_lo = zip(*(parts(m, m.w[:, i * 2 * D:(i + 1) * 2 * D]) for i in range(SLOTS)))
    raw = [m.w[:, (2 * SLOTS + i) * D:(2 * SLOTS + i + 1) * D] for i in range(SLOTS)]
    y = m.fm[:, FM_AT["gz"]:FM_AT["gz"] + DK, :]
    y_hi, y_lo = rounded(m, m.cv[:, 0:DK, :]), rounded(m, y[:])
    loaded, hi_ready, ready, used = (
        [core.sem(f"out2_{n}{i}") for i in range(SLOTS)] for n in ("loaded", "hi_ready", "ready", "used"))
    y_hi_ready, y_ready, done = (core.sem(f"out2_{n}") for n in ("y_hi_ready", "y_ready", "done"))
    with nc.Block() as block:
        @block.sync
        def _(sp):
            for k in range(DK):
                i = k % SLOTS
                if k >= SLOTS:
                    sp.wait_ge(ready[i], k // SLOTS)
                sp.dma_start(raw[i], w_dram[k]).then_inc(loaded[i], 16)
            core.zero_past(sp)

        @block.tensor
        def _(pe):
            for k in range(DK):
                i = k % SLOTS
                pe.wait_ge(ready[i], k // SLOTS + 1)
                pe.wait_ge(y_ready, k + 1)
                for c in range(DK):
                    cols = slice(c * P, (c + 1) * P)
                    last = split_product(nc, m.bank[:, c, :], (w_hi[i][:, cols], w_lo[i][:, cols]), (y_hi[:, k, :], y_lo[:, k, :]),
                                         start=k == 0, stop=k == DK - 1)
                    if k == DK - 1:
                        last.then_inc(done, 1)
                if k < DK - 1:
                    last.then_inc(used[i], 1)

        @block.scalar
        def _(act):
            for k in range(DK):
                i = k % SLOTS
                nc.scalar.copy(y_hi[:, k, :], y[:, k, :]).then_inc(y_hi_ready, 1)
                act.wait_ge(loaded[i], 16 * (k // SLOTS) + 16)
                if k >= SLOTS:
                    act.wait_ge(used[i], k // SLOTS)
                nc.scalar.copy(w_hi[i], raw[i]).then_inc(hi_ready[i], 1)

        @block.vector
        def _(dve):
            for k in range(DK):
                i = k % SLOTS
                dve.wait_ge(y_hi_ready, k + 1)
                nc.vector.tensor_tensor(y_lo[:, k, :], y[:, k, :], y_hi[:, k, :], ALU.subtract).then_inc(y_ready, 1)
                dve.wait_ge(hi_ready[i], k // SLOTS + 1)
                nc.vector.tensor_tensor(w_lo[i], raw[i], w_hi[i], ALU.subtract).then_inc(ready[i], 1)
            for c in range(DK):
                dve.wait_ge(done, c + 1)
                nc.vector.tensor_tensor(m.x[:, c, :], m.bank[:, c, :], m.x[:, c, :], ALU.add)


PH, KEYS, TOP = 8, 128, 16
PAIRS = 2 * PH
PICKS = PH * TOP
RING = 16


def expert_queries(core, m, a):
    nc = core.nc
    SLOTS = 2
    w_hi, w_lo = zip(*(parts(m, m.w[:, i * 2 * D:(i + 1) * 2 * D]) for i in range(SLOTS)))
    raw = [m.w[:, (2 * SLOTS + i) * D:(2 * SLOTS + i + 1) * D] for i in range(SLOTS)]
    free = m.arena[:, 14336:14336 + 2 * DK * SEQ]
    h_hi, h_lo = (v.rearrange("p (k t) -> p k t", k=DK) for v in parts(m, free))
    s = norm_steps(core, "peer")
    loaded, hi_ready, ready, done, copied = (
        [core.sem(f"wq_{n}{i}") for i in range(SLOTS)] for n in ("loaded", "hi_ready", "ready", "done", "copied"))
    rest_loaded = core.sem("peer_rest_loaded")
    rounds = PAIRS // SLOTS

    with nc.Block() as block:
        @block.sync
        def _(sp):
            sp.dma_start(m.gain[:], a["norm2_2"]).then_inc(s["gain_loaded"], 16)

            def load(r, i):
                sp.dma_start(raw[i], one(a["peer_wq_2"], r * SLOTS + i)).then_inc(loaded[i], 16)

            for i in range(SLOTS):
                load(0, i)
            sp.dma_start(m.keys, a["peer_keys_2"]).then_inc(rest_loaded, 16)
            sp.dma_start(m.final_gain, a["normf_2"]).then_inc(rest_loaded, 16)
            sp.dma_start(m.iota, a["iota"]).then_inc(rest_loaded, 16)
            with sp.Fori(1, rounds) as r:
                for i in range(SLOTS):
                    sp.wait_ge(ready[i], r)
                    load(r, i)
            sp.wait_ge(rest_loaded, 48)
            core.zero_past(sp)

        @block.tensor
        def _(pe):
            norm_tensor(nc, pe, m, s)
            pe.wait_ge(s["mean_ready"], 1)

            def chunk(r, i, first):
                pe.wait_ge(ready[i], r + 1)
                if not first:
                    pe.wait_ge(copied[i], r)
                for k in range(DK):
                    if first and i == 0:
                        pe.wait_ge(s["normed"], k + 1)
                    part = slice(k * P, (k + 1) * P)
                    last = split_product(nc, m.bank[:, i, :], (w_hi[i][:, part], w_lo[i][:, part]), (h_hi[:, k, :], h_lo[:, k, :]),
                                         start=k == 0, stop=k == DK - 1)
                last.then_inc(done[i], 1)

            for i in range(SLOTS):
                chunk(0, i, True)
            with pe.Fori(1, rounds) as r:
                for i in range(SLOTS):
                    chunk(r, i, False)

        @block.scalar
        def _(act):
            def split(r, i, first):
                act.wait_ge(loaded[i], r * 16 + 16)
                if not first:
                    act.wait_ge(done[i], r)
                nc.scalar.copy(w_hi[i], raw[i]).then_inc(hi_ready[i], 1)

            def store(r, i):
                act.wait_ge(done[i], r + 1)
                nc.scalar.copy(column(m.queries, r * SLOTS + i), m.bank[:, i, :]).then_inc(copied[i], 1)

            norm_scalar(nc, act, m, s, lambda: split(0, 0, True))
            norm_hi(nc, act, m, s, h_hi)
            split(0, 1, True)
            with act.Fori(0, rounds - 1) as r:
                for i in range(SLOTS):
                    store(r, i)
                    split(r + 1, i, False)
            for i in range(SLOTS):
                store(rounds - 1, i)

        @block.vector
        def _(dve):
            def split(r, i):
                dve.wait_ge(hi_ready[i], r + 1)
                nc.vector.tensor_tensor(w_lo[i], raw[i], w_hi[i], ALU.subtract).then_inc(ready[i], 1)

            norm_vector(nc, dve, m, s, m.gain, h_hi, h_lo, lambda: split(0, 0))
            split(0, 1)
            with dve.Fori(1, rounds) as r:
                for i in range(SLOTS):
                    split(r, i)


def choice_scores(core, m):
    nc = core.nc
    score_done, score_read = core.sem("choice_score_done"), core.sem("choice_score_read")
    QUARTERS = PAIRS * KEYS // SEQ

    with nc.Block() as block:
        @block.sync
        def _(sp):
            core.zero_past(sp)

        @block.tensor
        def _(pe):
            for t in range(TB):
                for q in range(QUARTERS):
                    if t >= 2:
                        pe.wait_ge(score_read, QUARTERS * (t - 2) + q + 1)
                    for j in range(SEQ // KEYS):
                        i = q * (SEQ // KEYS) + j
                        last = nc.tensor.matmul(m.bank[:, QUARTERS * (t % 2) + q, j * KEYS:(j + 1) * KEYS],
                                                m.queries[:, i, t * P:(t + 1) * P],
                                                m.keys[:, i * KEYS:(i + 1) * KEYS], start=True, stop=True)
                    last.then_inc(score_done, 1)

        @block.scalar
        def _(act):
            for t in range(TB):
                for q in range(QUARTERS):
                    act.wait_ge(score_done, QUARTERS * t + q + 1)
                    nc.scalar.copy(m.scores[:, t, q * SEQ:(q + 1) * SEQ], m.bank[:, QUARTERS * (t % 2) + q, :])\
                        .then_inc(score_read, 1)


def experts(core, m, a, out):
    nc = core.nc
    ROUNDS = PICKS // RING
    assert ROUNDS == PH
    ADDED = range(0, RING, 3)
    MULTIPLIED = [n for n in range(RING) if n not in ADDED]
    HERE = 8
    diagonal_end = len(MULTIPLIED) * P
    ring = [m.w[:, n * D:(n + 1) * D] if n < HERE else m.arena[:, diagonal_end + (n - HERE) * D:diagonal_end + (n - HERE + 1) * D]
            for n in range(RING)]
    junk, total, squares, result = (m.w[:, (HERE + i) * D:(HERE + i + 1) * D] for i in range(4))
    junks = (junk, total)
    stage_index = [m.staged[:, i * RING:(i + 1) * RING] for i in range(2)]
    dots = m.dots
    diagonal = m.arena[:, 0:diagonal_end].rearrange("p (j c) -> p j c", j=len(MULTIPLIED))
    z = m.choose
    taken = lambda at_, n: z[:, at_:at_ + n]
    halves, keys_of_halves = taken(0, PAIRS * TOP), taken(256, PAIRS * TOP)
    values, left = taken(512, 256), taken(768, 256)
    best, place = taken(1024, TOP), taken(1040, TOP).bitcast(U32)
    pair_scores, pair_keys = taken(1056, 2 * TOP), taken(1088, 2 * TOP)
    part, part_f, row = taken(1120, 2 * TOP).bitcast(U32), taken(1152, 2 * TOP), taken(1184, 2 * TOP)
    one_hot = taken(1216, 2 * TOP * TOP)
    gate_sums = taken(1728, PH)

    loaded = [core.sem(f"row_loaded{i}") for i in range(RING)]
    used = [core.sem(f"row_used{i}") for i in range(RING)]
    diagonal_ready = [core.sem(f"diagonal_ready{j}") for j in range(len(MULTIPLIED))]
    granted, index_staged, turned, acts_ready, gelu_done, dots_kept, index_ready, weighted = (
        core.sem(f"experts_{n}") for n in ("granted", "index_staged", "turned", "acts_ready", "gelu_done", "dots_kept",
                                            "index_ready", "weighted"))
    summed, squared, mean_ready, rooted, result_ready, stored, chain, choice, settled = (
        core.sem(f"experts_{n}") for n in ("summed", "squared", "mean_ready", "rooted", "result_ready", "stored",
                                            "chain", "choice", "settled"))
    sums = m.small[:, 0:1]
    H_BANK, ACC_BANK, PE_BANK = 0, 2, 4

    def wide(b):
        return m.bank[:, b:b + 2, :].rearrange("p b c -> p (b c)")

    def u_rounds(t):
        return 2 * t * ROUNDS

    def v_rounds(t):
        return (2 * t + 1) * ROUNDS

    with nc.Block() as block:
        @block.gpsimd
        def _(pool):
            for t in range(TB):
                pool.wait_ge(index_ready, t + 1)
                for before, table in ((u_rounds(t), a["peer_u_2"]), (v_rounds(t), a["peer_v_2"])):
                    with pool.Fori(0, ROUNDS // 2) as g:
                        for i in range(2):
                            cols = bass.ds((g * 2 + i) * RING, RING)
                            nc.gpsimd.tensor_copy(stage_index[i], m.index[:, t, cols]).then_inc(index_staged, 1)
                            pool.wait_ge(index_staged, g * 2 + (before + i + 1))
                            for n in range(RING):
                                pool.wait_ge(used[n], g * 2 + (before + i + 1))
                                pool.sem_inc(granted, 1)
                                nc.gpsimd.indirect_dma_start(
                                    ring[n], None, table,
                                    bass.IndirectOffsetOnAxis(ap=stage_index[i][:, n:n + 1], axis=0)).then_inc(loaded[n], 16)

        @block.tensor
        def _(pe):
            def turn_h(t):
                for k in range(DK):
                    last = nc.tensor.transpose(wide(H_BANK)[:, k * P:(k + 1) * P], m.h[:, k, t * P:(t + 1) * P], m.ident)
                last.then_inc(turned, 1)

            def multiplied_rows(t, g, end):
                for i in range(2):
                    for j, n in enumerate(MULTIPLIED):
                        pe.wait_ge(loaded[n], (g * 2 + (v_rounds(t) + i + 1)) * 16)
                        pe.wait_ge(diagonal_ready[j], g * 2 + (t * ROUNDS + i + 1))
                        stop = end and i == 1 and n == MULTIPLIED[-1]
                        for b in range(2):
                            last = nc.tensor.matmul(m.bank[:, PE_BANK + b, :], diagonal[:, j, :], ring[n][:, b * SEQ:(b + 1) * SEQ],
                                                    start=False, stop=stop)
                        last.then_inc(used[n], 1)

            turn_h(0)
            for t in range(TB):
                pe.wait_ge(acts_ready, t + 1)
                if t + 1 < TB:
                    turn_h(t + 1)
                if t >= 1:
                    pe.wait_ge(summed, t)
                for k in range(DK):
                    nc.tensor.matmul(wide(PE_BANK)[:, k * P:(k + 1) * P], m.x[:, k, t * P:(t + 1) * P], m.ident,
                                     start=k % (SEQ // P) == 0, stop=False)
                with pe.Fori(0, ROUNDS // 2 - 1) as g:
                    multiplied_rows(t, g, False)
                multiplied_rows(t, ROUNDS // 2 - 1, True)

        @block.scalar
        def _(act):
            for t in range(TB):
                act.wait_ge(acts_ready, t + 1)
                nc.scalar.activation(m.picked[:, t, :], m.picked[:, t, :], ACT.Exp).then_inc(gelu_done, 1)
                nc.scalar.activation(m.acts, m.acts, ACT.Gelu).then_inc(gelu_done, 1)
                act.wait_ge(weighted, t + 1)
                with act.Fori(0, ROUNDS // 2) as g:
                    for i in range(2):
                        for j, n in enumerate(MULTIPLIED):
                            act.wait_ge(used[n], g * 2 + (v_rounds(t) + i + 1))
                            weight = m.acts[:, bass.ds((g * 2 + i) * RING + n, 1)]
                            nc.scalar.activation(diagonal[:, j, :], m.ident, ACT.Copy, scale=weight).then_inc(diagonal_ready[j], 1)
                act.wait_ge(summed, t + 1)
                nc.scalar.activation(squares, total, ACT.Square, accum_out=sums).then_inc(squared, 1)
                act.wait_ge(mean_ready, t + 1)
                nc.scalar.activation(sums, sums, ACT.Sqrt).then_inc(rooted, 1)

        @block.vector
        def _(dve):
            link = chained(dve, chain)
            v = nc.vector
            chosen = [0]

            def steps(r, per, past):
                count = [0]

                def step(instruction, carried=False):
                    count[0] += 1
                    instruction.then_inc(choice, 1)
                    dve.wait_ge(choice, r * per + (chosen[0] + past + count[0]))
                    if carried and not isinstance(r, int):
                        dve.sem_inc(settled, 1)

                return step, count

            def top_16(step, n):
                step(v.max(best[:, 0:8], values[:, 0:n]), carried=True)
                v.max_index(place[:, 0:8], best[:, 0:8], values[:, 0:n])
                step(v.match_replace(left[:, 0:n], best[:, 0:8], values[:, 0:n], NEG), carried=True)
                step(v.max(best[:, 8:16], left[:, 0:n]), carried=True)
                step(v.max_index(place[:, 8:16], best[:, 8:16], left[:, 0:n]))

            HALF_STEPS, HEAD_STEPS = 6, 13

            def choose_half(t, h, which, per):
                step, count = steps(h, per, 0)
                i = h * 2 + which
                step(v.tensor_copy(values[:, 0:KEYS], m.scores[:, t, bass.ds(i * KEYS, KEYS)]), carried=True)
                top_16(step, KEYS)
                v.tensor_copy(halves[:, bass.ds(i * TOP, TOP)], best)
                step(v.tensor_copy(keys_of_halves[:, bass.ds(i * TOP, TOP)], place))
                assert count[0] == HALF_STEPS

            def choose_head(t, h, per):
                step, count = steps(h, per, HALF_STEPS)
                square = lambda x: x.rearrange("p (k j) -> p k j", k=TOP)
                twice = lambda x: x.rearrange("p (i k j) -> p i k j", i=2, k=TOP)
                v.tensor_copy(pair_scores, halves[:, bass.ds(h * 2 * TOP, 2 * TOP)])
                step(v.tensor_copy(pair_keys, keys_of_halves[:, bass.ds(h * 2 * TOP, 2 * TOP)]))
                step(v.tensor_tensor(square(values), per_head(pair_scores[:, 0:TOP], TOP), spread(pair_scores[:, TOP:], TOP), ALU.add),
                     carried=True)
                top_16(step, TOP * TOP)
                v.tensor_scalar(part[:, 0:TOP], place, 4, None, ALU.logical_shift_right)
                step(v.tensor_scalar(part[:, TOP:], place, TOP - 1, None, ALU.bitwise_and))
                step(v.tensor_copy(part_f, part))
                step(v.tensor_tensor(one_hot.rearrange("p (k j) -> p k j", j=TOP), per_head(part_f, TOP), spread(m.iota, 2 * TOP),
                                     ALU.is_equal))
                keys = pair_keys.rearrange("p (i one j) -> p i one j", i=2, one=1).broadcast_to([P, 2, TOP, TOP])
                step(v.tensor_tensor(twice(one_hot), twice(one_hot), keys, ALU.mult))
                step(v.tensor_reduce(row, one_hot.rearrange("p (k j) -> p k j", j=TOP), AX.X, ALU.add))
                step(v.scalar_tensor_tensor(row[:, 0:TOP], row[:, 0:TOP], float(KEYS), row[:, TOP:], ALU.mult, ALU.add))
                v.tensor_copy(m.index[:, t, bass.ds(h * TOP, TOP)], row[:, 0:TOP])
                step(v.tensor_scalar(m.picked[:, t, bass.ds(h * TOP, TOP)], best, best[:, 0:1], None, ALU.subtract))
                assert count[0] == HEAD_STEPS

            def dot_rows(t, g, i):
                for n in range(RING):
                    dve.wait_ge(loaded[n], (g * 2 + (u_rounds(t) + i + 1)) * 16)
                    v.tensor_tensor_reduce(out=junks[n % 2], in0=ring[n], in1=wide(H_BANK), scale=1.0, scalar=0.0, op0=ALU.mult,
                                           op1=ALU.add, accum_out=dots[:, n:n + 1]).then_inc(used[n], 1)
                    if n >= 1:
                        dve.wait_ge(used[n - 1], g * 2 + (u_rounds(t) + i + 2))
                dve.wait_ge(used[RING - 1], g * 2 + (u_rounds(t) + i + 2))
                v.tensor_copy(m.acts[:, bass.ds((g * 2 + i) * RING, RING)], dots[:, 0:RING]).then_inc(dots_kept, 1)
                dve.wait_ge(dots_kept, g * 2 + (t * ROUNDS + i + 1))

            def added_rows(t, g, i):
                for n in ADDED:
                    dve.wait_ge(loaded[n], (g * 2 + (v_rounds(t) + i + 1)) * 16)
                    weight = m.acts[:, bass.ds((g * 2 + i) * RING + n, 1)]
                    v.scalar_tensor_tensor(wide(ACC_BANK), ring[n], weight, wide(ACC_BANK), ALU.mult, ALU.add)\
                        .then_inc(used[n], 1)
                    dve.wait_ge(used[n], g * 2 + (v_rounds(t) + i + 2))

            for n in range(RING):
                dve.sem_inc(used[n], 1)
            for h in range(PH):
                choose_half(0, h, 0, HALF_STEPS)
            chosen[0] += PH * HALF_STEPS
            for h in range(PH):
                choose_half(0, h, 1, HALF_STEPS + HEAD_STEPS)
                choose_head(0, h, HALF_STEPS + HEAD_STEPS)
            chosen[0] += PH * (HALF_STEPS + HEAD_STEPS)
            dve.sem_inc(index_ready, 1)
            for t in range(TB):
                dve.wait_ge(turned, t + 1)
                with dve.Fori(0, ROUNDS // 2) as g:
                    for i in range(2):
                        dot_rows(t, g, i)
                        if t + 1 < TB:
                            choose_half(t + 1, g * 2 + i, 0, HALF_STEPS)
                if t + 1 < TB:
                    chosen[0] += PH * HALF_STEPS
                dve.sem_inc(acts_ready, 1)
                link(v.memset(wide(ACC_BANK), 0.0))
                dve.wait_ge(gelu_done, 2 * t + 1)
                gates = m.picked[:, t, :].rearrange("p (h k) -> p h k", h=PH)
                link(v.tensor_reduce(gate_sums, gates, AX.X, ALU.add))
                link(v.reciprocal(gate_sums, gate_sums))
                link(v.tensor_tensor(gates, gates, per_head(gate_sums, TOP), ALU.mult))
                dve.wait_ge(gelu_done, 2 * t + 2)
                link(v.tensor_tensor(m.acts, m.acts, m.picked[:, t, :], ALU.mult))
                dve.sem_inc(weighted, 1)
                with dve.Fori(0, ROUNDS // 2) as g:
                    for i in range(2):
                        added_rows(t, g, i)
                        if t + 1 < TB:
                            choose_half(t + 1, g * 2 + i, 1, HALF_STEPS + HEAD_STEPS)
                            choose_head(t + 1, g * 2 + i, HALF_STEPS + HEAD_STEPS)
                if t + 1 < TB:
                    chosen[0] += PH * (HALF_STEPS + HEAD_STEPS)
                    dve.sem_inc(index_ready, 1)
                if t >= 1:
                    dve.wait_ge(stored, 16 * t)
                link(v.tensor_copy(result, wide(ACC_BANK)))
                dve.wait_ge(used[MULTIPLIED[-1]], v_rounds(t) + ROUNDS + 1)
                if t >= 1:
                    dve.wait_ge(squared, t)
                v.tensor_tensor(total, result, wide(PE_BANK), ALU.add).then_inc(summed, 1)
                dve.wait_ge(squared, t + 1)
                v.tensor_scalar(sums, sums, 1.0 / D, EPS, ALU.mult, ALU.add).then_inc(mean_ready, 1)
                dve.wait_ge(rooted, t + 1)
                link(v.reciprocal(sums, sums))
                v.scalar_tensor_tensor(result, total, sums, m.final_gain, ALU.mult, ALU.mult).then_inc(result_ready, 1)
                dve.wait_ge(result_ready, t + 1)

        @block.sync
        def _(sp):
            core.zero_past(sp)
            for t in range(TB):
                sp.wait_ge(result_ready, t + 1)
                sp.dma_start(out[t * P:(t + 1) * P, :], result).then_inc(stored, 16)
            sp.wait_ge(stored, 16 * TB)


def second_block(core, m, a, out):
    m.fm = m.arena[:, 0:N_FM * SEQ].rearrange("p (c t) -> p c t", c=N_FM)
    m.cv = m.arena[:, 14336:14336 + 12 * SEQ].rearrange("p (c t) -> p c t", c=12)
    m.mv = m.arena[:, 20480:20480 + TB * GH * (P + 1)].rearrange("p (t h c) -> p t h c", t=TB, h=GH)
    m.gates = m.arena[:, 22544:22544 + TB * GATE_C].rearrange("p (t c) -> p t c", t=TB)
    m.rows = m.arena[0:GATE_ROWS, 23120:23120 + 6 * SEQ]
    m.select = m.rows[:, 2 * SEQ:4 * SEQ]
    m.o_tok = m.scratch.rearrange("p (t c) -> p t c", t=TB)
    m.k_tok, m.v_tok, m.kk = (m.arena[:, i * 2048:(i + 1) * 2048].rearrange("p (t c) -> p t c", t=TB) for i in range(3))
    m.qk = m.arena[:, 14336 + 8 * SEQ:14336 + 12 * SEQ].rearrange("p (t c) -> p t c", t=TB)
    m.qk_t = m.arena[:, 20 * SEQ:28 * SEQ].rearrange("p (n c) -> p n c", n=8)
    m.inverse = m.h.rearrange("p k t -> p (k t)").rearrange("p (n c) -> p n c", n=8)
    tok4 = [m.tail[:, i * 144:(i + 1) * 144].rearrange("p (t r) -> p t r", t=TB) for i in range(4)]
    m.g_tok, m.shift_tok, m.bm_tok, m.beta = tok4
    m.rate = m.tail[:, 576:577]
    m.gdn_small = m.tail[:, 580:580 + 96]
    m.anti = m.const[:, P:2 * P]
    m.block_mask = m.const[:, 2 * P:10 * P]
    m.const_2_width = 9 * P
    m.queries = m.arena[:, 0:PAIRS * SEQ].rearrange("p (n t) -> p n t", n=PAIRS)
    m.keys = m.arena[:, 8192:8192 + PAIRS * KEYS]
    m.final_gain = m.arena[:, 10240:10240 + D]
    m.picked = m.arena[:, 11264:11264 + TB * PICKS].rearrange("p (t c) -> p t c", t=TB)
    m.index = m.arena[:, 11776:11776 + TB * PICKS].bitcast(U32).rearrange("p (t c) -> p t c", t=TB)
    m.acts = m.arena[:, 12288:12288 + PICKS]
    m.iota = m.arena[:, 12416:12416 + TOP]
    m.staged = m.arena[:, 12432:12432 + 2 * RING].bitcast(U32)
    m.dots = m.arena[:, 12464:12464 + RING]
    m.choose = m.arena[:, 12800:12800 + 1792]
    m.scores = m.arena[:, 16384:16384 + TB * PAIRS * KEYS].rearrange("p (t c) -> p t c", t=TB)

    second_projection(core, m, a)
    core.next_stage()
    gate_rows(core, m)
    core.next_stage()
    mlstm(core, m)
    core.next_stage()
    gated_norm(core, m, "ml_norm", FM_AT["mo"], ACT.Sigmoid, lambda h: m.gdn_small[:, 77 + h:78 + h])
    core.next_stage()
    conv_and_turn(core, m)
    core.next_stage()
    delta_inverse(core, m)
    core.next_stage()
    delta_rule(core, m)
    core.next_stage()
    gated_norm(core, m, "gdn_norm", FM_AT["gz"], ACT.Silu, lambda h: m.gdn_small[:, 76:77])
    core.next_stage()
    out_projection(core, m, a["w_out_2"])
    core.next_stage()
    expert_queries(core, m, a)
    core.next_stage()
    choice_scores(core, m)
    core.next_stage()
    experts(core, m, a, out)
    core.zero_all()


def lay_out_second(i):
    f = lambda n: np.asarray(i[n])[0] if n != "normf_g_2" else np.asarray(i[n])

    def gain(n):
        return f(n).reshape(DK, P).T

    def chunks(w, c):
        return w.reshape(DK, P, -1, c).transpose(2, 1, 0, 3).reshape(-1, P, DK * c)

    sizes = (512, 512, 512, 512, 8, 8, 512, 512, 512, 512, 8, 8)
    names = ("gq", "gk", "gv", "gz", "a", "b", "mq", "mk", "mv", "mo", "i", "f")
    ends = np.cumsum(sizes)
    w_in = f("w_in_2")
    part = {n: w_in[:, e - s:e] for n, s, e in zip(names, sizes, ends)}
    gates = np.zeros((D, GATE_C), w_in.dtype)
    small = np.zeros((P, 96), w_in.dtype)
    for kind, at_ in KINDS.items():
        for d in range(DIRS):
            gates[:, at_ * GATE_ROWS + d * BACK:][:, :GH] = part[kind][:, d * GH:(d + 1) * GH]
    for n, name in enumerate(("gdn_dt_bias_2", "gdn_a_log_2", "mlstm_i_bias_2", "mlstm_f_bias_2")):
        for d in range(DIRS):
            small[d * BACK:d * BACK + GH, n] = f(name)[d]
    small[:, 16:76] = f("conv_w_2").reshape(12, P, CONV_K).transpose(1, 0, 2).reshape(P, -1)
    small[:, 76] = f("gdn_norm_g_2")
    small[:, 77:81] = f("mlstm_norm_g_2").reshape(GH, P).T
    t = np.arange(P)
    lower = []
    lower.append((t[:, None] // 16 == t[None, :] // 16) & (t[:, None] > t[None, :]))
    for size in (16, 32, 64):
        lower.append((t[:, None] // (2 * size) == t[None, :] // (2 * size)) & (t[:, None] // size > t[None, :] // size))
    masks = [x.astype(np.float32) for x in lower] + [x.T.astype(np.float32) for x in lower]
    anti = np.where(t[None, :] >= t[:, None], 0.0, NEG).astype(np.float32)
    keys = f("peer_keys_2").reshape(PAIRS, KEYS, P).transpose(2, 0, 1).reshape(P, -1)
    out = {
        "norm1_2": gain("norm1_g_2"), "norm2_2": gain("norm2_g_2"),
        "w_in_fm_2": np.concatenate([chunks(part[n], P) for n in ("gq", "gk", "gv", "gz", "mo", "mq", "mk")]
                                    + [chunks(part["mv"], SEQ)[0].reshape(P, DK // 2, D).transpose(1, 0, 2)]),
        "w_in_gates_2": chunks(gates, GATE_C)[0],
        "const_2": np.concatenate([anti] + masks, 1),
        "gdn_small_2": small,
        "w_out_2": f("w_out_2").reshape(DK, P, D),
        "peer_wq_2": chunks(f("peer_wq_2"), P),
        "peer_keys_2": keys,
        "normf_2": np.broadcast_to(f("normf_g_2")[None, :], (P, D)),
        "iota": np.broadcast_to(np.arange(TOP, dtype=np.float32)[None, :], (P, TOP)),
        "peer_u_2": f("peer_u_2"), "peer_v_2": f("peer_v_2"),
    }
    return {n: np.ascontiguousarray(v) for n, v in out.items()}


class Memory:
    pass


def program(nc, arrays, out):
    with ExitStack() as ctx:
        core, m = Core(nc, ctx), Memory()
        allocate(core, m)
        load_start(core, m, arrays)
        first_block(core, m, arrays)
        second_block(core, m, arrays, out)


def kernel(**inputs):
    import concourse.bacc as bacc
    from concourse.bass_utils import run_bass_kernel_spmd

    arrays = lay_out_first(inputs) | lay_out_second(inputs)
    nc = bacc.Bacc("TRN2", target_bir_lowering=False, num_devices=1)
    ins = {n: nc.dram_tensor(n, v.shape, mybir.dt.from_np(v.dtype), kind="ExternalInput").ap() for n, v in arrays.items()}
    out = nc.dram_tensor("out", (SEQ, D), F32, kind="ExternalOutput").ap()
    program(nc, ins, out)
    result = run_bass_kernel_spmd(nc, [arrays], core_ids=[0])
    return result.results[0]["out"].reshape(1, SEQ, D)
```
